# Optimizing a Trainium2 kernel written in Bass

```python
import math
import jax
import jax.numpy as jnp
from jax import lax
import numpy as np

D_MODEL = 1024
BATCH = 1
SEQ = 1024
DEPTH = 1

GRID_W = 64
CTX_LEN = 256

HY_WIDTH = D_MODEL // 4
NA_HEAD_DIM = 64
NA_WIDTH = D_MODEL // 2
NA_HEADS = NA_WIDTH // NA_HEAD_DIM
LRU_WIDTH = D_MODEL // 4
LRU_BLOCKS = 4
MIX_WIDTH = HY_WIDTH + NA_WIDTH + LRU_WIDTH
IN_WIDTH = 3 * HY_WIDTH + 3 * NA_WIDTH + 2 * LRU_WIDTH

HY_ORDER = 2
HY_SHORT_CONV = 3
HY_BANDS = 16
HY_EMB = 2 * HY_BANDS + 1
HY_FILTER_HIDDEN = 64
HY_FAST_DECAY = 0.3
HY_SLOW_DECAY = 1.5
HY_DECAY_TARGET = 1e-2

NA_WIN_ROWS = 8
NA_WIN_COLS = 16
NA_COL_BLOCK = 16
NA_KEY_COLS = 32

LRU_CONV = 4
LRU_C = 8.0

D_FF = -(-8 * D_MODEL // (3 * 256)) * 256
RMS_EPS = 1e-6
NEG_INF = -1e30

kernel_name = 'hybrid_hyena_natten_rglru_diffusion_block'

def rmsnorm(x, g):
    xf = x.astype(jnp.float32)
    y = xf * lax.rsqrt(jnp.mean(xf * xf, axis=-1, keepdims=True) + RMS_EPS)
    return (y * g.astype(jnp.float32)).astype(x.dtype)

def modulation(cond, w, b):
    m = jax.nn.silu(cond) @ w + b
    return jnp.split(m, 6, axis=-1)

def conv_centred(x, w, b):
    K = w.shape[0]
    L = x.shape[1]
    pl = K // 2
    pr = K - 1 - pl
    xp = jnp.pad(x, ((0, 0), (pl, pr), (0, 0)))
    y = b
    for k in range(K):
        y = y + w[k] * xp[:, k:k + L]
    return y

def hyena_filters(L, f_w1, f_b1, f_w2, f_b2, f_w3, f_freq):
    t = jnp.arange(L, dtype=jnp.float32) / L
    bands = jnp.arange(1, HY_BANDS + 1, dtype=jnp.float32)
    ang = 2.0 * math.pi * t[:, None] * bands[None, :]
    z = jnp.concatenate([t[:, None], jnp.cos(ang), jnp.sin(ang)], axis=-1)
    h = jnp.sin(f_freq[0] * (z @ f_w1 + f_b1))
    h = jnp.sin(f_freq[1] * (h @ f_w2 + f_b2))
    k = (h @ f_w3).astype(jnp.float32).reshape(L, HY_ORDER, 2, HY_WIDTH)
    deltas = jnp.abs(jnp.linspace(math.log(HY_DECAY_TARGET) / HY_FAST_DECAY,
                                  math.log(HY_DECAY_TARGET) / HY_SLOW_DECAY,
                                  HY_WIDTH, dtype=jnp.float32))
    k = k * jnp.exp(-t[:, None, None, None] * deltas)
    kf = k[:, :, 0]
    kb = k[:, :, 1]
    k_circ = jnp.concatenate([kf, jnp.zeros_like(kf[:1]), kb[:0:-1]], axis=0)
    k_circ = k_circ / jnp.sum(jnp.abs(k_circ), axis=0, keepdims=True)
    return jnp.fft.rfft(k_circ, axis=0)

def fft_conv(u, k_f):
    L = u.shape[1]
    U = jnp.fft.rfft(u, n=2 * L, axis=1)
    return jnp.fft.irfft(U * k_f[None], n=2 * L, axis=1)[:, :L]

def hyena_mixer(p, conv_w, conv_b, filt, hy_bias):
    L = p.shape[1]
    u = conv_centred(p, conv_w, conv_b).astype(jnp.float32)
    v, x1, x2 = jnp.split(u, 3, axis=-1)
    k_f = hyena_filters(L, *filt)
    z = v
    for n, gate in enumerate((x1, x2)):
        z = gate * (fft_conv(z, k_f[:, n]) + hy_bias[n].astype(jnp.float32) * z)
    return z

def na_static(grid_w):
    n_cb = grid_w // NA_COL_BLOCK
    qc = np.arange(grid_w).reshape(n_cb, NA_COL_BLOCK)
    kc0 = np.clip(np.arange(n_cb) * NA_COL_BLOCK - NA_WIN_COLS // 2, 0, grid_w - NA_KEY_COLS)
    kc = kc0[:, None] + np.arange(NA_KEY_COLS)[None, :]
    start = np.clip(qc - NA_WIN_COLS // 2, 0, grid_w - NA_WIN_COLS)
    valid = (kc[:, None, :] >= start[:, :, None]) & (kc[:, None, :] < start[:, :, None] + NA_WIN_COLS)
    dc = np.clip(kc[:, None, :] - qc[:, :, None], -(NA_WIN_COLS - 1), NA_WIN_COLS - 1) + NA_WIN_COLS - 1
    return kc, valid, dc

def na_latent(q, k, v, k_ctx, v_ctx, rpb, rows):
    B, L, H, dh = q.shape
    kr = min(NA_WIN_ROWS, rows)
    kc, valid, dc = na_static(GRID_W)
    n_cb = kc.shape[0]
    n_loc = kr * NA_KEY_COLS
    scale = dh ** -0.5
    valid = jnp.asarray(valid)[:, :, None, :]
    qg = q.reshape(B, rows, n_cb, NA_COL_BLOCK, H, dh).transpose(1, 0, 4, 2, 3, 5)
    kg = k.reshape(B, rows, GRID_W, H, dh).transpose(0, 3, 1, 2, 4)
    vg = v.reshape(B, rows, GRID_W, H, dh).transpose(0, 3, 1, 2, 4)
    kcx = k_ctx.transpose(0, 2, 1, 3)
    vcx = v_ctx.transpose(0, 2, 1, 3)

    def row_step(args):
        q_r, r = args
        rs = jnp.clip(r - kr // 2, 0, rows - kr)
        k_blk = lax.dynamic_slice_in_dim(kg, rs, kr, axis=2)[:, :, :, kc]
        v_blk = lax.dynamic_slice_in_dim(vg, rs, kr, axis=2)[:, :, :, kc]
        s_loc = jnp.einsum('bhnqd,bhrnkd->bhnqrk', q_r, k_blk).astype(jnp.float32) * scale
        dr = rs + jnp.arange(kr) - r + NA_WIN_ROWS - 1
        bias = rpb[:, dr][:, :, dc].transpose(0, 2, 3, 1, 4)
        s_loc = jnp.where(valid, s_loc + bias[None].astype(jnp.float32), NEG_INF)
        s_ctx = jnp.einsum('bhnqd,bhcd->bhnqc', q_r, kcx).astype(jnp.float32) * scale
        s = jnp.concatenate([s_loc.reshape(B, H, n_cb, NA_COL_BLOCK, n_loc), s_ctx], axis=-1)
        p = jax.nn.softmax(s, axis=-1)
        p_loc = p[..., :n_loc].reshape(B, H, n_cb, NA_COL_BLOCK, kr, NA_KEY_COLS).astype(v.dtype)
        p_ctx = p[..., n_loc:].astype(v.dtype)
        return (jnp.einsum('bhnqrk,bhrnkd->bhnqd', p_loc, v_blk)
                + jnp.einsum('bhnqc,bhcd->bhnqd', p_ctx, vcx))

    o = lax.map(row_step, (qg, jnp.arange(rows)))
    return o.transpose(1, 0, 3, 4, 2, 5).reshape(B, L, H * dh)

def attn_ctx(q, k, v):
    B, Lc, H, dh = q.shape
    s = jnp.einsum('bqhd,bkhd->bhqk', q, k).astype(jnp.float32) * (dh ** -0.5)
    p = jax.nn.softmax(s, axis=-1).astype(v.dtype)
    return jnp.einsum('bhqk,bkhd->bqhd', p, v).reshape(B, Lc, H * dh)

def linear_scan(a, b, h0, reverse):
    idx = -1 if reverse else 0
    b = b.at[:, idx].add(a[:, idx] * h0)

    def combine(e1, e2):
        a1, b1 = e1
        a2, b2 = e2
        return a1 * a2, a2 * b1 + b2

    _, h = lax.associative_scan(combine, (a, b), reverse=reverse, axis=1)
    return h

def rglru_coeffs(u, wa, ba, wi, bi, lam):
    B, L, C = u.shape
    ub = u.reshape(B, L, LRU_BLOCKS, C // LRU_BLOCKS)
    r = jax.nn.sigmoid(jnp.einsum('blnc,ncd->blnd', ub, wa.astype(jnp.float32)).reshape(B, L, C) + ba)
    i = jax.nn.sigmoid(jnp.einsum('blnc,ncd->blnd', ub, wi.astype(jnp.float32)).reshape(B, L, C) + bi)
    log_a = -LRU_C * r * jax.nn.softplus(-lam.astype(jnp.float32))
    a = jnp.exp(log_a)
    b = jnp.sqrt(-jnp.expm1(2.0 * log_a)) * (i * u)
    return a, b

def lru_mixer(p, pc, conv_w, conv_b, wa, ba, wi, bi, lam, with_ctx_out):
    xr, xg = jnp.split(p, 2, axis=-1)
    xr_c, xg_c = jnp.split(pc, 2, axis=-1)
    u = conv_centred(xr, conv_w, conv_b).astype(jnp.float32)
    u_c = conv_centred(xr_c, conv_w, conv_b).astype(jnp.float32)
    h_lat = 0.0
    h_ctx = 0.0
    for d, rev in enumerate((False, True)):
        a_c, b_c = rglru_coeffs(u_c, wa[d], ba[d], wi[d], bi[d], lam[d])
        hc = linear_scan(a_c, b_c, jnp.zeros_like(b_c[:, 0]), rev)
        h_end = hc[:, 0] if rev else hc[:, -1]
        a_l, b_l = rglru_coeffs(u, wa[d], ba[d], wi[d], bi[d], lam[d])
        h_lat = h_lat + linear_scan(a_l, b_l, h_end, rev)
        h_ctx = h_ctx + hc
    y = (h_lat * jax.nn.gelu(xg.astype(jnp.float32))).astype(p.dtype)
    if not with_ctx_out:
        return y, None
    yc = (h_ctx * jax.nn.gelu(xg_c.astype(jnp.float32))).astype(p.dtype)
    return y, yc

def mixer(h, hc, rows, with_ctx_out, w_in, w_out, hy_conv_w, hy_conv_b, hy_filt, hy_bias, na_rpb, lru_params):
    B, L, _ = h.shape
    Lc = hc.shape[1]
    s1 = 3 * HY_WIDTH
    s2 = s1 + 3 * NA_WIDTH
    p = h @ w_in
    pc = hc @ w_in
    y_hy = hyena_mixer(p[..., :s1], hy_conv_w, hy_conv_b, hy_filt, hy_bias).astype(h.dtype)
    qkv = p[..., s1:s2].reshape(B, L, 3, NA_HEADS, NA_HEAD_DIM)
    qkv_c = pc[..., s1:s2].reshape(B, Lc, 3, NA_HEADS, NA_HEAD_DIM)
    y_na = na_latent(qkv[:, :, 0], qkv[:, :, 1], qkv[:, :, 2], qkv_c[:, :, 1], qkv_c[:, :, 2], na_rpb, rows)
    y_lru, yc_lru = lru_mixer(p[..., s2:], pc[..., s2:], *lru_params, with_ctx_out)
    y = jnp.concatenate([y_hy, y_na, y_lru], axis=-1) @ w_out
    if not with_ctx_out:
        return y, None
    yc_hy = hyena_mixer(pc[..., :s1], hy_conv_w, hy_conv_b, hy_filt, hy_bias).astype(hc.dtype)
    yc_na = attn_ctx(qkv_c[:, :, 0], qkv_c[:, :, 1], qkv_c[:, :, 2])
    yc = jnp.concatenate([yc_hy, yc_na, yc_lru], axis=-1) @ w_out
    return y, yc

def swiglu(h, w_gu, w_down):
    g, u = jnp.split(h @ w_gu, 2, axis=-1)
    return (jax.nn.silu(g) * u) @ w_down

def setup_inputs(seed: int = 0) -> dict:
    key = jax.random.key(seed)
    ks = jax.random.split(key, 32)
    f32 = jnp.float32
    D = D_MODEL
    blk = LRU_WIDTH // LRU_BLOCKS

    def nrm(i, shape, scale):
        return scale * jax.random.normal(ks[i], shape, f32)

    a8 = jax.random.uniform(ks[28], (DEPTH, 2, LRU_WIDTH), f32, 0.9, 0.999)
    a_base = a8 ** (1.0 / LRU_C)
    lru_lam = jnp.log(a_base) - jnp.log1p(-a_base)
    return {
        'x': nrm(0, (BATCH, SEQ, D), 1.0),
        'c': nrm(1, (BATCH, D), 1.0),
        'ctx': nrm(2, (BATCH, CTX_LEN, D), 1.0),
        'c_ctx': nrm(3, (D,), 1.0),
        'ada_w': nrm(4, (DEPTH, D, 6 * D), D ** -0.5),
        'ada_b': nrm(5, (DEPTH, 6 * D), 0.02),
        'g_mix_pre': 1.0 + nrm(6, (DEPTH, D), 0.02),
        'g_mix_post': 1.0 + nrm(7, (DEPTH, D), 0.02),
        'g_ffn_pre': 1.0 + nrm(8, (DEPTH, D), 0.02),
        'g_ffn_post': 1.0 + nrm(9, (DEPTH, D), 0.02),
        'w_in': nrm(10, (DEPTH, D, IN_WIDTH), D ** -0.5),
        'w_out': nrm(11, (DEPTH, MIX_WIDTH, D), MIX_WIDTH ** -0.5),
        'hy_conv_w': nrm(12, (DEPTH, HY_SHORT_CONV, 3 * HY_WIDTH), HY_SHORT_CONV ** -0.5),
        'hy_conv_b': nrm(13, (DEPTH, 3 * HY_WIDTH), 0.02),
        'hy_f_w1': nrm(14, (DEPTH, HY_EMB, HY_FILTER_HIDDEN), HY_EMB ** -0.5),
        'hy_f_b1': nrm(15, (DEPTH, HY_FILTER_HIDDEN), 0.02),
        'hy_f_w2': nrm(16, (DEPTH, HY_FILTER_HIDDEN, HY_FILTER_HIDDEN), HY_FILTER_HIDDEN ** -0.5),
        'hy_f_b2': nrm(17, (DEPTH, HY_FILTER_HIDDEN), 0.02),
        'hy_f_w3': nrm(18, (DEPTH, HY_FILTER_HIDDEN, HY_ORDER * 2 * HY_WIDTH), HY_FILTER_HIDDEN ** -0.5),
        'hy_f_freq': 1.0 + nrm(19, (DEPTH, 2, HY_FILTER_HIDDEN), 0.1),
        'hy_bias': nrm(20, (DEPTH, HY_ORDER, HY_WIDTH), 1.0),
        'na_rpb': nrm(21, (DEPTH, NA_HEADS, 2 * NA_WIN_ROWS - 1, 2 * NA_WIN_COLS - 1), 0.02),
        'lru_conv_w': nrm(22, (DEPTH, LRU_CONV, LRU_WIDTH), LRU_CONV ** -0.5),
        'lru_conv_b': nrm(23, (DEPTH, LRU_WIDTH), 0.02),
        'lru_wa': nrm(24, (DEPTH, 2, LRU_BLOCKS, blk, blk), blk ** -0.5),
        'lru_ba': nrm(25, (DEPTH, 2, LRU_WIDTH), 0.02),
        'lru_wi': nrm(26, (DEPTH, 2, LRU_BLOCKS, blk, blk), blk ** -0.5),
        'lru_bi': nrm(27, (DEPTH, 2, LRU_WIDTH), 0.02),
        'lru_lam': lru_lam,
        'ffn_w_gu': nrm(29, (DEPTH, D, 2 * D_FF), D ** -0.5),
        'ffn_w_down': nrm(30, (DEPTH, D_FF, D), D_FF ** -0.5),
    }

def reference(x, c, ctx, c_ctx, ada_w, ada_b, g_mix_pre, g_mix_post, g_ffn_pre, g_ffn_post,
              w_in, w_out, hy_conv_w, hy_conv_b, hy_f_w1, hy_f_b1, hy_f_w2, hy_f_b2, hy_f_w3,
              hy_f_freq, hy_bias, na_rpb, lru_conv_w, lru_conv_b, lru_wa, lru_ba, lru_wi, lru_bi,
              lru_lam, ffn_w_gu, ffn_w_down):
    rows = x.shape[1] // GRID_W
    xc = ctx
    for l in range(DEPTH):
        with_ctx_out = l < DEPTH - 1
        sh_m, sc_m, gt_m, sh_f, sc_f, gt_f = [t[:, None, :] for t in modulation(c, ada_w[l], ada_b[l])]
        csh_m, csc_m, cgt_m, csh_f, csc_f, cgt_f = modulation(c_ctx, ada_w[l], ada_b[l])

        h = rmsnorm(x, g_mix_pre[l]) * (1.0 + sc_m) + sh_m
        hc = rmsnorm(xc, g_mix_pre[l]) * (1.0 + csc_m) + csh_m
        hy_filt = (hy_f_w1[l], hy_f_b1[l], hy_f_w2[l], hy_f_b2[l], hy_f_w3[l], hy_f_freq[l])
        lru_params = (lru_conv_w[l], lru_conv_b[l], lru_wa[l], lru_ba[l], lru_wi[l], lru_bi[l], lru_lam[l])
        y, yc = mixer(h, hc, rows, with_ctx_out, w_in[l], w_out[l], hy_conv_w[l], hy_conv_b[l],
                      hy_filt, hy_bias[l], na_rpb[l], lru_params)
        x = x + gt_m * rmsnorm(y, g_mix_post[l])

        h = rmsnorm(x, g_ffn_pre[l]) * (1.0 + sc_f) + sh_f
        x = x + gt_f * rmsnorm(swiglu(h, ffn_w_gu[l], ffn_w_down[l]), g_ffn_post[l])

        if with_ctx_out:
            xc = xc + cgt_m * rmsnorm(yc, g_mix_post[l])
            hc = rmsnorm(xc, g_ffn_pre[l]) * (1.0 + csc_f) + csh_f
            xc = xc + cgt_f * rmsnorm(swiglu(hc, ffn_w_gu[l], ffn_w_down[l]), g_ffn_post[l])
    return x


_drawn_inputs = setup_inputs


def setup_inputs(seed=0):
    import zlib

    import numpy as np

    out = dict(_drawn_inputs(seed))
    spreads = {}
    factors = {'g_mix_pre': 4.864,
     'g_mix_post': 5.205,
     'g_ffn_pre': 15.207,
     'g_ffn_post': 62.247,
     'hy_conv_b': 8.0,
     'hy_f_b1': 8.0,
     'hy_f_b2': 8.0,
     'hy_f_freq': 8.0,
     'na_rpb': 200.0,
     'lru_conv_b': 2.729,
     'lru_ba': 64.0,
     'lru_bi': 64.0}
    for name, (base, spread) in spreads.items():
        noise = np.random.default_rng([zlib.crc32(name.encode()), seed]).standard_normal(out[name].shape)
        drawn = base * np.exp(spread * noise) if base else spread * noise
        out[name] = jnp.asarray(drawn.astype(out[name].dtype))
    for name, factor in factors.items():
        out[name] = (out[name] * factor).astype(out[name].dtype)
    return out
```

```python
import math
from contextlib import ExitStack

import numpy as np

import concourse.bass as bass
from concourse import mybir

F32 = mybir.dt.float32
F32R = mybir.dt.float32r
ALU = mybir.AluOpType
ACT = mybir.ActivationFunctionType
AX = mybir.AxisListType.X
ds = bass.ds

P = 128
D = 1024
SEQ = 1024
CTX = 256
KT = D // P
HALF = 512
GRID_W = 64
ROWS = SEQ // GRID_W
HY = D // 4
HEADS = 8
DH = 64
WIN_R, WIN_C = 8, 16
FF = 2816
FT = FF // P
ALL = CTX + SEQ
NEG = -1e30
EPS = 1e-6
MAGIC = 12582912.0
TWO_PI_HEAD = 6.28125
TWO_PI_REST = 2.0 * math.pi - TWO_PI_HEAD

J_K, J_CTX, J_LAT, J_HY, J_OUT, J_FFN = 0, 16, 26, 70, 134, 150
E_K, E_CTX, E_LAT, E_FWD, E_OUT, E_GU = 0, 16, 26, 70, 102, 118
GU_JOBS, DOWN_JOBS = 2 * FT, 24
JOBS = J_FFN + 2 * (GU_JOBS + DOWN_JOBS)


def host_tables():
    t = np.arange(SEQ)
    ang4 = 2 * np.pi * (((2 * t[:, None] + 1) * (2 * t[None, :] + 1)) % (8 * SEQ)) / (8 * SEQ)
    angk = 2 * np.pi * ((2 * t[:, None] * (2 * t[None, :] + 1)) % (8 * SEQ)) / (8 * SEQ)

    def tiles(m):
        return np.ascontiguousarray(m.reshape(KT, P, KT, P).transpose(2, 1, 0, 3).reshape(KT, P, D))

    four = np.stack([tiles(np.cos(ang4)), tiles(np.sin(ang4))], 1).astype(np.float32)
    fourk = np.stack([tiles(np.cos(angk)), tiles(np.sin(angk))], 1).astype(np.float32)
    tt = t.astype(np.float32) / np.float32(SEQ)
    bands = np.arange(1, 17, dtype=np.float32)
    ang = np.float32(2 * math.pi) * tt[:, None] * bands[None, :]
    z = np.concatenate([tt[:, None], np.cos(ang), np.sin(ang)], 1).astype(np.float32).T
    deltas = np.abs(np.linspace(math.log(1e-2) / 0.3, math.log(1e-2) / 1.5, HY, dtype=np.float32))
    decay = np.exp(-tt[:, None] * deltas[None, :]).astype(np.float32)
    sel = np.zeros((32, GRID_W, GRID_W), np.float32)
    q = np.arange(GRID_W)
    start = np.clip(q - WIN_C // 2, 0, GRID_W - WIN_C)
    for kc in range(GRID_W):
        for qc in range(GRID_W):
            if start[qc] <= kc < start[qc] + WIN_C:
                sel[kc - qc + WIN_C - 1, kc, qc] = 1.0
            else:
                sel[31, kc, qc] = 1.0
    sel = np.concatenate([sel, sel], 2).reshape(32, GRID_W * P)
    return {
        "four": four, "fourk": fourk, "zfeat": np.ascontiguousarray(z),
        "decay": np.ascontiguousarray(decay.reshape(KT, P, HY).transpose(1, 0, 2)),
        "sel": np.ascontiguousarray(sel), "ident": np.eye(P, dtype=np.float32),
        "ones": np.ones((P, P), np.float32),
    }


def units():
    out = []
    for r in range(0, ROWS, 2):
        k0 = min(max(r - WIN_R // 2, 0), ROWS - WIN_R)
        k1 = min(max(r + 1 - WIN_R // 2, 0), ROWS - WIN_R) + WIN_R
        if k1 - k0 > WIN_R:
            out.append((r, k0, k1 - k0, 14))
        else:
            out.append((r, k0, k1 - k0, k0 - r + 7 - 1))
    return out


UNITS = units()


def program(nc, A, out):
    ctx = ExitStack()
    with ctx:
        base = 16512

        def at(name, off, shape, dt=F32):
            return nc.alloc_sbuf_tensor_at(name, [P] + list(shape), dt, offset=base + off)

        def sem(name):
            return ctx.enter_context(nc.semaphore(name))

        P_HY, P_Q, P_KV, P_XG, H_, S_, SM = 24576, 49152, 65536, 116736, 124928, 157696, 206848
        arena = nc.alloc_sbuf_tensor("arena", [P, 212832 // 4], F32)
        raw = at("raw", 0, [2, D])
        w_hi = at("w_hi", 8192, [2, D], F32R)
        w_lo = at("w_lo", 16384, [2, D], F32R)
        p_hy = at("p_hy", P_HY, [6, SEQ])
        p_q = at("p_q", P_Q, [4, SEQ])
        p_kv = at("p_kv", P_KV, [10, ALL])
        p_xg = at("p_xg", P_XG, [2, SEQ])
        hb_hi = at("hb_hi", H_, [KT, HALF], F32R)
        hb_lo = at("hb_lo", H_ + 16384, [KT, HALF], F32R)
        e_hi = at("e_hi", P_HY, [KT, HALF], F32R)
        e_lo = at("e_lo", P_HY + 16384, [KT, HALF], F32R)
        o_hi = at("o_hi", P_HY + 32768, [KT, HALF], F32R)
        o_lo = at("o_lo", P_HY + 49152, [KT, HALF], F32R)
        kt_ = at("kt_", 90112, [2, 2, 2, HY])
        eo = at("eo", 98304, [2, 2, HY])
        kabs = at("kabs", 102400, [2, D])
        inv = at("inv", 110592, [2, HY])
        inv_t = at("inv_t", 112640, [2, HY])
        zf = at("zf", H_, [SEQ])
        farg = at("farg", H_ + 4096, [SEQ])
        fturn = at("fturn", H_ + 8192, [SEQ])
        h1 = at("h1", H_ + 12288, [SEQ])
        h2f = at("h2f", H_ + 16384, [SEQ])
        w3s = at("w3s", H_ + 20480, [D])
        w12 = at("w12", H_ + 24576, [2, 64])
        rowsA = at("rowsA", H_ + 25600, [P])
        rowsB = at("rowsB", H_ + 26112, [P])
        rowsC = at("rowsC", H_ + 26624, [P])
        kspec = at("kspec", S_, [KT, 2, 2, HY])
        ada0 = at("ada0", S_ + 32768, [2, D])
        dec = at("dec", S_ + 40960, [KT, HY])
        xin = at("xin", S_ + 32768, [2, D])
        xmod = at("xmod", S_ + 40960, [2, D])
        l_u = at("l_u", H_, [ALL])
        l_r = at("l_r", H_ + 5120, [ALL])
        l_i = at("l_i", H_ + 10240, [ALL])
        l_s = at("l_s", H_ + 15360, [ALL])
        l_q = at("l_q", H_ + 20480, [ALL])
        l_a = at("l_a", H_ + 25600, [ALL])
        l_h = at("l_h", S_ + 32768, [2, ALL])
        l_w = at("l_w", S_ + 32768 + 10240, [8, P])
        tm = at("tm", H_, [KT, 3, HY])
        conv = at("conv", H_ + 24576, [2, SEQ])
        y_hi = at("y_hi", P_HY, [KT, 2, HY], F32R)
        y_lor = at("y_lor", P_HY + 16384, [KT, HY], F32R)
        y_loi = at("y_loi", H_ + 24576, [KT, HY], F32R)
        u_hi = at("u_hi", S_ + 32768, [KT, HY], F32R)
        u_lo = at("u_lo", S_ + 40960, [KT, HY], F32R)
        hy0 = P_KV + 8 * 5120
        prodA = at("prodA", hy0, [2, HY])
        prodB = at("prodB", hy0 + 2048, [2, HY])
        ysum = at("ysum", hy0 + 4096, [2, HY])
        hyb = at("hyb", hy0 + 6144, [2, HY])
        zb = at("zb", hy0 + 8192, [HY])
        zs = at("zs", hy0 + 9216, [HY])
        mix_hy = at("mix_hy", P_HY, [2, SEQ])
        bias = at("bias", H_, [HEADS, 23, GRID_W])
        A0 = H_ + 47104
        selt = at("selt", A0, [GRID_W, P])
        sc = at("sc", A0, [2, 832])
        pr = at("pr", A0 + 6656, [2, 832])
        pT = at("pT", A0 + 13312, [2, 7, P])
        qst = at("qst", A0 + 20480, [SEQ])
        kst = at("kst", A0 + 24576, [ALL])
        vst = at("vst", A0 + 29696, [ALL])
        vtm = at("vtm", P_HY + 8192, [10, P])
        bst = [at("bst0", hy0, [23, GRID_W]), at("bst1", 16384, [23, GRID_W])]
        onrm = at("onrm", P_HY + 13312, [2, P])
        rpbt = at("rpbt", P_HY + 14336, [120])
        rpbr = at("rpbr", P_HY + 14848, [32])
        ada1 = at("ada1", P_HY + 16384, [2, D])
        x1 = at("x1", S_, [KT, SEQ])
        yo = [at("yo0", P_KV, [KT, HALF]), at("yo1", P_KV + 16384, [KT, HALF])]
        xr2 = at("xr2", P_HY + 8192, [4, D])
        yd = at("yd", S_ + 32768, [KT, HALF])
        a_hi = at("a_hi", P_HY, [FT, HALF], F32R)
        a_lo = at("a_lo", P_HY + 45056, [FT, HALF], F32R)
        F0 = P_HY + 90112
        g_t = at("g_t", F0, [HALF])
        g_s = at("g_s", F0 + 2048, [HALF])
        sq = at("sq", F0, [2, HALF])
        a_f = at("a_f", F0 + 4096, [HALF])
        rstd = at("rstd", F0 + 6144, [HALF])
        nrm = at("nrm", F0 + 8192, [HALF])
        so = [SM]

        def small(name, shape):
            n = 4 * int(np.prod(shape))
            n = -(-n // 32) * 32
            t = at(name, so[0], shape)
            so[0] += n
            assert so[0] <= 212832 - 0, so[0]
            return t

        ident = small("ident", [P])
        ones = small("ones", [P])
        colA = small("colA", [96])
        colB = small("colB", [48])
        colC = small("colC", [4])
        sil = small("sil", [2, KT])
        sil_t = small("sil_t", [16])
        mod = small("mod", [48, 2])
        amix = small("amix", [KT, 2])
        affn = small("affn", [KT])
        gmix = small("gmix", [KT])
        gffn = small("gffn", [KT])
        ssq = small("ssq", [10])
        rx = small("rx", [10])
        lam = small("lam", [8, 4])
        hbias = small("hbias", [8])
        amax = small("amax", [2, 4])
        asum = small("asum", [2, 4])

        ps = ctx.enter_context(nc.psum_tensor("ps", [P, 8, 512], F32))

        raw_ld = [sem("raw_ld0"), sem("raw_ld1")]
        hi_done, lo_done, job_done, acc_free = sem("hi_done"), sem("lo_done"), sem("job_done"), sem("acc_free")
        ada_ld = [sem("ada_ld0"), sem("ada_ld1")]
        mod_done = sem("mod_done")
        par_ld, flt_ld, dec_ld = sem("par_ld"), sem("flt_ld"), sem("dec_ld")
        x_ld = [sem("x_ld0"), sem("x_ld1")]
        dchain = sem("dchain")
        achain = sem("achain")
        cols_ps, cols_ok = sem("cols_ps"), sem("cols_ok")
        silt_ok, sil_ok, silp_ok = sem("silt_ok"), sem("sil_ok"), sem("silp_ok")
        f_ps, f_arg, f_sin = sem("f_ps"), sem("f_arg"), sem("f_sin")
        k_ps, k_dec, k_abs, k_eo, k_hi, k_lo, k_sum = [sem("k_" + n) for n in ("ps", "dec", "abs", "eo", "hi", "lo", "sum")]
        amix_ok = sem("amix_ok")
        x_sq, x_rs, x_sqrt, x_n, x_tp, x_mod, x_hi, x_lo = [sem("x_" + n) for n in ("sq", "rs", "sqrt", "n", "tp", "mod", "hi", "lo")]
        lw_ld, l_conv, l_gp, l_gate, l_dve, l_act, l_done, lam_a, lam_d, l_zero = [
            sem(n) for n in ("lw_ld", "l_conv", "l_gp", "l_gate", "l_dve", "l_act", "l_done", "lam_a", "lam_d", "l_zero")]
        hyb_ld, c_ok, c_tp, c_ev, u_hi_ok, u_lo_ok, y_f, y_h, y_l, inv_free, z_ok, z_tp, z_ev = [
            sem(n) for n in ("hyb_ld", "c_ok", "c_tp", "c_ev", "u_hi_ok", "u_lo_ok", "y_f", "y_h", "y_l",
                             "inv_free", "z_ok", "z_tp", "z_ev")]
        sel_ld, rp_tp, rp_ok, b_ps, b_evd, b_eva, b_ok = [
            sem(n) for n in ("sel_ld", "rp_tp", "rp_ok", "b_ps", "b_evd", "b_eva", "b_ok")]
        st_free, st_ok, v_tp, v_ev, qk_done, mx_ok, exp_ok, t_done, pt_d, pt_a, pv_done, rec_ok, o_ok, ot_done, ot_free, modp, att_x = [
            sem(n) for n in ("st_free", "st_ok", "v_tp", "v_ev", "qk_done", "mx_ok", "exp_ok", "t_done", "pt_d",
                             "pt_a", "pv_done", "rec_ok", "o_ok", "ot_done", "ot_free", "modp", "att_x")]
        m_hi, m_lo, xr_ld, gates_ok, n_sq, n_ps, n_var, n_sqrt, n_fin, n_tp, n_x1, n_h, n_hh, n_hl, bst_ok, f_mm = [
            sem(n) for n in ("m_hi", "m_lo", "xr_ld", "gates_ok", "n_sq", "n_ps", "n_var", "n_sqrt", "n_fin",
                             "n_tp", "n_x1", "n_h", "n_hh", "n_hl", "bst_ok", "f_mm")]
        g_tanh, g_a, g_ah, g_al, dn_done, dn_free, y_ok = [
            sem(n) for n in ("g_tanh", "g_a", "g_ah", "g_al", "dn_done", "dn_free", "y_ok")]
        o_tp, o_ev, st_out = sem("o_tp"), sem("o_ev"), [sem("st_out0"), sem("st_out1")]

        block = ctx.enter_context(nc.Block())

        w_in = A["w_in"][0].rearrange("(k p) n -> p k n", p=P)
        w_out = A["w_out"][0].rearrange("(k p) n -> p k n", p=P)
        w_gu = A["ffn_w_gu"][0].rearrange("(k p) n -> p k n", p=P)
        w_dn = A["ffn_w_down"][0].rearrange("(k p) n -> p k n", p=P)
        ada = A["ada_w"][0].rearrange("(k p) n -> p k n", p=P)
        x_tok = A["x"][0]
        c_tok = A["ctx"][0]

        BLOCKS = [(c_tok, 0, 2, 1, J_CTX, 10), (x_tok, 0, 4, 0, J_LAT, 22), (x_tok, 4, 4, 0, J_LAT + 22, 22)]
        TILES = [(src, t0 + t) for src, t0, cnt, _, _, _ in BLOCKS for t in range(cnt)]
        HS = [slice(0, HALF), slice(HALF, SEQ)]

        def mix_src(k, h):
            src = (mix_hy[:, k] if k < 2 else p_q[:, k - 2] if k < 6 else p_xg[:, k - 6])
            return src[:, HS[h]]

        def bias_ps(g, half):
            v = ps[64 * half:64 * half + 64, g % 4, 0:480].rearrange("p (j h r) -> p h r j", j=4, h=HEADS)
            return v[:, :, 1:15, :] if half == 0 else v[:, :, 0:14, :]

        def s_all(s):
            return ps[:, 2 * (s % 2):2 * (s % 2) + 2, :].rearrange("p a b -> p (a b)")

        @block.sync
        def _(sp):
            sp.dma_start(ident[:], A["ident"]).then_inc(par_ld, 16)
            sp.dma_start(ones[:], A["ones"]).then_inc(par_ld, 16)
            r8 = lambda ap: ap.rearrange("(k p) -> k p", p=P)
            off = 0
            for src in [A[n][0] for n in ("g_mix_pre", "g_mix_post", "g_ffn_pre", "g_ffn_post", "ada_b", "c")] + [A["c_ctx"]]:
                src = r8(src)
                sp.dma_start(rowsA[off:off + src.shape[0], :], src).then_inc(par_ld, 16)
                off += src.shape[0]
            off = 0
            for name in ("hy_conv_w", "hy_conv_b", "lru_conv_w", "lru_conv_b", "lru_ba", "lru_bi", "lru_lam"):
                src = A[name][0] if len(A[name].shape) == 3 else A[name]
                for r in range(src.shape[0]):
                    v = r8(src[r])
                    sp.dma_start(rowsB[off:off + v.shape[0], :], v).then_inc(par_ld, 16)
                    off += v.shape[0]
            sp.dma_start(rowsC[0:1, 0:64], A["hy_f_b1"]).then_inc(par_ld, 16)
            sp.dma_start(rowsC[1:2, 0:64], A["hy_f_b2"]).then_inc(par_ld, 16)
            sp.dma_start(rowsC[2:4, 0:64], A["hy_f_freq"][0]).then_inc(par_ld, 16)
            sp.dma_start(zf[0:33, :], A["zfeat"]).then_inc(flt_ld, 16)
            sp.dma_start(w12[0:33, 0, :], A["hy_f_w1"][0]).then_inc(flt_ld, 16)
            sp.dma_start(w12[0:64, 1, :], A["hy_f_w2"][0]).then_inc(flt_ld, 16)
            sp.dma_start(w3s[0:64, :], A["hy_f_w3"][0]).then_inc(flt_ld, 16)
            sp.dma_start(dec[:], A["decay"]).then_inc(dec_ld, 16)

            def raw_dma(b, J, src, nk=KT, first=False):
                if not first:
                    sp.wait_ge(lo_done, J - 1)
                sp.dma_start(raw[:, b, 0:nk * P].rearrange("p (k n) -> p k n", n=P), src).then_inc(raw_ld[b], 16)

            def phase(J0, pairs, src, begin=1):
                with sp.Fori(begin, pairs) as i:
                    for b in range(2):
                        raw_dma(b, i * 2 + (J0 + b), src(i, b))

            def pair0(J0, src):
                for b in range(2):
                    raw_dma(b, J0 + b, src(0, b), first=J0 == 0)

            fk = A["fourk"].rearrange("m c p n -> (m c) p n")
            f4 = A["four"].rearrange("m c p n -> (m c) p n")
            one = lambda ap: ap.rearrange("o p (k n) -> p (o k) n", n=P)
            src_k = lambda i, b: one(fk[ds(i * 2 + b, 1)])
            src_4 = lambda i, b: one(f4[ds(i * 2 + b, 1)])
            src_c = lambda i, b: w_in[:, :, ds((i * 2 + (10 + b)) * P, P)]
            src_l = lambda i, b: w_in[:, :, ds((i * 2 + b) * P, P)]
            src_o = lambda i, b: w_out[:, :, ds((i * 2 + b) * P, P)]
            src_g = lambda i, b: w_gu[:, :, ds(i * P + b * FF, P)]

            pair0(J_K, src_k)
            for n in range(16):
                if n >= 2:
                    sp.wait_ge(mod_done, n - 1)
                sp.dma_start(ada0[:, n % 2, :].rearrange("p (k n) -> p k n", n=P),
                             ada[:, :, n * P:(n + 1) * P]).then_inc(ada_ld[n % 2], 16)
            phase(J_K, 8, src_k)
            pair0(J_CTX, src_c)
            phase(J_CTX, 5, src_c)
            pair0(J_LAT, src_l)
            phase(J_LAT, 11, src_l)
            pair0(J_LAT + 22, src_l)
            phase(J_LAT + 22, 11, src_l)
            pair0(J_HY, src_4)
            sp.wait_ge(l_zero, 1)
            for g, name in enumerate(("lru_wa", "lru_wi")):
                for d in range(2):
                    for c in range(2):
                        for e in range(2):
                            sp.dma_start(l_w[64 * e:64 * e + 64, g * 4 + d * 2 + c, 64 * e:64 * e + 64],
                                         A[name][0, d, 2 * c + e]).then_inc(lw_ld, 16)
            sp.wait_ge(l_done, 4)
            sp.dma_start(hyb[:].rearrange("p a b -> p (a b)"),
                         A["hy_bias"].rearrange("a o c -> a (o c)").broadcast_to([P, 2 * HY])).then_inc(hyb_ld, 16)
            for p in range(4):
                phase(J_HY + 16 * p, 8, src_4)
                if p < 3:
                    pair0(J_HY + 16 * (p + 1), src_4)
            pair0(J_OUT, src_o)
            sp.wait_ge(z_tp, 2)
            sp.dma_start(selt[0:32, :, :], A["sel"].rearrange("j (k q) -> j k q", q=P)).then_inc(sel_ld, 16)
            sp.dma_start(rpbr[0:120, 0:31], A["na_rpb"][0].rearrange("h r c -> (h r) c")).then_inc(sel_ld, 16)
            for b in range(2):
                sp.dma_start(ada1[:, b, :].rearrange("p (k n) -> p k n", n=P),
                             ada[:, :, (16 + b) * P:(17 + b) * P]).then_inc(ada_ld[b], 16)
            with sp.Fori(1, 16) as i:
                for b in range(2):
                    sp.wait_ge(mod_done, i * 2 + (15 + b))
                    sp.dma_start(ada1[:, b, :].rearrange("p (k n) -> p k n", n=P),
                                 ada[:, :, ds((i * 2 + (16 + b)) * P, P)]).then_inc(ada_ld[b], 16)
            phase(J_OUT, 4, src_o)
            pair0(J_OUT + 8, src_o)
            phase(J_OUT + 8, 4, src_o)
            pair0(J_FFN, src_g)
            for h in range(2):
                if h == 0:
                    sp.wait_ge(mod_done, 48)
                    sp.wait_ge(o_ok, 64)
                    sp.wait_ge(pv_done, 64)
                else:
                    sp.wait_ge(n_tp, 8)
                for q in range(4):
                    sp.dma_start(xr2[:, q, :], x_tok[(4 * h + q) * P:(4 * h + q + 1) * P, :]).then_inc(xr_ld, 16)
            for h in range(2):
                J0 = J_FFN + h * (GU_JOBS + DOWN_JOBS)
                phase(J0, FT, src_g)
                J0 += GU_JOBS
                with sp.Fori(0, 4) as i:
                    for q in range(6):
                        c = q % 3
                        nk = KT if c < 2 else FT - 2 * KT
                        raw_dma(q % 2, i * 6 + (J0 + q),
                                w_dn[:, c * KT:c * KT + nk, ds((i * 2 + q // 3) * P, P)], nk)
                if h == 0:
                    pair0(J0 + DOWN_JOBS, src_g)
                for q in range(4):
                    sp.wait_ge(o_ev, 4 * h + q + 1)
                    sp.dma_start(out[0, (4 * h + q) * P:(4 * h + q + 1) * P, :], xin[:, q % 2, :]).then_inc(st_out[q % 2], 16)
            for b in range(2):
                sp.wait_ge(st_out[b], 64)

        @block.scalar
        def _(act):
            def split(J, half, b, first=False):
                act.wait_ge(raw_ld[b], half * 16 + 16)
                if not first:
                    act.wait_ge(job_done, J - 1)
                act.activation(w_hi[:, b, :], raw[:, b, :], ACT.Copy).then_inc(hi_done, 1)

            def split_next(i, J0, b):
                split(i * 2 + (J0 + b + 1), i + (J0 // 2 + b), 1 - b)

            def split_loop(n, J0):
                with act.Fori(0, n // 2) as i:
                    for b in range(2):
                        split_next(i, J0, b)

            def x_dma(n):
                src, t = TILES[n]
                act.dma_start(xin[:, n % 2, :], src[t * P:(t + 1) * P, :]).then_inc(x_ld[n % 2], 16)

            act.wait_ge(cols_ok, 1)
            act.activation(sil_t[:], colA[:, 80:96], ACT.Tanh, scale=0.5).then_inc(silt_ok, 1)
            for layer, dst in ((0, h1), (1, h2f)):
                act.wait_ge(f_arg, layer + 1)
                act.activation(dst[0:64, :], farg[0:64, :], ACT.Sin).then_inc(f_sin, 1)
            split(0, 0, 0, first=True)
            split(1, 0, 1, first=True)
            for t in range(KT):
                s = t % 2
                act.wait_ge(k_dec, t + 1)
                if t >= 2:
                    act.wait_ge(k_sum, t - 1)
                act.activation(kabs[:, s, :], kt_[:, s].rearrange("p a b c -> p (a b c)"), ACT.Abs).then_inc(k_abs, 1)
                act.wait_ge(k_eo, t + 1)
                act.activation(e_hi[:, t, :], eo[:, 0].rearrange("p a b -> p (a b)"), ACT.Copy)
                act.activation(o_hi[:, t, :], eo[:, 1].rearrange("p a b -> p (a b)"), ACT.Copy).then_inc(k_hi, 1)
            with act.Fori(1, 8) as i:
                for b in range(2):
                    split(i * 2 + (J_K + b), i + J_K // 2, b)
            split(J_CTX, J_CTX // 2, 0)
            act.wait_ge(mod_done, 16)
            act.wait_ge(k_lo, KT)
            act.wait_ge(k_dec, KT)
            x_dma(0)
            x_dma(1)
            n = 0
            for blk, (_, _, cnt, _, J0, jobs) in enumerate(BLOCKS):
                for t in range(cnt):
                    act.wait_ge(x_ld[n % 2], 16 * (n // 2 + 1))
                    act.activation(xmod[:, 0, :], xin[:, n % 2, :], ACT.Square,
                                   accum_out=ssq[:, n:n + 1]).then_inc(x_sq, 1)
                    act.wait_ge(x_rs, n + 1)
                    act.activation(rx[:, n:n + 1], rx[:, n:n + 1], ACT.Sqrt).then_inc(x_sqrt, 1)
                    act.wait_ge(x_mod, n + 1)
                    if n + 2 < len(TILES):
                        x_dma(n + 2)
                    if t == 0:
                        act.wait_ge(job_done, J0)
                    act.activation(hb_hi[:, :, t * P:(t + 1) * P],
                                   xmod[:, 1, :].rearrange("p (k n) -> p k n", n=P), ACT.Copy).then_inc(x_hi, 1)
                    n += 1
                split_loop(jobs, J0)

            act.wait_ge(lam_d, 1)
            act.activation(lam[:, 1, :], lam[:, 0, :], ACT.Exp, scale=-1.0).then_inc(lam_a, 1)
            act.wait_ge(lam_d, 2)
            for c in range(2):
                for d in range(2):
                    q = c * 2 + d
                    if q:
                        act.wait_ge(l_done, q)
                    for g, dst in ((0, l_r), (1, l_i)):
                        for part, (o0, w) in enumerate(((0, 256), (256, 512), (768, 512))):
                            act.wait_ge(l_gp, (q * 2 + g) * 3 + part + 1)
                            act.activation(dst[:, o0:o0 + w], ps[:, g * 3 + part, 0:w], ACT.Tanh, scale=0.5,
                                           bias=hbias[:, g * 4 + d * 2 + c:g * 4 + d * 2 + c + 1]).then_inc(l_gate, 1)
                    act.wait_ge(l_gate, q * 6 + 6)
                    act.activation(l_s[:], l_r[:], ACT.Tanh, scale=lam[:, 2, d * 2 + c:d * 2 + c + 1],
                                   bias=lam[:, 2, d * 2 + c:d * 2 + c + 1]).then_inc(l_act, 1)
                    act.wait_ge(l_act, 5 * c + 2 * d + 1)
                    act.activation(l_r[:], l_s[:], ACT.Sqrt).then_inc(l_act, 1)
                act.wait_ge(l_dve, c + 1)
                act.activation(l_s[:, 0:SEQ], l_q[:, 0:SEQ], ACT.Tanh, scale=0.7978845608028654).then_inc(l_act, 1)

            for c in range(6):
                act.wait_ge(c_tp, c + 1)
                act.activation(tm[:, :, c // 2, (c % 2) * P:(c % 2) * P + P],
                               ps[:, 4 + 2 * (c % 2):6 + 2 * (c % 2), :].rearrange("p a (t n) -> p (a t) n", n=P),
                               ACT.Copy).then_inc(c_ev, 1)
            act.wait_ge(c_ev, 2)
            act.activation(u_hi[:], tm[:, :, 0, :], ACT.Copy).then_inc(u_hi_ok, 1)
            for o in range(2):
                J0 = J_HY + 32 * o
                with act.Fori(0, 8) as i:
                    for b in range(2):
                        split_next(i, J0, b)
                    act.wait_ge(y_f, i + (8 * o + 1))
                    act.wait_ge(cols_ok, 1)
                    act.activation(y_hi[:, ds(i, 1)].rearrange("p a b c -> p (a b) c"), ysum[:], ACT.Copy).then_inc(y_h, 1)
                J0 += 16
                with act.Fori(0, 8) as i:
                    for b in range(2):
                        split_next(i, J0, b)
                    if o == 0:
                        act.wait_ge(z_ok, i + 1)
                        act.wait_ge(cols_ok, 1)
                        act.activation(u_hi[:, ds(i, 1), :].rearrange("p a c -> p (a c)"),
                                       tm[:, ds(i, 1), 0, :].rearrange("p a c -> p (a c)"), ACT.Copy).then_inc(u_hi_ok, 1)

            for g in range(1, 16, 2):
                act.wait_ge(b_ps, g + 1)
                act.activation(bias[0:64, :, 0:14, 4 * g:4 * g + 4], bias_ps(g, 0), ACT.Copy)
                act.activation(bias[64:128, :, 0:14, 4 * g:4 * g + 4], bias_ps(g, 1), ACT.Copy).then_inc(b_eva, 1)
            with act.Fori(0, 4) as hp:
                act.wait_ge(v_tp, hp + 1)
                act.activation(vtm[:, 4:8, :], ps[:, 5, :].rearrange("p (a b) -> p a b", b=P), ACT.Copy)
                act.activation(vtm[:, 8:10, :], ps[:, 6, 0:256].rearrange("p (a b) -> p a b", b=P), ACT.Copy).then_inc(v_ev, 1)
                for s in range(18):
                    if s < 16:
                        L = UNITS[s // 2][2] * GRID_W
                        if s >= 2:
                            act.wait_ge(t_done, hp * 16 + (s - 1))
                            act.wait_ge(rec_ok, hp * 16 + (s - 1))
                        act.wait_ge(mx_ok, hp * 16 + (s + 1))
                        act.activation(pr[:, s % 2, 0:L], sc[:, s % 2, 0:L], ACT.Exp,
                                       bias=amax[:, s % 2, 2:3], accum_out=asum[:, s % 2, 0:1])
                        act.activation(pr[:, s % 2, L:L + CTX], s_all(s)[:, L:L + CTX], ACT.Exp,
                                       bias=amax[:, s % 2, 2:3], accum_out=asum[:, s % 2, 1:2]).then_inc(exp_ok, 1)
                    if 1 <= s <= 16:
                        u = s - 1
                        act.wait_ge(t_done, hp * 16 + (u + 1))
                        if u >= 2:
                            act.wait_ge(pv_done, hp * 16 + (u - 1))
                        ins = act.activation(pT[:, u % 2, 4:6, :],
                                             ps[:, 6, 0:256].rearrange("p (a b) -> p a b", b=P), ACT.Copy)
                        if UNITS[u // 2][2] > WIN_R:
                            ins = act.activation(pT[0:64, u % 2, 6, :], ps[0:64, 6, 256:384], ACT.Copy)
                        ins.then_inc(pt_a, 1)
                    if s >= 2:
                        u = s - 2
                        act.wait_ge(rec_ok, hp * 16 + (u + 1))
                        if u // 2 >= 2:
                            act.wait_ge(ot_done, hp * 8 + (u // 2 - 1))
                        act.wait_ge(pv_done, hp * 16 + (u + 1))
                        act.activation(onrm[:, (u // 2) % 2, 64 * (u % 2):64 * (u % 2) + 64],
                                       ps[:, 7, 64 * (u % 2):64 * (u % 2) + 64], ACT.Copy,
                                       scale=asum[:, u % 2, 3:4]).then_inc(o_ok, 1)

            act.wait_ge(ot_free, 33)
            for h in range(2):
                if h == 1:
                    act.wait_ge(job_done, J_OUT + 8)
                for k in range(KT):
                    act.activation(hb_hi[:, k, :], mix_src(k, h), ACT.Copy).then_inc(m_hi, 1)
                split_loop(8, J_OUT + 8 * h)

            def squares(N, src, ready):
                for k in range(KT):
                    q = KT * N + k
                    if q >= 2:
                        act.wait_ge(n_ps, q - 1)
                    act.wait_ge(*ready(k))
                    act.activation(sq[:, k % 2, :], src(k), ACT.Square).then_inc(n_sq, 1)
                act.wait_ge(n_var, N + 1)
                act.activation(nrm[:], nrm[:], ACT.Sqrt).then_inc(n_sqrt, 1)

            def h2_heads(h):
                for k in range(KT):
                    act.wait_ge(n_h, KT * h + k + 1)
                    if k == 0:
                        act.wait_ge(job_done, J_FFN + h * GU_JOBS)
                    act.activation(hb_hi[:, k, :], sq[:, k % 2, :], ACT.Copy).then_inc(n_hh, 1)

            norm_b = lambda N, h: squares(N, lambda k: x1[:, k, HS[h]], lambda k: (n_x1, KT * h + k + 1))
            squares(0, lambda k: yo[0][:, k, :], lambda k: (acc_free, E_OUT + 8 + 2))
            norm_b(1, 0)
            h2_heads(0)
            act.wait_ge(n_hl, KT)
            squares(2, lambda k: yo[1][:, k, :], lambda k: (acc_free, E_OUT + 16 + 2))

            for h in range(2):
                J0 = J_FFN + h * (GU_JOBS + DOWN_JOBS)
                with act.Fori(0, FT) as i:
                    split_next(i, J0, 0)
                    act.wait_ge(job_done, i * 2 + (J0 + 1))
                    act.activation(g_t[:], ps[:, 0, :], ACT.Tanh, scale=0.5).then_inc(g_tanh, 1)
                    split_next(i, J0, 1)
                    act.wait_ge(g_a, i + (FT * h + 1))
                    act.wait_ge(cols_ok, 1)
                    act.activation(a_hi[:, ds(i, 1), :].rearrange("p a c -> p (a c)"), a_f[:], ACT.Copy).then_inc(g_ah, 1)
                J0 += GU_JOBS
                with act.Fori(0, 4 - h) as i:
                    for q in range(6):
                        split(i * 6 + (J0 + q + 1), i * 3 + (J0 // 2 + (q + 1) // 2), (q + 1) % 2)
                if h == 1:
                    for q in range(5):
                        split(18 + J0 + q + 1, 9 + J0 // 2 + (q + 1) // 2, (q + 1) % 2)
                squares(3 + 2 * h, lambda k: yd[:, k, :], lambda k: (dn_free, 8 * h + 8 + 2))
                if h == 0:
                    norm_b(4, 1)
                    h2_heads(1)

        @block.gpsimd
        def _(pool):
            def rest(i, J0, b):
                pool.wait_ge(hi_done, i * 2 + (J0 + b + 1))
                pool.tensor_tensor(w_lo[:, b, :], raw[:, b, :], w_hi[:, b, :].bitcast(F32), ALU.subtract).then_inc(lo_done, 1)

            def rests(n, J0):
                with pool.Fori(0, n // 2) as i:
                    for b in range(2):
                        rest(i, J0, b)

            for t in range(KT):
                pool.wait_ge(k_hi, t + 1)
                pool.tensor_tensor(e_lo[:, t, :], eo[:, 0].rearrange("p a b -> p (a b)"), e_hi[:, t, :].bitcast(F32), ALU.subtract)
                pool.tensor_tensor(o_lo[:, t, :], eo[:, 1].rearrange("p a b -> p (a b)"), o_hi[:, t, :].bitcast(F32),
                                   ALU.subtract).then_inc(k_lo, 1)
            rests(16, J_K)
            n = 0
            for blk, (_, _, cnt, _, J0, jobs) in enumerate(BLOCKS):
                for t in range(cnt):
                    pool.wait_ge(x_hi, n + 1)
                    pool.tensor_tensor(hb_lo[:, :, t * P:(t + 1) * P], xmod[:, 1, :].rearrange("p (k n) -> p k n", n=P),
                                       hb_hi[:, :, t * P:(t + 1) * P].bitcast(F32), ALU.subtract).then_inc(x_lo, 1)
                    n += 1
                rests(jobs, J0)
            pool.memset(l_w[:], 0.0).then_inc(l_zero, 1)
            for p in range(4):
                rests(16, J_HY + 16 * p)
            pool.wait_ge(b_evd, 8)
            pool.wait_ge(b_eva, 8)
            pool.tensor_copy(bias[0:64, :, 14:22, :], bias[0:64, :, 2:10, :])
            pool.tensor_copy(bias[64:128, :, 15:23, :], bias[64:128, :, 3:11, :])
            pool.memset(bias[0:64, :, 22:23, :], NEG)
            pool.memset(bias[64:128, :, 14:15, :], NEG).then_inc(b_ok, 1)
            pool.wait_ge(b_ok, 1)
            with pool.Fori(0, 4) as hp:
                pool.wait_ge(st_free, hp + 1)
                pool.wait_ge(b_ok, 1)
                pool.tensor_copy(kst[:], p_kv[:, ds(hp, 1), :].rearrange("p a n -> p (a n)"))
                pool.tensor_copy(qst[:], p_q[:, ds(hp, 1), :].rearrange("p a n -> p (a n)"))
                for hh in range(2):
                    pool.tensor_copy(bst[hh][:].rearrange("p a b -> p (a b)"),
                                     bias[:].rearrange("p h a b -> p h (a b)")[:, ds(hp * 2 + hh, 1), :].rearrange("p o n -> p (o n)"))
                pool.tensor_copy(vst[:], p_kv[:, ds(hp + 4, 1), :].rearrange("p a n -> p (a n)")).then_inc(st_ok, 1)
            for h in range(2):
                for k in range(KT):
                    pool.wait_ge(m_hi, KT * h + k + 1)
                    pool.tensor_tensor(hb_lo[:, k, :], mix_src(k, h), hb_hi[:, k, :].bitcast(F32), ALU.subtract).then_inc(m_lo, 1)
                rests(8, J_OUT + 8 * h)

            def h2_rests(h):
                for k in range(KT):
                    pool.wait_ge(n_hh, KT * h + k + 1)
                    pool.tensor_tensor(hb_lo[:, k, :], sq[:, k % 2, :], hb_hi[:, k, :].bitcast(F32), ALU.subtract).then_inc(n_hl, 1)

            for h in range(2):
                h2_rests(h)
                rests(GU_JOBS + DOWN_JOBS, J_FFN + h * (GU_JOBS + DOWN_JOBS))

        @block.vector
        def _(dve):
            class Chain:

                def __init__(self):
                    self.n, self.i, self.per = 0, None, 0

                def __call__(self, ins):
                    ins.then_inc(dchain, 1)
                    self.n += 1
                    dve.wait_ge(dchain, self.n if self.i is None else self.i * self.per + self.n)

                def loop(self, i, per):
                    self.i, self.per, self.start = i, per, self.n

                def end(self, times):
                    assert self.n - self.start == self.per, (self.n - self.start, self.per)
                    self.n, self.i = self.start + self.per * times, None

            link = Chain()

            def evac(i, J, dst, scale=1.0):
                dve.wait_ge(job_done, J + 1)
                dve.tensor_scalar(dst, i, scale, None, ALU.mult).then_inc(acc_free, 1)

            for _ in range(2):
                dve.nop().then_inc(acc_free, 1)
                dve.nop().then_inc(inv_free, 1)
                dve.nop().then_inc(dn_free, 1)
            dve.nop().then_inc(ot_free, 1)
            dve.nop().then_inc(modp, 1)
            dve.nop().then_inc(st_free, 1)

            dve.wait_ge(cols_ps, 1)
            dve.tensor_copy(colA[:], ps[:, 2, 0:96])
            dve.tensor_copy(colB[:, 0:46], ps[:, 2, 96:142])
            dve.tensor_copy(colC[0:64, :], ps[0:64, 2, 142:146]).then_inc(cols_ok, 1)
            dve.wait_ge(cols_ok, 1)
            dve.wait_ge(silt_ok, 1)
            link(dve.scalar_tensor_tensor(sil_t[:], sil_t[:], 1.0, colA[:, 80:96], ALU.add, ALU.mult))
            dve.tensor_scalar(sil[:].rearrange("p a b -> p (a b)"), sil_t[:], 0.5, None, ALU.mult).then_inc(sil_ok, 1)

            for layer in range(2):
                dve.wait_ge(f_ps, layer + 1)
                z = ps[0:64, 4 + 2 * layer:6 + 2 * layer, :].rearrange("p a b -> p (a b)")
                if layer == 1:
                    dve.wait_ge(f_sin, 1)
                link(dve.tensor_scalar(farg[0:64, :], z, colC[0:64, layer:layer + 1], colC[0:64, 2 + layer:3 + layer],
                                       ALU.add, ALU.mult))
                link(dve.tensor_scalar(fturn[0:64, :], farg[0:64, :], 1.0 / (2 * math.pi), MAGIC, ALU.mult, ALU.add))
                link(dve.tensor_scalar(fturn[0:64, :], fturn[0:64, :], MAGIC, None, ALU.subtract))
                for part in (TWO_PI_HEAD, TWO_PI_REST):
                    link(dve.scalar_tensor_tensor(farg[0:64, :], fturn[0:64, :], -part, farg[0:64, :], ALU.mult, ALU.add))
                dve.tensor_scalar(farg[0:64, :], farg[0:64, :], 3.1415925, -3.1415925, ALU.min, ALU.max).then_inc(f_arg, 1)

            dve.wait_ge(dec_ld, 16)
            for t in range(KT):
                s = t % 2
                dve.wait_ge(k_ps, t + 1)
                if t >= 2:
                    dve.wait_ge(k_abs, t - 1)
                for o in range(2):
                    link(dve.tensor_tensor(kt_[:, s, o], ps[:, 4 + 2 * s + o, :].rearrange("p (a b) -> p a b", a=2),
                                           dec[:, t:t + 1, :].broadcast_to([P, 2, HY]), ALU.mult))
                if t == 0:
                    link(dve.memset(kt_[0:1, s, :, 1, :], 0.0))
                dve.nop().then_inc(k_dec, 1)
                if t >= 1:
                    dve.wait_ge(k_hi, t)
                    dve.wait_ge(k_lo, t)
                dve.tensor_tensor(eo[:, 0], kt_[:, s, :, 0, :], kt_[:, s, :, 1, :], ALU.add)
                dve.tensor_tensor(eo[:, 1], kt_[:, s, :, 0, :], kt_[:, s, :, 1, :], ALU.subtract).then_inc(k_eo, 1)
            dve.wait_ge(k_sum, KT)
            dve.tensor_copy(inv_t[:, 0], ps[:, 2, 0:HY])
            link(dve.tensor_copy(inv_t[:, 1], ps[:, 3, 0:HY]))
            for o in range(2):
                link(dve.tensor_tensor(inv_t[:, o], inv_t[:, o], ps[:, 2 + o, HY:2 * HY], ALU.add))
            link(dve.tensor_scalar(inv_t[:], inv_t[:], float(SEQ), None, ALU.mult))
            link(dve.reciprocal(inv[:], inv_t[:]))
            dve.wait_ge(mod_done, 16)
            link(dve.tensor_tensor(mod[:, 0:16, :], ps[:, 7, 0:32].rearrange("p (a b) -> p a b", b=2),
                                   colA[:, 32:48].unsqueeze(2).broadcast_to([P, 16, 2]), ALU.add))
            link(dve.tensor_scalar(amix[:], mod[:, 8:16, :], 1.0, None, ALU.add))
            link(dve.tensor_tensor(amix[:], amix[:], colA[:, 0:8].unsqueeze(2).broadcast_to([P, KT, 2]), ALU.mult))
            with dve.Fori(0, 8) as i:
                for b in range(2):
                    dve.wait_ge(job_done, i * 2 + (J_K + b + 1))
                    dve.tensor_tensor(kspec[:, ds(i, 1), :, b, :].rearrange("p m a c -> p (m a) c"),
                                      ps[:, b, :].rearrange("p (a c) -> p a c", a=2), inv[:], ALU.mult).then_inc(acc_free, 1)

            n = 0
            for blk, (_, _, cnt, cond, J0, jobs) in enumerate(BLOCKS):
                for t in range(cnt):
                    dve.wait_ge(x_sq, n + 1)
                    dve.tensor_scalar(rx[:, n:n + 1], ssq[:, n:n + 1], 1.0 / D, EPS, ALU.mult, ALU.add).then_inc(x_rs, 1)
                    dve.wait_ge(x_sqrt, n + 1)
                    link(dve.reciprocal(rx[:, n:n + 1], rx[:, n:n + 1]))
                    dve.tensor_scalar(xin[:, n % 2, :], xin[:, n % 2, :], rx[:, n:n + 1], None, ALU.mult).then_inc(x_n, 1)
                    dve.wait_ge(x_tp, n + 1)
                    bank = 2 + 2 * (n % 2)
                    src = ps[:, bank:bank + 2, :].rearrange("p a (k n) -> p (a k) n", n=P)
                    x3 = lambda s: xmod[:, s, :].rearrange("p (k n) -> p k n", n=P)
                    col = lambda v: v.broadcast_to([P, KT, P])
                    link(dve.tensor_tensor(x3(0), src, col(amix[:, :, cond:cond + 1]), ALU.mult))
                    if n >= 1:
                        dve.wait_ge(x_lo, n)
                    dve.tensor_tensor(x3(1), x3(0), col(mod[:, 0:8, cond:cond + 1]), ALU.add).then_inc(x_mod, 1)
                    n += 1
                if blk == 0:
                    with dve.Fori(0, 5) as i:
                        for b in range(2):
                            evac(ps[:, b, 0:CTX], i * 2 + (J0 + b),
                                 p_kv[:, ds(i * 2 + b, 1), 0:CTX].rearrange("p a n -> p (a n)"))
                else:
                    hs = HS[blk - 1]
                    lat = slice(CTX + hs.start, CTX + hs.stop)
                    spans = ((0, 6, lambda j: p_hy[:, ds(j, 1), hs], 1.0),
                             (6, 10, lambda j: p_q[:, ds(j, 1), hs], DH ** -0.5),
                             (10, 20, lambda j: p_kv[:, ds(j, 1), lat], 1.0),
                             (20, 22, lambda j: p_xg[:, ds(j, 1), hs], 1.0))
                    for a, z, dst, scale in spans:
                        with dve.Fori(0, (z - a) // 2) as i:
                            for b in range(2):
                                evac(ps[:, b, :], i * 2 + (J0 + a + b), dst(i * 2 + b).rearrange("p a n -> p (a n)"), scale)

            x_, e_, two_sp, mlam, z_, z2, poly = (lam[:, r, :] for r in (0, 1, 2, 3, 4, 5, 6))
            link(dve.tensor_scalar(mlam, colB[:, 42:46], -1.0, None, ALU.mult))
            link(dve.scalar_tensor_tensor(x_, mlam, -1.0, mlam, ALU.mult, ALU.max))
            dve.nop().then_inc(lam_d, 1)
            dve.wait_ge(lam_a, 1)
            link(dve.tensor_scalar(z_, e_, 2.0, None, ALU.add))
            link(dve.reciprocal(z_, z_))
            link(dve.tensor_tensor(z_, z_, e_, ALU.mult))
            link(dve.tensor_tensor(z2, z_, z_, ALU.mult))
            link(dve.tensor_scalar(poly, z2, 1.0 / 19, 1.0 / 17, ALU.mult, ALU.add))
            for k in (15, 13, 11, 9, 7, 5, 3, 1):
                link(dve.tensor_tensor(poly, poly, z2, ALU.mult))
                link(dve.tensor_scalar(poly, poly, 1.0 / k, None, ALU.add))
            link(dve.tensor_tensor(poly, poly, z_, ALU.mult))
            link(dve.tensor_scalar(two_sp, mlam, 0.0, 2.0, ALU.max, ALU.mult))
            link(dve.scalar_tensor_tensor(two_sp, poly, 4.0, two_sp, ALU.mult, ALU.add))
            dve.tensor_scalar(hbias[:], colB[:, 34:42], 0.5, None, ALU.mult).then_inc(lam_d, 1)
            dve.wait_ge(job_done, J_HY)
            dve.wait_ge(x_lo, 10)
            for c in range(2):
                xr = p_kv[:, 8 + c, :]
                w = lambda k: colB[:, 24 + 2 * k + c:25 + 2 * k + c]
                link(dve.tensor_scalar(l_u[:], xr, w(2), colB[:, 32 + c:33 + c], ALU.mult, ALU.add))
                for k, sh in ((0, -2), (1, -1), (3, 1)):
                    for a, z in ((0, CTX), (CTX, ALL)):
                        lo, hi = (a - sh, z) if sh < 0 else (a, z - sh)
                        ins = dve.scalar_tensor_tensor(l_u[:, lo:hi], xr[:, lo + sh:hi + sh], w(k), l_u[:, lo:hi],
                                                       ALU.mult, ALU.add)
                        link(ins)
                dve.nop().then_inc(l_conv, 1)
                for d in range(2):
                    dve.wait_ge(l_act, 5 * c + 2 * d + 2)
                    link(dve.tensor_scalar(l_q[:], l_s[:], 1.0, None, ALU.add))
                    link(dve.reciprocal(l_q[:], l_q[:]))
                    link(dve.scalar_tensor_tensor(l_i[:], l_i[:], 1.0, l_u[:], ALU.add, ALU.mult))
                    link(dve.tensor_tensor(l_i[:], l_i[:], l_q[:], ALU.mult))
                    link(dve.tensor_tensor(l_i[:], l_i[:], l_r[:], ALU.mult))
                    link(dve.tensor_scalar(l_a[:], l_q[:], 2.0, -1.0, ALU.mult, ALU.add))
                    if d == 0:
                        link(dve.tensor_tensor_scan(l_h[:, 0, :], l_a[:], l_i[:], 0.0, ALU.mult, ALU.add))
                    else:
                        link(dve.tensor_tensor_scan(l_h[:, 1, 0:CTX][:, ::-1], l_a[:, 0:CTX][:, ::-1],
                                                    l_i[:, 0:CTX][:, ::-1], 0.0, ALU.mult, ALU.add))
                        link(dve.tensor_tensor_scan(l_h[:, 1, CTX:ALL][:, ::-1], l_a[:, CTX:ALL][:, ::-1],
                                                    l_i[:, CTX:ALL][:, ::-1], l_h[:, 1, 0:1], ALU.mult, ALU.add))
                        xg, hsum, inner = p_xg[:, c, :], l_a[:, 0:SEQ], l_q[:, 0:SEQ]
                        link(dve.tensor_tensor(hsum, l_h[:, 0, CTX:ALL], l_h[:, 1, CTX:ALL], ALU.add))
                        link(dve.tensor_tensor(inner, xg, xg, ALU.mult))
                        link(dve.tensor_scalar(inner, inner, 0.044715, 1.0, ALU.mult, ALU.add))
                        dve.tensor_tensor(inner, inner, xg, ALU.mult).then_inc(l_dve, 1)
                        dve.wait_ge(l_act, 5 * c + 5)
                        link(dve.scalar_tensor_tensor(l_s[:, 0:SEQ], l_s[:, 0:SEQ], 1.0, xg, ALU.add, ALU.mult))
                        link(dve.scalar_tensor_tensor(xg, l_s[:, 0:SEQ], 0.5, hsum, ALU.mult, ALU.mult))
                    dve.nop().then_inc(l_done, 1)

            for c in range(6):
                x, y = p_hy[:, c, :], conv[:, c % 2, :]
                w = lambda k: colB[:, 6 * k + c:6 * k + c + 1]
                if c >= 2:
                    dve.wait_ge(c_tp, c - 1)
                link(dve.tensor_scalar(y, x, w(1), colB[:, 18 + c:19 + c], ALU.mult, ALU.add))
                link(dve.scalar_tensor_tensor(y[:, 1:SEQ], x[:, 0:SEQ - 1], w(0), y[:, 1:SEQ], ALU.mult, ALU.add))
                dve.scalar_tensor_tensor(y[:, 0:SEQ - 1], x[:, 1:SEQ], w(2), y[:, 0:SEQ - 1],
                                         ALU.mult, ALU.add).then_inc(c_ok, 1)
            dve.wait_ge(u_hi_ok, 1)
            dve.tensor_tensor(u_lo[:], tm[:, :, 0, :], u_hi[:].bitcast(F32), ALU.subtract).then_inc(u_lo_ok, 1)
            dve.wait_ge(c_ev, 6)
            dve.wait_ge(hyb_ld, 16)
            for o in range(2):
                J0, E0 = J_HY + 32 * o, E_FWD + 16 * o
                with dve.Fori(0, 8) as i:
                    link.loop(i, 4)
                    k1 = kspec[:, ds(i, 1), o, :, :].rearrange("p m a c -> p (m a) c")
                    bc = lambda bank: ps[:, bank:bank + 1, 0:HY].broadcast_to([P, 2, HY])
                    dve.wait_ge(job_done, i * 2 + (J0 + 1))
                    dve.tensor_tensor(prodA[:], bc(0), k1, ALU.mult).then_inc(acc_free, 1)
                    dve.wait_ge(job_done, i * 2 + (J0 + 2))
                    dve.tensor_tensor(prodB[:, ::-1, :], bc(1), k1, ALU.mult).then_inc(acc_free, 1)
                    dve.wait_ge(acc_free, i * 2 + (E0 + 4))
                    link(dve.tensor_tensor(ysum[:, 0], prodA[:, 0], prodB[:, 0], ALU.subtract))
                    link(dve.tensor_tensor(ysum[:, 1], prodA[:, 1], prodB[:, 1], ALU.add))
                    dve.nop().then_inc(y_f, 1)
                    dve.wait_ge(y_h, i + (8 * o + 1))
                    link(dve.tensor_tensor(y_lor[:, ds(i, 1), :].rearrange("p a c -> p (a c)"), ysum[:, 0],
                                           y_hi[:, ds(i, 1), 0, :].bitcast(F32).rearrange("p a c -> p (a c)"), ALU.subtract))
                    link(dve.tensor_tensor(y_loi[:, ds(i, 1), :].rearrange("p a c -> p (a c)"), ysum[:, 1],
                                           y_hi[:, ds(i, 1), 1, :].bitcast(F32).rearrange("p a c -> p (a c)"), ALU.subtract))
                    dve.nop().then_inc(y_l, 1)
                link.end(8)
                with dve.Fori(0, 4) as i:
                    link.loop(i, 4)
                    for tp in range(2):
                        T = i * 2 + tp
                        row = lambda part: tm[:, ds(T, 1), part, :].rearrange("p a c -> p (a c)")
                        link(dve.tensor_tensor(zb[:], row(0), hyb[:, o], ALU.mult))
                        dve.wait_ge(job_done, i * 4 + (J0 + 16 + 2 * tp + 2))
                        dve.tensor_tensor(zs[:], ps[:, 2 + tp, 0:HY], zb[:], ALU.add).then_inc(inv_free, 1)
                        dve.wait_ge(inv_free, T + (8 * o + 3))
                        dve.tensor_tensor(row(0), zs[:], row(1 + o), ALU.mult).then_inc(z_ok, 1)
                        if o == 0:
                            dve.wait_ge(u_hi_ok, T + 2)
                            link(dve.tensor_tensor(u_lo[:, ds(T, 1), :].rearrange("p a c -> p (a c)"), row(0),
                                                   u_hi[:, ds(T, 1), :].bitcast(F32).rearrange("p a c -> p (a c)"),
                                                   ALU.subtract))
                            dve.nop().then_inc(u_lo_ok, 1)
                        else:
                            dve.wait_ge(z_ok, T + 9)
                            link(dve.tensor_copy(zs[:, 0:2], zb[:, 0:2]))
                link.end(4)
            for c in range(2):
                dve.wait_ge(z_tp, c + 1)
                dve.tensor_copy(mix_hy[:, c, :], ps[:, 4 + 2 * c:6 + 2 * c, :].rearrange("p a b -> p (a b)")).then_inc(z_ev, 1)

            link(dve.memset(rpbt[0:32, :], NEG))
            dve.wait_ge(rp_tp, 1)
            dve.tensor_copy(rpbt[0:31, :], ps[0:31, 2, 0:120]).then_inc(rp_ok, 1)
            for g in range(0, 16, 2):
                dve.wait_ge(b_ps, g + 1)
                dve.tensor_copy(bias[0:64, :, 0:14, 4 * g:4 * g + 4], bias_ps(g, 0))
                dve.tensor_copy(bias[64:128, :, 0:14, 4 * g:4 * g + 4], bias_ps(g, 1)).then_inc(b_evd, 1)
            with dve.Fori(0, 4) as hp:
                dve.wait_ge(st_ok, hp + 1)
                dve.wait_ge(v_tp, hp + 1)
                dve.tensor_copy(vtm[:, 0:4, :], ps[:, 4, :].rearrange("p (a b) -> p a b", b=P)).then_inc(v_ev, 1)
                link.loop(hp, 32)
                for s in range(19):
                    if s < 16:
                        _, _, kr, slot0 = UNITS[s // 2]
                        L, e = kr * GRID_W, s % 2
                        dve.wait_ge(qk_done, hp * 16 + (s + 1))
                        dve.tensor_reduce(amax[:, e, 1:2], s_all(s)[:, L:L + CTX], axis=AX, op=ALU.max)
                        link(dve.tensor_tensor_reduce(out=sc[:, e, 0:L], in0=s_all(s)[:, 0:L],
                                                      in1=bst[e][:, slot0:slot0 + kr, :].rearrange("p a b -> p (a b)"),
                                                      scale=1.0, scalar=-3.0e38, op0=ALU.add, op1=ALU.max,
                                                      accum_out=amax[:, e, 0:1]))
                        dve.tensor_scalar(amax[:, e, 2:3], amax[:, e, 0:1], amax[:, e, 1:2], -1.0,
                                          ALU.max, ALU.mult).then_inc(mx_ok, 1)
                        if s == 15:
                            dve.nop().then_inc(st_free, 1)
                    if 1 <= s <= 16:
                        u = s - 1
                        if u >= 2:
                            dve.wait_ge(pv_done, hp * 16 + (u - 1))
                        dve.wait_ge(t_done, hp * 16 + (u + 1))
                        dve.tensor_copy(pT[:, u % 2, 0:4, :],
                                        ps[:, 4 + u % 2, :].rearrange("p (a b) -> p a b", b=P)).then_inc(pt_d, 1)
                        if u >= 2:
                            dve.wait_ge(o_ok, hp * 16 + (u - 1))
                        link(dve.tensor_tensor(asum[:, u % 2, 2:3], asum[:, u % 2, 0:1], asum[:, u % 2, 1:2], ALU.add))
                        dve.reciprocal(asum[:, u % 2, 3:4], asum[:, u % 2, 2:3]).then_inc(rec_ok, 1)
                    if s >= 4 and s % 2 == 0:
                        qt = (s - 4) // 2
                        dve.wait_ge(ot_done, hp * 8 + (qt + 1))
                        dve.tensor_scalar(p_q[:, ds(hp, 1), qt * P:(qt + 1) * P].rearrange("p a n -> p (a n)"),
                                          ps[:, 7, 128:256], 1.0, None, ALU.mult).then_inc(ot_free, 1)
                link.end(4)
                dve.wait_ge(mod_done, hp * 8 + 24)
                dve.tensor_tensor(mod[:, ds(hp * 8 + 16, 8), :], ps[:, 7, 384:400].rearrange("p (a b) -> p a b", b=2),
                                  colA[:, ds(hp * 8 + 48, 8)].unsqueeze(2).broadcast_to([P, 8, 2]), ALU.add).then_inc(modp, 1)

            dve.wait_ge(modp, 5)
            link(dve.tensor_tensor(gmix[:], mod[:, 16:24, 0], colA[:, 8:16], ALU.mult))
            link(dve.tensor_tensor(gffn[:], mod[:, 40:48, 0], colA[:, 24:32], ALU.mult))
            link(dve.scalar_tensor_tensor(affn[:], mod[:, 32:40, 0], 1.0, colA[:, 16:24], ALU.add, ALU.mult))
            for h in range(2):
                with dve.Fori(0, 4) as i:
                    for b in range(2):
                        evac(ps[:, b, :], i * 2 + (J_OUT + 8 * h + b),
                             yo[h][:, ds(i * 2 + b, 1), :].rearrange("p a n -> p (a n)"))

            def rstd_of(N):
                dve.wait_ge(n_ps, KT * N + KT)
                dve.tensor_scalar(nrm[:], ps[:, 2, :], 1.0 / D, EPS, ALU.mult, ALU.add).then_inc(n_var, 1)
                dve.wait_ge(n_sqrt, N + 1)
                link(dve.reciprocal(rstd[:], nrm[:]))

            def norm_a(N, h):
                rstd_of(N)
                for k in range(KT):
                    link(dve.scalar_tensor_tensor(a_f[:], yo[h][:, k, :], gmix[:, k:k + 1], rstd[:], ALU.mult, ALU.mult))
                    dve.wait_ge(n_tp, KT * h + k + 1)
                    dve.tensor_tensor(x1[:, k, HS[h]], a_f[:], ps[:, 4 + k % 2, :], ALU.add).then_inc(n_x1, 1)
                    dve.wait_ge(n_x1, KT * h + k + 1)

            def norm_b(N, h):
                rstd_of(N)
                for k in range(KT):
                    link(dve.scalar_tensor_tensor(a_f[:], x1[:, k, HS[h]], affn[:, k:k + 1], rstd[:], ALU.mult, ALU.mult))
                    if k >= 2:
                        dve.wait_ge(n_hl, KT * h + k - 1)
                    dve.tensor_scalar(sq[:, k % 2, :], a_f[:], mod[:, 24 + k, 0:1], None, ALU.add).then_inc(n_h, 1)
                    dve.wait_ge(n_h, KT * h + k + 1)

            norm_a(0, 0)
            norm_b(1, 0)
            dve.wait_ge(n_hl, KT)
            norm_a(2, 1)

            for h in range(2):
                J0, E0 = J_FFN + h * (GU_JOBS + DOWN_JOBS), E_GU + h * GU_JOBS
                with dve.Fori(0, FT) as i:
                    link.loop(i, 1)
                    dve.wait_ge(g_tanh, i + (FT * h + 1))
                    dve.scalar_tensor_tensor(g_s[:], g_t[:], 1.0, ps[:, 0, :], ALU.add, ALU.mult).then_inc(acc_free, 1)
                    dve.wait_ge(acc_free, i * 2 + (E0 + 3))
                    dve.wait_ge(job_done, i * 2 + (J0 + 2))
                    dve.scalar_tensor_tensor(a_f[:], g_s[:], 0.5, ps[:, 1, :], ALU.mult, ALU.mult).then_inc(acc_free, 1)
                    dve.wait_ge(acc_free, i * 2 + (E0 + 4))
                    dve.nop().then_inc(g_a, 1)
                    dve.wait_ge(g_ah, i + (FT * h + 1))
                    link(dve.tensor_tensor(a_lo[:, ds(i, 1), :].rearrange("p a c -> p (a c)"), a_f[:],
                                           a_hi[:, ds(i, 1), :].bitcast(F32).rearrange("p a c -> p (a c)"), ALU.subtract))
                    dve.nop().then_inc(g_al, 1)
                link.end(FT)
                J0 += GU_JOBS
                if h == 1:
                    for b in range(2):
                        dve.wait_ge(st_out[b], 32)
                with dve.Fori(0, 4) as i:
                    for f in range(2):
                        dve.wait_ge(job_done, i * 6 + (J0 + 3 * f + 3))
                        dve.tensor_scalar(yd[:, ds(i * 2 + f, 1), :].rearrange("p a n -> p (a n)"),
                                          ps[:, 2 + f, :], 1.0, None, ALU.mult).then_inc(dn_free, 1)
                dve.wait_ge(dn_free, 8 * h + 10)
                rstd_of(3 + 2 * h)
                for k in range(KT):
                    link(dve.scalar_tensor_tensor(a_f[:], yd[:, k, :], gffn[:, k:k + 1], rstd[:], ALU.mult, ALU.mult))
                    link(dve.tensor_tensor(x1[:, k, HS[h]], a_f[:], x1[:, k, HS[h]], ALU.add))
                dve.nop().then_inc(n_fin, 1)
                for q in range(4):
                    o = 4 * h + q
                    dve.wait_ge(o_tp, o + 1)
                    if o >= 2:
                        dve.wait_ge(st_out[q % 2], 16 * (o // 2))
                    dve.tensor_copy(xin[:, q % 2, :],
                                    ps[:, 4 + 2 * (q % 2):6 + 2 * (q % 2), :].rearrange("p a b -> p (a b)")).then_inc(o_ev, 1)
                if h == 0:
                    norm_b(4, 1)

        @block.tensor
        def _(pe):
            def product(J, b, dst, rhs, nk=KT, start=True, stop=True):
                pe.wait_ge(lo_done, J + 1)
                for k in range(nk):
                    x_hi_, x_lo_ = rhs(k)
                    for n, (w, x) in enumerate(((w_hi, x_hi_), (w_hi, x_lo_), (w_lo, x_hi_))):
                        ins = pe.matmul(dst, w[:, b, k * P:(k + 1) * P], x, start=start and k == 0 and n == 0,
                                        stop=stop and k == nk - 1 and n == 2)
                ins.then_inc(job_done, 1)
                return ins

            npar = 2 + 7 + sum(A[n].shape[1] if len(A[n].shape) == 3 else 1 for n in
                               ("hy_conv_w", "hy_conv_b", "lru_conv_w", "lru_conv_b", "lru_ba", "lru_bi", "lru_lam")) + 3
            pe.wait_ge(par_ld, 16 * npar)
            pe.transpose(ps[:, 2, 0:96], rowsA[0:96, :], ident[0:96, 0:96])
            pe.transpose(ps[:, 2, 96:142], rowsB[0:46, :], ident[0:46, 0:46])
            pe.transpose(ps[0:64, 2, 142:146], rowsC[0:4, 0:64], ident[0:4, 0:4]).then_inc(cols_ps, 1)
            pe.wait_ge(flt_ld, 64)
            for j in range(2):
                ins = pe.matmul(ps[0:64, 4 + j, :], w12[0:33, 0, :], zf[0:33, j * 512:(j + 1) * 512], start=True, stop=True)
            ins.then_inc(f_ps, 1)
            pe.wait_ge(f_sin, 1)
            for j in range(2):
                ins = pe.matmul(ps[0:64, 6 + j, :], w12[0:64, 1, :], h1[0:64, j * 512:(j + 1) * 512], start=True, stop=True)
            ins.then_inc(f_ps, 1)
            pe.wait_ge(f_sin, 2)

            def taps(t):
                if t >= 2:
                    pe.wait_ge(k_dec, t - 1)
                for o in range(2):
                    ins = pe.matmul(ps[:, 4 + 2 * (t % 2) + o, :], h2f[0:64, t * P:(t + 1) * P],
                                    w3s[0:64, o * 512:(o + 1) * 512], start=True, stop=True)
                ins.then_inc(k_ps, 1)

            def magnitudes(t):
                pe.wait_ge(k_abs, t + 1)
                for o in range(2):
                    ins = pe.matmul(ps[:, 2 + o, :], ones[:], kabs[:, t % 2, o * 512:(o + 1) * 512], start=t == 0, stop=t == KT - 1)
                ins.then_inc(k_sum, 1)

            taps(0)
            for t in range(KT):
                if t + 1 < KT:
                    taps(t + 1)
                magnitudes(t)

            def modulation(n, slot, count, dst):
                pe.wait_ge(ada_ld[slot], count)
                src = ada0 if dst[0] == 7 else ada1
                for k in range(KT):
                    ins = pe.matmul(ps[:, dst[0], dst[1]:dst[1] + 2], src[:, slot, k * P:(k + 1) * P], sil[:, :, k],
                                    start=k == 0, stop=k == KT - 1)
                ins.then_inc(mod_done, 1)

            pe.wait_ge(sil_ok, 1)
            pe.wait_ge(k_dec, KT)
            for n in range(16):
                modulation(n, n % 2, 16 * (n // 2 + 1), (7, 2 * n))
            pe.wait_ge(k_lo, KT)
            with pe.Fori(0, 8) as i:
                for b, (hi, lo) in enumerate(((e_hi, e_lo), (o_hi, o_lo))):
                    pe.wait_ge(acc_free, i * 2 + (E_K + b + 1))
                    product(i * 2 + (J_K + b), b, ps[:, b, :], lambda k: (hi[:, k, :], lo[:, k, :]))

            n = 0
            for blk, (_, _, cnt, _, J0, jobs) in enumerate(BLOCKS):
                for t in range(cnt):
                    pe.wait_ge(x_n, n + 1)
                    if n >= 2:
                        pe.wait_ge(x_mod, n - 1)
                    for k in range(KT):
                        bank = 2 + 2 * (n % 2) + k // 4
                        ins = pe.transpose(ps[:, bank, (k % 4) * P:(k % 4 + 1) * P], xin[:, n % 2, k * P:(k + 1) * P], ident[:])
                    ins.then_inc(x_tp, 1)
                    n += 1
                pe.wait_ge(x_lo, n)
                w = cnt * P
                with pe.Fori(0, jobs // 2) as i:
                    for b in range(2):
                        pe.wait_ge(acc_free, i * 2 + (J0 + b + 1))
                        product(i * 2 + (J0 + b), b, ps[:, b, 0:w], lambda k: (hb_hi[:, k, 0:w], hb_lo[:, k, 0:w]))

            pe.wait_ge(lw_ld, 256)
            for c in range(2):
                pe.wait_ge(l_conv, c + 1)
                for d in range(2):
                    q = c * 2 + d
                    for g in range(2):
                        for part, (o0, w) in enumerate(((0, 256), (256, 512), (768, 512))):
                            if q:
                                pe.wait_ge(l_gate, (q - 1) * 6 + g * 3 + part + 1)
                            elif g * 3 + part < 2:
                                pe.wait_ge(acc_free, J_HY + 2)
                            pe.matmul(ps[:, g * 3 + part, 0:w], l_w[:, g * 4 + d * 2 + c, :], l_u[:, o0:o0 + w],
                                      start=True, stop=True).then_inc(l_gp, 1)

            for c in range(6):
                pe.wait_ge(c_ok, c + 1)
                if c >= 2:
                    pe.wait_ge(c_ev, c - 1)
                for t in range(KT):
                    bank = 4 + 2 * (c % 2) + t // 4
                    ins = pe.transpose(ps[:, bank, (t % 4) * P:(t % 4 + 1) * P], conv[:, c % 2, t * P:(t + 1) * P], ident[:])
                ins.then_inc(c_tp, 1)
            for o in range(2):
                J0, E0 = J_HY + 32 * o, E_FWD + 16 * o
                pe.wait_ge(u_lo_ok, 1 + 8 * o)
                pe.wait_ge(l_gate, 24)
                with pe.Fori(0, 8) as i:
                    for b in range(2):
                        pe.wait_ge(acc_free, i * 2 + (E0 + b + 1))
                        product(i * 2 + (J0 + b), b, ps[:, b, 0:HY], lambda k: (u_hi[:, k, :], u_lo[:, k, :]))
                pe.wait_ge(y_l, 8 * (o + 1))
                J0 += 16
                with pe.Fori(0, 4) as i:
                    for tp in range(2):
                        pe.wait_ge(inv_free, i * 2 + (8 * o + tp + 1))
                        for b, lo in enumerate((y_lor, y_loi)):
                            product(i * 4 + (J0 + 2 * tp + b), b, ps[:, 2 + tp, 0:HY],
                                    lambda k: (y_hi[:, k, b, :], lo[:, k, :]), start=b == 0, stop=b == 1)
            pe.wait_ge(z_ok, 16)
            for c in range(2):
                for t in range(KT):
                    ins = pe.transpose(ps[:, 4 + 2 * c + t // 4, (t % 4) * P:(t % 4 + 1) * P], tm[:, t, 0, c * P:(c + 1) * P], ident[:])
                ins.then_inc(z_tp, 1)

            pe.wait_ge(sel_ld, 32)
            pe.transpose(ps[0:31, 2, 0:120], rpbr[0:120, 0:31], ident[0:120, 0:120]).then_inc(rp_tp, 1)
            pe.wait_ge(rp_ok, 1)
            for g in range(16):
                if g >= 4:
                    pe.wait_ge(b_evd if g % 2 == 0 else b_eva, (g - 4) // 2 + 1)
                for j in range(4):
                    ins = pe.matmul(ps[:, g % 4, j * 120:(j + 1) * 120], selt[0:32, 4 * g + j, :], rpbt[0:32, :],
                                    start=True, stop=True)
                ins.then_inc(b_ps, 1)
            pe.wait_ge(b_evd, 8)
            pe.wait_ge(b_eva, 8)
            pe.wait_ge(z_ev, 2)
            with pe.Fori(0, 4) as hp:
                pe.wait_ge(st_ok, hp + 1)
                for j in range(10):
                    ins = pe.transpose(ps[:, 4 + j // 4, (j % 4) * P:(j % 4 + 1) * P], vst[:, j * P:(j + 1) * P], ident[:])
                ins.then_inc(v_tp, 1)

                def scores(s):
                    e, (_, k0, kr, _) = s % 2, UNITS[s // 2]
                    if s >= 2:
                        pe.wait_ge(exp_ok, hp * 16 + (s - 1))
                    hh = slice(64 * e, 64 * e + 64)
                    q_ = qst[hh, (s // 2) * P:(s // 2 + 1) * P]
                    L, key0 = kr * GRID_W, CTX + k0 * GRID_W
                    pe.matmul(ps[:, 2 * e, :], q_, kst[hh, key0:key0 + 512], start=True, stop=True)
                    if L > 512:
                        pe.matmul(ps[:, 2 * e + 1, 0:L - 512], q_, kst[hh, key0 + 512:key0 + L], start=True, stop=True)
                    ins = pe.matmul(ps[:, 2 * e + 1, L - 512:L - 512 + CTX], q_, kst[hh, 0:CTX], start=True, stop=True)
                    ins.then_inc(qk_done, 1)

                def turn(u):
                    e, kr = u % 2, UNITS[u // 2][2]
                    L = kr * GRID_W
                    if u == 0:
                        pe.wait_ge(v_ev, hp * 2 + 2)
                    if u >= 2:
                        pe.wait_ge(pt_d, hp * 16 + (u - 1))
                    pe.wait_ge(exp_ok, hp * 16 + (u + 1))
                    for c in range(4):
                        pe.transpose(ps[:, 4 + e, c * P:(c + 1) * P], pr[:, e, c * P:(c + 1) * P], ident[:])
                    if u >= 1:
                        pe.wait_ge(pt_a, hp * 16 + u)
                    for c in range(2):
                        ins = pe.transpose(ps[:, 6, c * P:(c + 1) * P], pr[:, e, L + c * P:L + (c + 1) * P], ident[:])
                    if L > 512:
                        ins = pe.transpose(ps[0:64, 6, 256:384], pr[:, e, 512:576], ident[:])
                    ins.then_inc(t_done, 1)

                def values(u):
                    e, (_, k0, kr, _) = u % 2, UNITS[u // 2]
                    pe.wait_ge(pt_d, hp * 16 + (u + 1))
                    pe.wait_ge(pt_a, hp * 16 + (u + 1))
                    hh = slice(64 * e, 64 * e + 64)
                    o_ = ps[:, 7, 64 * e:64 * e + 64]
                    for c in range(4):
                        pe.matmul(o_, pT[:, e, c, :], vtm[:, 2 + k0 // 2 + c, hh], start=c == 0, stop=False)
                    if kr > WIN_R:
                        pe.matmul(o_, pT[0:64, e, 6, :], vtm[0:64, 2 + k0 // 2 + 4, hh], start=False, stop=False)
                    for c in range(2):
                        ins = pe.matmul(o_, pT[:, e, 4 + c, :], vtm[:, c, hh], start=False, stop=c == 1)
                    ins.then_inc(pv_done, 1)

                for s in range(19):
                    if s < 16:
                        scores(s)
                    if 1 <= s <= 16:
                        turn(s - 1)
                    if s >= 3:
                        pe.wait_ge(o_ok, hp * 16 + (s - 2))
                    if s % 2 == 1 and s < 16:
                        j = s // 2
                        if j == 0:
                            pe.wait_ge(modp, hp + 1)
                        pe.wait_ge(ada_ld[j % 2], hp * 64 + 16 * (8 + j // 2 + 1))
                        for k in range(KT):
                            ins = pe.matmul(ps[:, 7, 384 + 2 * j:386 + 2 * j], ada1[:, j % 2, k * P:(k + 1) * P], sil[:, :, k],
                                            start=k == 0, stop=k == KT - 1)
                        ins.then_inc(mod_done, 1)
                    if s >= 4 and s % 2 == 0:
                        qt = (s - 4) // 2
                        pe.transpose(ps[:, 7, 128:256], onrm[:, qt % 2, :], ident[:]).then_inc(ot_done, 1)
                        pe.wait_ge(ot_free, hp * 8 + (qt + 2))
                    if 2 <= s <= 17:
                        values(s - 2)

            for h in range(2):
                J0 = J_OUT + 8 * h
                pe.wait_ge(m_lo, KT * (h + 1))
                if h == 0:
                    pe.wait_ge(ot_free, 33)
                    pe.wait_ge(modp, 5)
                with pe.Fori(0, 4) as i:
                    for b in range(2):
                        pe.wait_ge(acc_free, i * 2 + (E_OUT + 8 * h + b + 1))
                        product(i * 2 + (J0 + b), b, ps[:, b, :], lambda k: (hb_hi[:, k, :], hb_lo[:, k, :]))

            def sum_squares(N):
                if N:
                    pe.wait_ge(n_var, N)
                for k in range(KT):
                    pe.wait_ge(n_sq, KT * N + k + 1)
                    pe.matmul(ps[:, 2, :], ones[:], sq[:, k % 2, :], start=k == 0, stop=k == KT - 1).then_inc(n_ps, 1)

            def x_turns(h):
                pe.wait_ge(xr_ld, 64 * (h + 1))
                for k in range(KT):
                    if KT * h + k >= 2:
                        pe.wait_ge(n_x1, KT * h + k - 1)
                    for q in range(4):
                        ins = pe.transpose(ps[:, 4 + k % 2, q * P:(q + 1) * P], xr2[:, q, k * P:(k + 1) * P], ident[:])
                    ins.then_inc(n_tp, 1)

            sum_squares(0)
            x_turns(0)
            sum_squares(1)
            sum_squares(2)
            x_turns(1)

            for h in range(2):
                J0, E0 = J_FFN + h * (GU_JOBS + DOWN_JOBS), E_GU + h * GU_JOBS
                pe.wait_ge(n_hl, KT * (h + 1))
                with pe.Fori(0, FT) as i:
                    for b in range(2):
                        pe.wait_ge(acc_free, i * 2 + (E0 + b + 1))
                        product(i * 2 + (J0 + b), b, ps[:, b, :], lambda k: (hb_hi[:, k, :], hb_lo[:, k, :]))
                J0 += GU_JOBS
                pe.wait_ge(g_al, FT * (h + 1))
                if h == 0:
                    pe.wait_ge(n_var, 3)
                with pe.Fori(0, 4) as i:
                    for q in range(6):
                        f, c = q // 3, q % 3
                        nk = KT if c < 2 else FT - 2 * KT
                        if c == 0:
                            pe.wait_ge(dn_free, i * 2 + (8 * h + f + 1))
                        product(i * 6 + (J0 + q), q % 2, ps[:, 2 + f, :],
                                lambda k: (a_hi[:, c * KT + k, :], a_lo[:, c * KT + k, :]), nk, start=c == 0, stop=c == 2)
                pe.wait_ge(dn_free, 8 * h + 10)
                sum_squares(3 + 2 * h)
                pe.wait_ge(n_fin, h + 1)
                for q in range(4):
                    o = 4 * h + q
                    if o >= 2:
                        pe.wait_ge(o_ev, o - 1)
                    for k in range(KT):
                        ins = pe.transpose(ps[:, 4 + 2 * (q % 2) + k // 4, (k % 4) * P:(k % 4 + 1) * P],
                                           x1[:, k, h * HALF + q * P:h * HALF + (q + 1) * P], ident[:])
                    ins.then_inc(o_tp, 1)
                if h == 0:
                    sum_squares(4)


_INS = ['x', 'c', 'ctx', 'c_ctx', 'ada_w', 'ada_b', 'g_mix_pre', 'g_mix_post', 'g_ffn_pre', 'g_ffn_post',
        'w_in', 'w_out', 'hy_conv_w', 'hy_conv_b', 'hy_f_w1', 'hy_f_b1', 'hy_f_w2', 'hy_f_b2', 'hy_f_w3',
        'hy_f_freq', 'hy_bias', 'na_rpb', 'lru_conv_w', 'lru_conv_b', 'lru_wa', 'lru_ba', 'lru_wi', 'lru_bi',
        'lru_lam', 'ffn_w_gu', 'ffn_w_down']


def kernel(**inputs):
    import concourse.bacc as bacc
    from concourse.bass_utils import run_bass_kernel_spmd

    nc = bacc.Bacc("TRN2", target_bir_lowering=False, num_devices=1)
    arrays = {name: np.ascontiguousarray(inputs[name]) for name in _INS}
    arrays.update(host_tables())
    aps = {}
    for name, a in arrays.items():
        aps[name] = nc.dram_tensor(f"in_{name}", a.shape, mybir.dt.from_np(a.dtype), kind="ExternalInput").ap()
    out = nc.dram_tensor("out_y", (1, SEQ, D), F32, kind="ExternalOutput").ap()
    program(nc, aps, out)
    r = run_bass_kernel_spmd(nc, [{f"in_{name}": a for name, a in arrays.items()}], core_ids=[0])
    return r.results[0]["out_y"]
```

```python
import math
from contextlib import ExitStack

import numpy as np

import concourse.bass as bass
from concourse import mybir

F32 = mybir.dt.float32
F32R = mybir.dt.float32r
ALU = mybir.AluOpType
ACT = mybir.ActivationFunctionType
AX = mybir.AxisListType.X
ds = bass.ds

P = 128
D = 1024
SEQ = 1024
CTX = 256
KT = D // P
HALF = 512
GRID_W = 64
ROWS = SEQ // GRID_W
HY = D // 4
HEADS = 8
DH = 64
WIN_R, WIN_C = 8, 16
FF = 2816
FT = FF // P
ALL = CTX + SEQ
NEG = -1e30
EPS = 1e-6
MAGIC = 12582912.0
TWO_PI_HEAD = 6.28125
TWO_PI_REST = 2.0 * math.pi - TWO_PI_HEAD

J_K, J_CTX, J_LAT, J_HY, J_OUT, J_FFN = 0, 16, 26, 70, 134, 150
E_K, E_CTX, E_LAT, E_FWD, E_OUT, E_GU = 0, 16, 26, 70, 102, 118
GU_JOBS, DOWN_JOBS = 2 * FT, 24
LRU_AFTER = (1, 3, 5, 7)
JOBS = J_FFN + 2 * (GU_JOBS + DOWN_JOBS)


def host_tables():
    t = np.arange(SEQ)
    ang4 = 2 * np.pi * (((2 * t[:, None] + 1) * (2 * t[None, :] + 1)) % (8 * SEQ)) / (8 * SEQ)
    angk = 2 * np.pi * ((2 * t[:, None] * (2 * t[None, :] + 1)) % (8 * SEQ)) / (8 * SEQ)

    def tiles(m):
        return np.ascontiguousarray(m.reshape(KT, P, KT, P).transpose(2, 1, 0, 3).reshape(KT, P, D))

    four = np.stack([tiles(np.cos(ang4)), tiles(np.sin(ang4))], 1).astype(np.float32)
    fourk = np.stack([tiles(np.cos(angk)), tiles(np.sin(angk))], 1).astype(np.float32)
    tt = t.astype(np.float32) / np.float32(SEQ)
    bands = np.arange(1, 17, dtype=np.float32)
    ang = np.float32(2 * math.pi) * tt[:, None] * bands[None, :]
    z = np.concatenate([tt[:, None], np.cos(ang), np.sin(ang)], 1).astype(np.float32).T
    deltas = np.abs(np.linspace(math.log(1e-2) / 0.3, math.log(1e-2) / 1.5, HY, dtype=np.float32))
    decay = np.exp(-tt[:, None] * deltas[None, :]).astype(np.float32)
    sel = np.zeros((32, GRID_W, GRID_W), np.float32)
    q = np.arange(GRID_W)
    start = np.clip(q - WIN_C // 2, 0, GRID_W - WIN_C)
    for kc in range(GRID_W):
        for qc in range(GRID_W):
            if start[qc] <= kc < start[qc] + WIN_C:
                sel[kc - qc + WIN_C - 1, kc, qc] = 1.0
            else:
                sel[31, kc, qc] = 1.0
    sel = np.concatenate([sel, sel], 2).reshape(32, GRID_W * P)
    return {
        "four": four, "fourk": fourk, "zfeat": np.ascontiguousarray(z),
        "decay": np.ascontiguousarray(decay.reshape(KT, P, HY).transpose(1, 0, 2)),
        "sel": np.ascontiguousarray(sel), "ident": np.eye(P, dtype=np.float32),
        "ones": np.ones((P, P), np.float32),
    }


def units():
    out = []
    for r in range(0, ROWS, 2):
        k0 = min(max(r - WIN_R // 2, 0), ROWS - WIN_R)
        k1 = min(max(r + 1 - WIN_R // 2, 0), ROWS - WIN_R) + WIN_R
        if k1 - k0 > WIN_R:
            out.append((r, k0, k1 - k0, 14))
        else:
            out.append((r, k0, k1 - k0, k0 - r + 7 - 1))
    return out


UNITS = units()


def program(nc, A, out):
    ctx = ExitStack()
    with ctx:
        base = 16512

        def at(name, off, shape, dt=F32):
            return nc.alloc_sbuf_tensor_at(name, [P] + list(shape), dt, offset=base + off)

        def sem(name):
            return ctx.enter_context(nc.semaphore(name))

        P_HY, P_Q, P_KV, P_XG, H_, S_, SM = 24576, 49152, 65536, 116736, 124928, 157696, 206848
        arena = nc.alloc_sbuf_tensor("arena", [P, 212832 // 4], F32)
        raw = at("raw", 0, [2, D])
        w_hi = at("w_hi", 8192, [2, D], F32R)
        w_lo = at("w_lo", 16384, [2, D], F32R)
        p_hy = at("p_hy", P_HY, [6, SEQ])
        p_q = at("p_q", P_Q, [4, SEQ])
        p_kv = at("p_kv", P_KV, [10, ALL])
        p_xg = at("p_xg", P_XG, [2, SEQ])
        hb_hi = at("hb_hi", H_, [KT, HALF], F32R)
        hb_lo = at("hb_lo", H_ + 16384, [KT, HALF], F32R)
        e_hi = at("e_hi", P_HY, [KT, HALF], F32R)
        e_lo = at("e_lo", P_HY + 16384, [KT, HALF], F32R)
        o_hi = at("o_hi", P_HY + 32768, [KT, HALF], F32R)
        o_lo = at("o_lo", P_HY + 49152, [KT, HALF], F32R)
        kt_ = at("kt_", 90112, [2, 2, 2, HY])
        eo = at("eo", 98304, [2, 2, HY])
        kabs = at("kabs", 102400, [2, D])
        inv = at("inv", 110592, [2, HY])
        inv_t = at("inv_t", 112640, [2, HY])
        zf = at("zf", H_, [SEQ])
        farg = at("farg", H_ + 4096, [SEQ])
        fturn = at("fturn", H_ + 8192, [SEQ])
        h1 = at("h1", H_ + 12288, [SEQ])
        h2f = at("h2f", H_ + 16384, [SEQ])
        w3s = at("w3s", H_ + 20480, [D])
        w12 = at("w12", H_ + 24576, [2, 64])
        rowsA = at("rowsA", H_ + 25600, [P])
        rowsB = at("rowsB", H_ + 26112, [P])
        rowsC = at("rowsC", H_ + 26624, [P])
        kev = at("kev", S_, [2, 2, HY])
        mprod = at("mprod", S_ + 4096, [D])
        macc = at("macc", S_ + 8192, [2, 2, P])
        ada0 = at("ada0", S_ + 12288, [4, D])
        dec = at("dec", S_ + 40960, [KT, HY])
        xin = at("xin", S_ + 32768, [2, D])
        xmod = at("xmod", S_ + 40960, [2, D])
        hb2_hi = at("hb2_hi", S_, [KT, HALF], F32R)
        hb2_lo = at("hb2_lo", S_ + 16384, [KT, HALF], F32R)
        xstat = at("xstat", S_ + 28672, [2, D])
        xsqr = at("xsqr", S_ + 36864, [D])
        l_u, l_r, l_i, l_s, l_q, l_a = (at(f"l_{n}", S_ + 5120 * k, [ALL]) for k, n in enumerate("urisqa"))
        l_h = at("l_h", S_ + 30720, [2, ALL])
        l_w = at("l_w", S_ + 40960, [8, P])
        tm = at("tm", H_, [KT, 3, HY])
        conv = at("conv", H_ + 24576, [2, SEQ])
        kspec = at("kspec", S_, [KT, 2, HY])
        y_s = [at("y_re", P_HY, [KT, 2, HY], F32R), at("y_im", S_ + 16384, [KT, 2, HY], F32R)]
        u_s = at("u_s", S_ + 32768, [KT, 2, HY], F32R)
        hy0 = P_KV + 8 * 5120
        prodA = at("prodA", hy0, [2, HY])
        prodB = at("prodB", hy0 + 2048, [2, HY])
        ysum = at("ysum", hy0 + 4096, [2, HY])
        hyb = at("hyb", hy0 + 6144, [2, HY])
        zb = at("zb", hy0 + 8192, [HY])
        zs = at("zs", hy0 + 9216, [HY])
        mix_hy = at("mix_hy", P_HY, [2, SEQ])
        bias = at("bias", H_, [HEADS, 23, GRID_W])
        A0 = H_ + 47104
        selt = at("selt", A0, [GRID_W, P])
        pr = at("pr", A0, [2, 832])
        pT = at("pT", A0 + 6656, [2, 7, P])
        qh, ql = at("qh", A0 + 13824, [SEQ], F32R), at("ql", A0 + 17920, [SEQ], F32R)
        kh, kl = at("kh", A0 + 22016, [ALL], F32R), at("kl", A0 + 27136, [ALL], F32R)
        bst = [at("bst0", 0, [23, GRID_W]), at("bst1", 5888, [23, GRID_W])]
        vst = at("vst", 11776, [ALL])
        mprod1 = at("mprod1", 16896, [D])
        macc1 = at("macc1", 20992, [2, P])
        vtm = at("vtm", P_HY + 8192, [10, P])
        rpbt = at("rpbt", P_HY + 13312, [120])
        rpbr = at("rpbr", P_HY + 13824, [32])
        ada1 = at("ada1", P_HY + 14336, [2, D])
        x1 = at("x1", S_, [KT, SEQ])
        yo = [at("yo0", P_KV, [KT, HALF]), at("yo1", P_KV + 16384, [KT, HALF])]
        xr2 = at("xr2", P_HY + 8192, [4, D])
        yd = at("yd", S_ + 32768, [KT, HALF])
        a_hi = at("a_hi", P_HY, [FT, HALF], F32R)
        a_lo = at("a_lo", P_HY + 45056, [FT, HALF], F32R)
        F0 = P_HY + 90112
        g_t = at("g_t", F0, [HALF])
        g_s = at("g_s", F0 + 2048, [HALF])
        sq = at("sq", F0, [2, HALF])
        a_f = at("a_f", F0 + 4096, [HALF])
        rstd = at("rstd", F0 + 6144, [HALF])
        nrm = at("nrm", F0 + 8192, [HALF])
        so = [SM]

        def small(name, shape):
            n = 4 * int(np.prod(shape))
            n = -(-n // 32) * 32
            t = at(name, so[0], shape)
            so[0] += n
            assert so[0] <= 212832 - 0, so[0]
            return t

        ident = small("ident", [P])
        ones = small("ones", [P])
        colA = small("colA", [96])
        colB = small("colB", [48])
        colC = small("colC", [4])
        sil = small("sil", [2, KT])
        sil_t = small("sil_t", [16])
        mod = small("mod", [48, 2])
        amix = small("amix", [KT, 2])
        affn = small("affn", [KT])
        gmix = small("gmix", [KT])
        gffn = small("gffn", [KT])
        ssq = small("ssq", [10])
        rx = small("rx", [10])
        lam = small("lam", [8, 4])
        hbias = small("hbias", [8])
        amax = small("amax", [2, 4])
        asum = small("asum", [2, 4])

        ps = ctx.enter_context(nc.psum_tensor("ps", [P, 8, 512], F32))

        raw_ld = [sem("raw_ld0"), sem("raw_ld1")]
        hi_done, lo_done, job_done, acc_free = sem("hi_done"), sem("lo_done"), sem("job_done"), sem("acc_free")
        ada_ld = [sem("ada_ld0"), sem("ada_ld1")]
        mix_ld = [sem(f"mix_ld{q}") for q in range(4)]
        mod_done, mod_rd = sem("mod_done"), sem("mod_rd")
        macc_ok, kspec_ld, nrm_ok, kh_ok = [sem(n) for n in ("macc_ok", "kspec_ld", "nrm_ok", "kh_ok")]
        ks_out = [sem("ks_out0"), sem("ks_out1")]
        spec = nc.dram_tensor("spec", (2, KT, P, 2 * HY), F32, kind="Internal").ap()
        par_ld, flt_ld, dec_ld = sem("par_ld"), sem("flt_ld"), sem("dec_ld")
        x_ld = [sem("x_ld0"), sem("x_ld1")]
        xs_ld = [sem("xs_ld0"), sem("xs_ld1")]
        dchain = sem("dchain")
        achain = sem("achain")
        cols_ps, cols_ok = sem("cols_ps"), sem("cols_ok")
        silt_ok, sil_ok, silp_ok = sem("silt_ok"), sem("sil_ok"), sem("silp_ok")
        f_ps, f_arg, f_sin = sem("f_ps"), sem("f_arg"), sem("f_sin")
        k_ps, k_dec, k_abs, k_eo, k_hi, k_lo, k_sum = [sem("k_" + n) for n in ("ps", "dec", "abs", "eo", "hi", "lo", "sum")]
        amix_ok = sem("amix_ok")
        x_sq, x_rs, x_sqrt, x_n, x_tp, x_mod, x_hi, x_lo = [sem("x_" + n) for n in ("sq", "rs", "sqrt", "n", "tp", "mod", "hi", "lo")]
        lw_ld, l_conv, l_gp, l_gate, l_dve, l_act, l_done, lam_a, lam_d, l_zero = [
            sem(n) for n in ("lw_ld", "l_conv", "l_gp", "l_gate", "l_dve", "l_act", "l_done", "lam_a", "lam_d", "l_zero")]
        hyb_ld, c_ok, c_tp, c_ev, u_hi_ok, u_lo_ok, y_f, y_h, y_l, inv_free, z_ok, z_tp, z_ev = [
            sem(n) for n in ("hyb_ld", "c_ok", "c_tp", "c_ev", "u_hi_ok", "u_lo_ok", "y_f", "y_h", "y_l",
                             "inv_free", "z_ok", "z_tp", "z_ev")]
        sel_ld, rp_tp, rp_ok, b_ps, b_evd, b_eva, b_ok = [
            sem(n) for n in ("sel_ld", "rp_tp", "rp_ok", "b_ps", "b_evd", "b_eva", "b_ok")]
        st_free, st_ok, v_tp, v_ev, qk_done, mx_ok, exp_ok, t_done, pt_d, pt_a, pv_done, rec_ok, o_ok, ot_done, ot_free, modp, att_x = [
            sem(n) for n in ("st_free", "st_ok", "v_tp", "v_ev", "qk_done", "mx_ok", "exp_ok", "t_done", "pt_d",
                             "pt_a", "pv_done", "rec_ok", "o_ok", "ot_done", "ot_free", "modp", "att_x")]
        m_hi, m_lo, xr_ld, gates_ok, n_sq, n_ps, n_var, n_sqrt, n_fin, n_tp, n_x1, n_h, n_hh, n_hl, bst_ok, f_mm = [
            sem(n) for n in ("m_hi", "m_lo", "xr_ld", "gates_ok", "n_sq", "n_ps", "n_var", "n_sqrt", "n_fin",
                             "n_tp", "n_x1", "n_h", "n_hh", "n_hl", "bst_ok", "f_mm")]
        g_tanh, g_a, g_ah, g_al, dn_done, dn_free, y_ok = [
            sem(n) for n in ("g_tanh", "g_a", "g_ah", "g_al", "dn_done", "dn_free", "y_ok")]
        o_tp, o_ev, st_out = sem("o_tp"), sem("o_ev"), [sem("st_out0"), sem("st_out1")]

        block = ctx.enter_context(nc.Block())

        w_in = A["w_in"][0].rearrange("(k p) n -> p k n", p=P)
        w_out = A["w_out"][0].rearrange("(k p) n -> p k n", p=P)
        w_gu = A["ffn_w_gu"][0].rearrange("(k p) n -> p k n", p=P)
        w_dn = A["ffn_w_down"][0].rearrange("(k p) n -> p k n", p=P)
        ada = A["ada_w"][0].rearrange("(k p) n -> p k n", p=P)
        x_tok = A["x"][0]
        c_tok = A["ctx"][0]

        BLOCKS = [(c_tok, 0, 2, 1, J_CTX, 10), (x_tok, 0, 4, 0, J_LAT, 22), (x_tok, 4, 4, 0, J_LAT + 22, 22)]
        TILES = [(src, t0 + t) for src, t0, cnt, _, _, _ in BLOCKS for t in range(cnt)]
        HB = [(hb_hi, hb_lo), (hb2_hi, hb2_lo), (hb_hi, hb_lo)]
        HS = [slice(0, HALF), slice(HALF, SEQ)]

        def mix_src(k, h):
            src = (mix_hy[:, k] if k < 2 else p_q[:, k - 2] if k < 6 else p_xg[:, k - 6])
            return src[:, HS[h]]

        def bias_ps(g, half):
            v = ps[64 * half:64 * half + 64, g % 4, 0:480].rearrange("p (j h r) -> p h r j", j=4, h=HEADS)
            return v[:, :, 1:15, :] if half == 0 else v[:, :, 0:14, :]

        def s_all(s):
            return ps[:, 2 * (s % 2):2 * (s % 2) + 2, :].rearrange("p a b -> p (a b)")

        @block.sync
        def _(sp):
            sp.dma_start(ident[:], A["ident"]).then_inc(par_ld, 16)
            sp.dma_start(ones[:], A["ones"]).then_inc(par_ld, 16)
            r8 = lambda ap: ap.rearrange("(k p) -> k p", p=P)
            off = 0
            for src in [A[n][0] for n in ("g_mix_pre", "g_mix_post", "g_ffn_pre", "g_ffn_post", "ada_b", "c")] + [A["c_ctx"]]:
                src = r8(src)
                sp.dma_start(rowsA[off:off + src.shape[0], :], src).then_inc(par_ld, 16)
                off += src.shape[0]
            off = 0
            for name in ("hy_conv_w", "hy_conv_b", "lru_conv_w", "lru_conv_b", "lru_ba", "lru_bi", "lru_lam"):
                src = A[name][0] if len(A[name].shape) == 3 else A[name]
                for r in range(src.shape[0]):
                    v = r8(src[r])
                    sp.dma_start(rowsB[off:off + v.shape[0], :], v).then_inc(par_ld, 16)
                    off += v.shape[0]
            sp.dma_start(rowsC[0:1, 0:64], A["hy_f_b1"]).then_inc(par_ld, 16)
            sp.dma_start(rowsC[1:2, 0:64], A["hy_f_b2"]).then_inc(par_ld, 16)
            sp.dma_start(rowsC[2:4, 0:64], A["hy_f_freq"][0]).then_inc(par_ld, 16)
            sp.dma_start(zf[0:33, :], A["zfeat"]).then_inc(flt_ld, 16)
            sp.dma_start(w12[0:33, 0, :], A["hy_f_w1"][0]).then_inc(flt_ld, 16)
            sp.dma_start(w12[0:64, 1, :], A["hy_f_w2"][0]).then_inc(flt_ld, 16)
            sp.dma_start(w3s[0:64, :], A["hy_f_w3"][0]).then_inc(flt_ld, 16)
            sp.dma_start(dec[:], A["decay"]).then_inc(dec_ld, 16)

            def raw_dma(b, J, src, nk=KT, first=False):
                if not first:
                    sp.wait_ge(lo_done, J - 1)
                sp.dma_start(raw[:, b, 0:nk * P].rearrange("p (k n) -> p k n", n=P), src).then_inc(raw_ld[b], 16)

            def phase(J0, pairs, src, begin=1):
                with sp.Fori(begin, pairs) as i:
                    for b in range(2):
                        raw_dma(b, i * 2 + (J0 + b), src(i, b))

            def pair0(J0, src):
                for b in range(2):
                    raw_dma(b, J0 + b, src(0, b), first=J0 == 0)

            fk = A["fourk"].rearrange("m c p n -> (m c) p n")
            f4 = A["four"].rearrange("m c p n -> (m c) p n")
            one = lambda ap: ap.rearrange("o p (k n) -> p (o k) n", n=P)
            src_k = lambda i, b: one(fk[ds(i * 2 + b, 1)])
            src_4 = lambda i, b: one(f4[ds(i * 2 + b, 1)])
            src_c = lambda i, b: w_in[:, :, ds((i * 2 + (10 + b)) * P, P)]
            src_l = lambda i, b: w_in[:, :, ds((i * 2 + b) * P, P)]
            src_o = lambda i, b: w_out[:, :, ds((i * 2 + b) * P, P)]
            src_g = lambda i, b: w_gu[:, :, ds(i * P + b * FF, P)]

            def ada_dma(dst, q, n, src, landed):
                if n is not None:
                    sp.wait_ge(mod_rd, n)
                sp.dma_start(dst[:, q, :].rearrange("p (k n) -> p k n", n=P), src).then_inc(landed[q], 16)

            def lru_w_dma():
                sp.wait_ge(l_zero, 1)
                for g, name in enumerate(("lru_wa", "lru_wi")):
                    for d in range(2):
                        for c in range(2):
                            for e in range(2):
                                sp.dma_start(l_w[64 * e:64 * e + 64, g * 4 + d * 2 + c, 64 * e:64 * e + 64],
                                             A[name][0, d, 2 * c + e]).then_inc(lw_ld, 16)

            pair0(J_K, src_k)
            for q in range(4):
                ada_dma(ada0, q, None, ada[:, :, q * P:(q + 1) * P], mix_ld)
            ks_dst = spec.rearrange("o m p (c n) -> c p m o n", c=2)

            def spectrum_out(i, b, n):
                sp.wait_ge(acc_free, n)
                sp.dma_start(ks_dst[b, :, ds(i, 1)].rearrange("p m o n -> p (m o) n"), kev[:, b]).then_inc(ks_out[b], 16)

            raw_dma(0, J_K + 2, src_k(1, 0))
            with sp.Fori(0, 3) as i:
                for q in range(4):
                    b, pair = (q + 1) % 2, i * 2 + (q + 3) // 2
                    raw_dma(b, i * 4 + (J_K + q + 3), src_k(pair, b))
                    spectrum_out(i * 2 + q // 2, q % 2, i * 4 + (q + 3))
                    ada_dma(ada0, q, i * 4 + (q + 1), ada[:, :, ds((i * 4 + (q + 4)) * P, P)], mix_ld)
            raw_dma(1, J_K + 15, src_k(7, 1))
            for b in range(2):
                spectrum_out(6, b, 15 + b)
            pair0(J_CTX, src_c)
            for b in range(2):
                spectrum_out(7, b, 17 + b)
            phase(J_CTX, 5, src_c)
            for J0 in (J_LAT, J_LAT + 22):
                pair0(J0, lambda i, b: w_in[:, :, (18 + b) * P:(19 + b) * P])
                pair0(J0 + 2, lambda i, b: w_in[:, :, (20 + b) * P:(21 + b) * P])
                if J0 == J_LAT + 22:
                    lru_w_dma()
                phase(J0 + 4, 9, src_l, 0)
            pair0(J_HY, src_4)
            sp.wait_ge(l_done, 4)
            sp.dma_start(hyb[:].rearrange("p a b -> p (a b)"),
                         A["hy_bias"].rearrange("a o c -> a (o c)").broadcast_to([P, 2 * HY])).then_inc(hyb_ld, 16)
            def kspec_dma(o):
                sp.dma_start(kspec[:].rearrange("p m c n -> p m (c n)"), spec[o].rearrange("m p n -> p m n")).then_inc(kspec_ld, 16)

            for b in range(2):
                sp.wait_ge(ks_out[b], 144)
            kspec_dma(0)
            for p in range(4):
                phase(J_HY + 16 * p, 8, src_4)
                if p < 3:
                    pair0(J_HY + 16 * (p + 1), src_4)
                if p == 0:
                    sp.wait_ge(inv_free, 3)
                    kspec_dma(1)
            sp.wait_ge(z_tp, 2)
            sp.dma_start(selt[0:32, :, :], A["sel"].rearrange("j (k q) -> j k q", q=P)).then_inc(sel_ld, 16)
            sp.dma_start(rpbr[0:120, 0:31], A["na_rpb"][0].rearrange("h r c -> (h r) c")).then_inc(sel_ld, 16)
            for b in range(2):
                ada_dma(ada1, b, 15 + b, ada[:, :, (16 + b) * P:(17 + b) * P], ada_ld)
            with sp.Fori(1, 16) as i:
                for b in range(2):
                    ada_dma(ada1, b, i * 2 + (15 + b), ada[:, :, ds((i * 2 + (16 + b)) * P, P)], ada_ld)
            sp.wait_ge(pv_done, 64)
            sp.wait_ge(mod_done, 50)
            pair0(J_OUT, src_o)
            phase(J_OUT, 4, src_o)
            pair0(J_OUT + 8, src_o)
            phase(J_OUT + 8, 4, src_o)
            pair0(J_FFN, src_g)
            for h in range(2):
                if h == 1:
                    sp.wait_ge(n_tp, 8)
                for q in range(4):
                    sp.dma_start(xr2[:, q, :], x_tok[(4 * h + q) * P:(4 * h + q + 1) * P, :]).then_inc(xr_ld, 16)
            for h in range(2):
                J0 = J_FFN + h * (GU_JOBS + DOWN_JOBS)
                phase(J0, FT, src_g)
                J0 += GU_JOBS
                with sp.Fori(0, 4) as i:
                    for q in range(6):
                        c = q % 3
                        nk = KT if c < 2 else FT - 2 * KT
                        raw_dma(q % 2, i * 6 + (J0 + q),
                                w_dn[:, c * KT:c * KT + nk, ds((i * 2 + q // 3) * P, P)], nk)
                if h == 0:
                    pair0(J0 + DOWN_JOBS, src_g)
                for q in range(4):
                    sp.wait_ge(o_ev, 4 * h + q + 1)
                    sp.dma_start(out[0, (4 * h + q) * P:(4 * h + q + 1) * P, :], xin[:, q % 2, :]).then_inc(st_out[q % 2], 16)
            for b in range(2):
                sp.wait_ge(st_out[b], 64)

        @block.scalar
        def _(act):
            def split(J, half, b, first=False):
                act.wait_ge(raw_ld[b], half * 16 + 16)
                if not first:
                    act.wait_ge(job_done, J - 1)
                act.activation(w_hi[:, b, :], raw[:, b, :], ACT.Copy).then_inc(hi_done, 1)

            def split_next(i, J0, b):
                split(i * 2 + (J0 + b + 1), i + (J0 // 2 + b), 1 - b)

            def split_loop(n, J0):
                with act.Fori(0, n // 2) as i:
                    for b in range(2):
                        split_next(i, J0, b)

            def x_dma(n):
                src, t = TILES[n]
                act.dma_start(xin[:, n % 2, :], src[t * P:(t + 1) * P, :]).then_inc(x_ld[n % 2], 16)

            def stats_dma(n):
                src, t = TILES[n]
                act.dma_start(xstat[:, n % 2, :], src[t * P:(t + 1) * P, :]).then_inc(xs_ld[n % 2], 16)

            def mean_square(n):
                if n:
                    act.wait_ge(x_sq, n)
                act.wait_ge(xs_ld[n % 2], 16 * (n // 2 + 1))
                act.activation(xsqr[:], xstat[:, n % 2, :], ACT.Square, accum_out=ssq[:, n:n + 1]).then_inc(x_sq, 1)
                if n + 2 < len(TILES):
                    act.wait_ge(x_sq, n + 1)
                    stats_dma(n + 2)

            stats_dma(0)
            stats_dma(1)
            act.wait_ge(cols_ok, 1)
            act.activation(sil_t[:], colA[:, 80:96], ACT.Tanh, scale=0.5).then_inc(silt_ok, 1)
            for layer, dst in ((0, h1), (1, h2f)):
                act.wait_ge(f_arg, layer + 1)
                act.activation(dst[0:64, :], farg[0:64, :], ACT.Sin).then_inc(f_sin, 1)
            split(0, 0, 0, first=True)
            split(1, 0, 1, first=True)
            mean_square(0)
            mean_square(1)
            for t in range(KT):
                s = t % 2
                mean_square(t + 2)
                act.wait_ge(k_dec, t + 1)
                if t >= 2:
                    act.wait_ge(k_sum, t - 1)
                act.activation(kabs[:, s, :], kt_[:, s].rearrange("p a b c -> p (a b c)"), ACT.Abs).then_inc(k_abs, 1)
                act.wait_ge(k_eo, t + 1)
                act.activation(e_hi[:, t, :], eo[:, 0].rearrange("p a b -> p (a b)"), ACT.Copy)
                act.activation(o_hi[:, t, :], eo[:, 1].rearrange("p a b -> p (a b)"), ACT.Copy).then_inc(k_hi, 1)
            act.wait_ge(x_rs, 1)
            act.activation(rx[:], rx[:], ACT.Sqrt).then_inc(x_sqrt, 1)
            act.wait_ge(x_sq, 10)
            x_dma(0)
            x_dma(1)
            with act.Fori(1, 8) as i:
                for b in range(2):
                    split(i * 2 + (J_K + b), i + J_K // 2, b)

            def head_of(J):
                split(J, J // 2, J % 2)

            def tile_head(n, blk, t):
                act.wait_ge(x_mod, n + 1)
                if n + 2 < len(TILES):
                    x_dma(n + 2)
                act.activation(HB[blk][0][:, :, t * P:(t + 1) * P],
                               xmod[:, 1, :].rearrange("p (k n) -> p k n", n=P), ACT.Copy).then_inc(x_hi, 1)

            head_of(J_CTX)
            tile_head(0, 0, 0)
            tile_head(1, 0, 1)
            for b in range(2):
                act.wait_ge(ks_out[b], 144)
            for t in range(4):
                head_of(J_CTX + 2 * t + 1)
                head_of(J_CTX + 2 * t + 2)
                tile_head(2 + t, 1, t)
            head_of(J_CTX + 9)
            head_of(J_LAT)
            for t in range(4):
                for m in range(1, 5):
                    if m == 3:
                        if t == 0:
                            act.wait_ge(job_done, J_LAT)
                        tile_head(6 + t, 2, t)
                    head_of(J_LAT + 4 * t + m)
            with act.Fori(8, 11) as i:
                for b in range(2):
                    split_next(i, J_LAT, b)

            J0 = J_LAT + 22
            step = iter(range(22))

            def split_step(n=1):
                for _ in range(n):
                    j = next(step)
                    split_next(j // 2, J0, j % 2)

            act.wait_ge(lam_d, 1)
            act.activation(lam[:, 1, :], lam[:, 0, :], ACT.Exp, scale=-1.0).then_inc(lam_a, 1)
            split_step(4)
            act.wait_ge(lam_d, 2)
            for c in range(2):
                for d in range(2):
                    q = c * 2 + d
                    split_step(LRU_AFTER[q] * 2 - (LRU_AFTER[q - 1] * 2 + 2 if q else 0))
                    if q:
                        act.wait_ge(l_done, q)
                    for g, dst in ((0, l_r), (1, l_i)):
                        for part, (o0, w) in enumerate(((0, 256), (256, 512), (768, 512))):
                            act.wait_ge(l_gp, (q * 2 + g) * 3 + part + 1)
                            act.activation(dst[:, o0:o0 + w], ps[:, 2 + g * 3 + part, 0:w], ACT.Tanh, scale=0.5,
                                           bias=hbias[:, g * 4 + d * 2 + c:g * 4 + d * 2 + c + 1]).then_inc(l_gate, 1)
                    split_step()
                    act.wait_ge(l_gate, q * 6 + 6)
                    act.activation(l_a[:], l_r[:], ACT.Exp, scale=lam[:, 7, d * 2 + c:d * 2 + c + 1],
                                   bias=lam[:, 7, d * 2 + c:d * 2 + c + 1])
                    act.activation(l_s[:], l_r[:], ACT.Tanh, scale=lam[:, 2, d * 2 + c:d * 2 + c + 1],
                                   bias=lam[:, 2, d * 2 + c:d * 2 + c + 1]).then_inc(l_act, 1)
                    act.wait_ge(l_act, 5 * c + 2 * d + 1)
                    act.activation(l_r[:], l_s[:], ACT.Sqrt, scale=0.25).then_inc(l_act, 1)
                    split_step()
                act.wait_ge(l_dve, c + 1)
                act.activation(l_s[:, 0:SEQ], l_q[:, 0:SEQ], ACT.Tanh, scale=0.7978845608028654).then_inc(l_act, 1)
            split_step(2)
            assert next(step, None) is None

            for c in range(6):
                act.wait_ge(c_tp, c + 1)
                act.activation(tm[:, :, c // 2, (c % 2) * P:(c % 2) * P + P],
                               ps[:, 4 + 2 * (c % 2):6 + 2 * (c % 2), :].rearrange("p a (t n) -> p (a t) n", n=P),
                               ACT.Copy).then_inc(c_ev, 1)
            act.wait_ge(c_ev, 2)
            act.activation(u_s[:, :, 0, :], tm[:, :, 0, :], ACT.Copy).then_inc(u_hi_ok, 1)
            for o in range(2):
                J0 = J_HY + 32 * o
                def y_heads(i):
                    act.wait_ge(y_f, i + (8 * o + 1))
                    act.wait_ge(cols_ok, 1)
                    for part in range(2):
                        ins = act.activation(y_s[part][:, ds(i, 1), 0, :].rearrange("p a c -> p (a c)"), ysum[:, part], ACT.Copy)
                    ins.then_inc(y_h, 1)

                def z_head(i):
                    act.wait_ge(z_ok, i + 1)
                    act.wait_ge(cols_ok, 1)
                    act.activation(u_s[:, ds(i, 1), 0, :].rearrange("p a c -> p (a c)"),
                                   tm[:, ds(i, 1), 0, :].rearrange("p a c -> p (a c)"), ACT.Copy).then_inc(u_hi_ok, 1)

                for J, between in ((J0, y_heads), (J0 + 16, z_head if o == 0 else None)):
                    split_next(0, J, 0)
                    split_next(0, J, 1)
                    with act.Fori(1, 7 if between is None else 8) as i:
                        split_next(i, J, 0)
                        if between:
                            between(i - 1)
                        split_next(i, J, 1)
                    if between:
                        between(7)
            split_next(7, J_HY + 48, 0)

            for g in range(1, 16, 2):
                act.wait_ge(b_ps, g + 1)
                act.activation(bias[0:64, :, 0:14, 4 * g:4 * g + 4], bias_ps(g, 0), ACT.Copy)
                act.activation(bias[64:128, :, 0:14, 4 * g:4 * g + 4], bias_ps(g, 1), ACT.Copy).then_inc(b_eva, 1)
            act.wait_ge(b_evd, 8)
            act.wait_ge(b_eva, 8)
            act.activation(bias[64:128, :, 15:23, :], bias[64:128, :, 3:11, :], ACT.Copy).then_inc(b_eva, 1)
            with act.Fori(0, 4) as hp:
                act.wait_ge(st_free, hp + 1)
                act.wait_ge(cols_ok, 1)
                act.activation(kh[:], p_kv[:, ds(hp, 1), :].rearrange("p a n -> p (a n)"), ACT.Copy)
                act.activation(qh[:], p_q[:, ds(hp, 1), :].rearrange("p a n -> p (a n)"), ACT.Copy).then_inc(kh_ok, 1)
                act.activation(vst[:], p_kv[:, ds(hp + 4, 1), :].rearrange("p a n -> p (a n)"), ACT.Copy).then_inc(st_ok, 1)
                act.wait_ge(v_tp, hp + 1)
                act.activation(vtm[:, 4:8, :], ps[:, 5, :].rearrange("p (a b) -> p a b", b=P), ACT.Copy)
                act.activation(vtm[:, 8:10, :], ps[:, 6, 0:256].rearrange("p (a b) -> p a b", b=P), ACT.Copy).then_inc(v_ev, 1)
                for s in range(17):
                    if s < 16:
                        L = UNITS[s // 2][2] * GRID_W
                        act.wait_ge(mx_ok, hp * 16 + (s + 1))
                        act.activation(pr[:, s % 2, 0:L], pr[:, s % 2, 0:L], ACT.Exp,
                                       bias=amax[:, s % 2, 2:3], accum_out=asum[:, s % 2, 0:1])
                        act.activation(pr[:, s % 2, L:L + CTX], s_all(s)[:, L:L + CTX], ACT.Exp,
                                       bias=amax[:, s % 2, 2:3], accum_out=asum[:, s % 2, 1:2]).then_inc(exp_ok, 1)
                    if s >= 1:
                        u = s - 1
                        if u >= 2:
                            act.wait_ge(pv_done, hp * 16 + (u - 1))
                        act.wait_ge(t_done, hp * 16 + (u + 1))
                        act.activation(pT[:, u % 2, 0:4, :], ps[:, 4 + u % 2, :].rearrange("p (a b) -> p a b", b=P), ACT.Copy)
                        ins = act.activation(pT[:, u % 2, 4:6, :], ps[:, 6, 0:256].rearrange("p (a b) -> p a b", b=P), ACT.Copy)
                        if UNITS[u // 2][2] > WIN_R:
                            ins = act.activation(pT[0:64, u % 2, 6, :], ps[0:64, 6, 256:384], ACT.Copy)
                        ins.then_inc(pt_a, 1)

            act.wait_ge(ot_free, 34)
            for h in range(2):
                if h == 0:
                    split(J_OUT, J_OUT // 2, 0)
                if h == 1:
                    act.wait_ge(job_done, J_OUT + 8)
                for k in range(KT):
                    act.activation(hb_hi[:, k, :], mix_src(k, h), ACT.Copy).then_inc(m_hi, 1)
                split_loop(8, J_OUT + 8 * h)

            def squares(N, src, ready):
                for k in range(KT):
                    q = KT * N + k
                    if q >= 2:
                        act.wait_ge(n_ps, q - 1)
                    act.wait_ge(*ready(k))
                    act.activation(sq[:, k % 2, :], src(k), ACT.Square).then_inc(n_sq, 1)
                act.wait_ge(n_var, N + 1)
                act.activation(nrm[:], nrm[:], ACT.Sqrt).then_inc(n_sqrt, 1)

            def h2_heads(h):
                for k in range(KT):
                    act.wait_ge(n_h, KT * h + k + 1)
                    if k == 0:
                        act.wait_ge(job_done, J_FFN + h * GU_JOBS)
                    act.activation(hb_hi[:, k, :], sq[:, k % 2, :], ACT.Copy).then_inc(n_hh, 1)

            norm_b = lambda N, h: squares(N, lambda k: x1[:, k, HS[h]], lambda k: (n_x1, KT * h + k + 1))
            squares(0, lambda k: yo[0][:, k, :], lambda k: (acc_free, E_OUT + 8 + 2))
            norm_b(1, 0)
            h2_heads(0)
            act.wait_ge(n_hl, KT)
            squares(2, lambda k: yo[1][:, k, :], lambda k: (acc_free, E_OUT + 16 + 2))

            for h in range(2):
                J0 = J_FFN + h * (GU_JOBS + DOWN_JOBS)
                with act.Fori(0, FT) as i:
                    split_next(i, J0, 0)
                    act.wait_ge(job_done, i * 2 + (J0 + 1))
                    act.activation(g_t[:], ps[:, 0, :], ACT.Tanh, scale=0.5).then_inc(g_tanh, 1)
                    split_next(i, J0, 1)
                    act.wait_ge(g_a, i + (FT * h + 1))
                    act.wait_ge(cols_ok, 1)
                    act.activation(a_hi[:, ds(i, 1), :].rearrange("p a c -> p (a c)"), a_f[:], ACT.Copy).then_inc(g_ah, 1)
                J0 += GU_JOBS
                with act.Fori(0, 4 - h) as i:
                    for q in range(6):
                        split(i * 6 + (J0 + q + 1), i * 3 + (J0 // 2 + (q + 1) // 2), (q + 1) % 2)
                if h == 1:
                    for q in range(5):
                        split(18 + J0 + q + 1, 9 + J0 // 2 + (q + 1) // 2, (q + 1) % 2)
                squares(3 + 2 * h, lambda k: yd[:, k, :], lambda k: (dn_free, 8 * h + 8 + 2))
                if h == 0:
                    norm_b(4, 1)
                    h2_heads(1)

        @block.gpsimd
        def _(pool):
            def rest(i, J0, b):
                pool.wait_ge(hi_done, i * 2 + (J0 + b + 1))
                pool.tensor_tensor(w_lo[:, b, :], raw[:, b, :], w_hi[:, b, :].bitcast(F32), ALU.subtract).then_inc(lo_done, 1)

            def rests(n, J0):
                with pool.Fori(0, n // 2) as i:
                    for b in range(2):
                        rest(i, J0, b)

            for t in range(KT):
                pool.wait_ge(k_hi, t + 1)
                pool.tensor_tensor(e_lo[:, t, :], eo[:, 0].rearrange("p a b -> p (a b)"), e_hi[:, t, :].bitcast(F32), ALU.subtract)
                pool.tensor_tensor(o_lo[:, t, :], eo[:, 1].rearrange("p a b -> p (a b)"), o_hi[:, t, :].bitcast(F32),
                                   ALU.subtract).then_inc(k_lo, 1)
            rests(16, J_K)

            def rest_of(J):
                rest(0, J - J % 2, J % 2)

            def tile_rest(n, blk, t):
                pool.wait_ge(x_hi, n + 1)
                hi, lo = HB[blk]
                pool.tensor_tensor(lo[:, :, t * P:(t + 1) * P], xmod[:, 1, :].rearrange("p (k n) -> p k n", n=P),
                                   hi[:, :, t * P:(t + 1) * P].bitcast(F32), ALU.subtract).then_inc(x_lo, 1)

            rest_of(J_CTX)
            tile_rest(0, 0, 0)
            tile_rest(1, 0, 1)
            for t in range(4):
                rest_of(J_CTX + 2 * t + 1)
                rest_of(J_CTX + 2 * t + 2)
                tile_rest(2 + t, 1, t)
            rest_of(J_CTX + 9)
            rest_of(J_LAT)
            for t in range(4):
                for m in range(1, 5):
                    if m == 3:
                        tile_rest(6 + t, 2, t)
                    rest_of(J_LAT + 4 * t + m)
            pool.memset(l_w[:], 0.0).then_inc(l_zero, 1)
            rest_of(J_LAT + 17)
            with pool.Fori(9, 22) as i:
                for b in range(2):
                    rest(i, J_LAT, b)
            for p in range(4):
                rests(16, J_HY + 16 * p)
            pool.wait_ge(y_h, 16)
            pool.wait_ge(z_tp, 2)
            pool.memset(bias[0:64, :, 22:23, :], NEG)
            pool.memset(bias[64:128, :, 14:15, :], NEG).then_inc(b_ok, 1)
            for h in range(2):
                for k in range(KT):
                    pool.wait_ge(m_hi, KT * h + k + 1)
                    pool.tensor_tensor(hb_lo[:, k, :], mix_src(k, h), hb_hi[:, k, :].bitcast(F32), ALU.subtract).then_inc(m_lo, 1)
                rests(8, J_OUT + 8 * h)

            def h2_rests(h):
                for k in range(KT):
                    pool.wait_ge(n_hh, KT * h + k + 1)
                    pool.tensor_tensor(hb_lo[:, k, :], sq[:, k % 2, :], hb_hi[:, k, :].bitcast(F32), ALU.subtract).then_inc(n_hl, 1)

            for h in range(2):
                h2_rests(h)
                rests(GU_JOBS + DOWN_JOBS, J_FFN + h * (GU_JOBS + DOWN_JOBS))

        @block.vector
        def _(dve):
            class Chain:

                def __init__(self):
                    self.n, self.i, self.per = 0, None, 0

                def __call__(self, ins):
                    ins.then_inc(dchain, 1)
                    self.n += 1
                    dve.wait_ge(dchain, self.n if self.i is None else self.i * self.per + self.n)

                def loop(self, i, per):
                    self.i, self.per, self.start = i, per, self.n

                def end(self, times):
                    assert self.n - self.start == self.per, (self.n - self.start, self.per)
                    self.n, self.i = self.start + self.per * times, None

            link = Chain()

            def evac(i, J, dst, scale=1.0):
                dve.wait_ge(job_done, J + 1)
                dve.tensor_scalar(dst, i, scale, None, ALU.mult).then_inc(acc_free, 1)

            for _ in range(2):
                dve.nop().then_inc(acc_free, 1)
                dve.nop().then_inc(inv_free, 1)
                dve.nop().then_inc(dn_free, 1)
                dve.nop().then_inc(mod_done, 1)
                dve.nop().then_inc(ks_out[_], 16)
                dve.nop().then_inc(ot_free, 1)
            dve.nop().then_inc(modp, 1)
            dve.nop().then_inc(st_free, 1)

            dve.wait_ge(cols_ps, 1)
            dve.tensor_copy(colA[:], ps[:, 2, 0:96])
            dve.tensor_copy(colB[:, 0:46], ps[:, 2, 96:142])
            dve.tensor_copy(colC[0:64, :], ps[0:64, 2, 142:146]).then_inc(cols_ok, 1)
            dve.wait_ge(cols_ok, 1)
            dve.wait_ge(silt_ok, 1)
            link(dve.scalar_tensor_tensor(sil_t[:], sil_t[:], 1.0, colA[:, 80:96], ALU.add, ALU.mult))
            dve.tensor_scalar(sil[:].rearrange("p a b -> p (a b)"), sil_t[:], 0.5, None, ALU.mult).then_inc(sil_ok, 1)

            for layer in range(2):
                dve.wait_ge(f_ps, layer + 1)
                z = ps[0:64, 4 + 2 * layer:6 + 2 * layer, :].rearrange("p a b -> p (a b)")
                if layer == 1:
                    dve.wait_ge(f_sin, 1)
                link(dve.tensor_scalar(farg[0:64, :], z, colC[0:64, layer:layer + 1], colC[0:64, 2 + layer:3 + layer],
                                       ALU.add, ALU.mult))
                link(dve.tensor_scalar(fturn[0:64, :], farg[0:64, :], 1.0 / (2 * math.pi), MAGIC, ALU.mult, ALU.add))
                link(dve.tensor_scalar(fturn[0:64, :], fturn[0:64, :], MAGIC, None, ALU.subtract))
                for part in (TWO_PI_HEAD, TWO_PI_REST):
                    link(dve.scalar_tensor_tensor(farg[0:64, :], fturn[0:64, :], -part, farg[0:64, :], ALU.mult, ALU.add))
                dve.tensor_scalar(farg[0:64, :], farg[0:64, :], 3.1415925, -3.1415925, ALU.min, ALU.max).then_inc(f_arg, 1)

            dve.wait_ge(dec_ld, 16)
            for t in range(KT):
                s = t % 2
                dve.wait_ge(k_ps, t + 1)
                if t >= 2:
                    dve.wait_ge(k_abs, t - 1)
                for o in range(2):
                    link(dve.tensor_tensor(kt_[:, s, o], ps[:, 4 + 2 * s + o, :].rearrange("p (a b) -> p a b", a=2),
                                           dec[:, t:t + 1, :].broadcast_to([P, 2, HY]), ALU.mult))
                if t == 0:
                    link(dve.memset(kt_[0:1, s, :, 1, :], 0.0))
                dve.nop().then_inc(k_dec, 1)
                if t >= 1:
                    dve.wait_ge(k_hi, t)
                    dve.wait_ge(k_lo, t)
                dve.tensor_tensor(eo[:, 0], kt_[:, s, :, 0, :], kt_[:, s, :, 1, :], ALU.add)
                dve.tensor_tensor(eo[:, 1], kt_[:, s, :, 0, :], kt_[:, s, :, 1, :], ALU.subtract).then_inc(k_eo, 1)
            dve.wait_ge(k_sum, KT)
            dve.tensor_copy(inv_t[:, 0], ps[:, 2, 0:HY])
            link(dve.tensor_copy(inv_t[:, 1], ps[:, 3, 0:HY]))
            for o in range(2):
                link(dve.tensor_tensor(inv_t[:, o], inv_t[:, o], ps[:, 2 + o, HY:2 * HY], ALU.add))
            link(dve.tensor_scalar(inv_t[:], inv_t[:], float(SEQ), None, ALU.mult))
            link(dve.reciprocal(inv[:], inv_t[:]))
            def mod_products(tile, prod, cond):
                return dve.tensor_tensor(prod[:].rearrange("p (k n) -> p k n", n=P), tile.rearrange("p (k n) -> p k n", n=P),
                                         sil[:, cond, :].unsqueeze(2).broadcast_to([P, KT, P]), ALU.mult)

            def mod_reduce(prod, acc):
                return dve.tensor_reduce(acc, prod[:].rearrange("p (k n) -> p n k", n=P), axis=AX, op=ALU.add)

            dve.wait_ge(x_sq, 10)
            dve.tensor_scalar(rx[:], ssq[:], 1.0 / D, EPS, ALU.mult, ALU.add).then_inc(x_rs, 1)
            with dve.Fori(0, 4) as i:
                link.loop(i, 16)
                for q in range(4):
                    b = q % 2
                    dve.wait_ge(ks_out[b], i * 32 + 16 * (q // 2 + 1))
                    dve.wait_ge(job_done, i * 4 + (J_K + q + 1))
                    dve.tensor_tensor(kev[:, b], ps[:, b, :].rearrange("p (a c) -> p a c", a=2), inv[:], ALU.mult).then_inc(acc_free, 1)
                    dve.wait_ge(mix_ld[q], i * 16 + 16)
                    dve.wait_ge(mod_done, i * 4 + (q + 1))
                    for cond in range(2):
                        link(mod_products(ada0[:, q, :], mprod, cond))
                        link(mod_reduce(mprod, macc[:, b, cond, :]))
                    dve.nop().then_inc(mod_rd, 1)
            link.end(4)
            dve.wait_ge(mod_done, 18)
            link(dve.tensor_tensor(mod[:, 0:16, :], ps[:, 7, 0:32].rearrange("p (a b) -> p a b", b=2),
                                   colA[:, 32:48].unsqueeze(2).broadcast_to([P, 16, 2]), ALU.add))
            link(dve.tensor_scalar(amix[:], mod[:, 8:16, :], 1.0, None, ALU.add))
            link(dve.tensor_tensor(amix[:], amix[:], colA[:, 0:8].unsqueeze(2).broadcast_to([P, KT, 2]), ALU.mult))

            def SPANS(h):
                hs = HS[h]
                lat = slice(CTX + hs.start, CTX + hs.stop)
                flat = lambda ap: ap.rearrange("p a n -> p (a n)")
                return ((18, 20, lambda t: flat(p_kv[:, ds(t + 8, 1), lat]), 1.0),
                        (20, 22, lambda t: flat(p_xg[:, ds(t, 1), hs]), 1.0),
                        (0, 6, lambda t: flat(p_hy[:, ds(t, 1), hs]), 1.0),
                        (6, 10, lambda t: flat(p_q[:, ds(t, 1), hs]), DH ** -0.5),
                        (10, 18, lambda t: flat(p_kv[:, ds(t, 1), lat]), 1.0))

            dve.wait_ge(x_sqrt, 1)
            link(dve.reciprocal(rx[:], rx[:]))

            def normalise(n):
                dve.wait_ge(x_ld[n % 2], 16 * (n // 2 + 1))
                dve.tensor_scalar(xin[:, n % 2, :], xin[:, n % 2, :], rx[:, n:n + 1], None, ALU.mult).then_inc(x_n, 1)

            def modulate(n):
                cond = 1 if n < 2 else 0
                if n >= 1:
                    dve.wait_ge(x_mod, n)
                dve.wait_ge(x_tp, n + 1)
                bank = 2 + 2 * (n % 2)
                src = ps[:, bank:bank + 2, :].rearrange("p a (k n) -> p (a k) n", n=P)
                x3 = lambda s: xmod[:, s, :].rearrange("p (k n) -> p k n", n=P)
                col = lambda v: v.broadcast_to([P, KT, P])
                link(dve.tensor_tensor(x3(0), src, col(amix[:, :, cond:cond + 1]), ALU.mult))
                if n >= 1:
                    dve.wait_ge(x_lo, n)
                dve.tensor_tensor(x3(1), x3(0), col(mod[:, 0:8, cond:cond + 1]), ALU.add).then_inc(x_mod, 1)

            def evac_span(J0, a, z):
                for f0, f1, dst, scale in SPANS(0):
                    j0 = (f0 + 4) % 22
                    lo, hi = max(a, j0), min(z, j0 + f1 - f0)
                    for j in range(lo, hi):
                        evac(ps[:, j % 2, :], J0 + j, dst(j - j0), scale)

            normalise(0)
            normalise(1)
            modulate(0)
            modulate(1)
            normalise(2)
            for t in range(5):
                for b in range(2):
                    evac(ps[:, b, 0:CTX], J_CTX + 2 * t + b, p_kv[:, 2 * t + b, 0:CTX])
                if t < 4:
                    modulate(2 + t)
                    normalise(3 + t)
            for t in range(4):
                evac_span(J_LAT, 4 * t, 4 * t + 2)
                modulate(6 + t)
                if t < 3:
                    normalise(7 + t)
                evac_span(J_LAT, 4 * t + 2, 4 * t + 4)
            evac_span(J_LAT, 16, 22)

            J0 = J_LAT + 22
            jobs1 = iter([(j, dst, scale) for a, z, dst, scale in SPANS(1) for j in [None]
                          for j, dst, scale in [((a + 4) % 22 + t, (lambda t=t, dst=dst: dst(t)), scale) for t in range(z - a)]])
            count1 = [0]

            def evac_to(n):
                while count1[0] < n:
                    j, dst, scale = next(jobs1)
                    evac(ps[:, j % 2, :], J0 + j, dst(), scale)
                    count1[0] += 1

            x_, e_, two_sp, mlam, z_, z2, poly = (lam[:, r, :] for r in (0, 1, 2, 3, 4, 5, 6))
            link(dve.tensor_scalar(mlam, colB[:, 42:46], -1.0, None, ALU.mult))
            link(dve.scalar_tensor_tensor(x_, mlam, -1.0, mlam, ALU.mult, ALU.max))
            dve.nop().then_inc(lam_d, 1)
            evac_to(4)
            dve.wait_ge(lam_a, 1)
            link(dve.tensor_scalar(z_, e_, 2.0, None, ALU.add))
            link(dve.reciprocal(z_, z_))
            link(dve.tensor_tensor(z_, z_, e_, ALU.mult))
            link(dve.tensor_tensor(z2, z_, z_, ALU.mult))
            link(dve.tensor_scalar(poly, z2, 1.0 / 19, 1.0 / 17, ALU.mult, ALU.add))
            for k in (15, 13, 11, 9, 7, 5, 3, 1):
                link(dve.tensor_tensor(poly, poly, z2, ALU.mult))
                link(dve.tensor_scalar(poly, poly, 1.0 / k, None, ALU.add))
            link(dve.tensor_tensor(poly, poly, z_, ALU.mult))
            link(dve.tensor_scalar(two_sp, mlam, 0.0, 2.0, ALU.max, ALU.mult))
            link(dve.scalar_tensor_tensor(two_sp, poly, 4.0, two_sp, ALU.mult, ALU.add))
            link(dve.tensor_scalar(lam[:, 7, :], two_sp, -2.0, None, ALU.mult))
            dve.tensor_scalar(hbias[:], colB[:, 34:42], 0.5, None, ALU.mult).then_inc(lam_d, 1)
            dve.wait_ge(x_lo, 10)
            for b in range(2):
                dve.wait_ge(ks_out[b], 144)
            for c in range(2):
                xr = p_kv[:, 8 + c, :]
                w = lambda k: colB[:, 24 + 2 * k + c:25 + 2 * k + c]
                link(dve.tensor_scalar(l_u[:], xr, w(2), colB[:, 32 + c:33 + c], ALU.mult, ALU.add))
                for k, sh in ((0, -2), (1, -1), (3, 1)):
                    for a, z in ((0, CTX), (CTX, ALL)):
                        lo, hi = (a - sh, z) if sh < 0 else (a, z - sh)
                        ins = dve.scalar_tensor_tensor(l_u[:, lo:hi], xr[:, lo + sh:hi + sh], w(k), l_u[:, lo:hi],
                                                       ALU.mult, ALU.add)
                        link(ins)
                    if c == 0:
                        evac_to(min(count1[0] + 1, 4 + 2 * LRU_AFTER[0]))
                dve.nop().then_inc(l_conv, 1)
                for d in range(2):
                    q = c * 2 + d
                    evac_to(4 + 2 * LRU_AFTER[q])
                    later = iter(range(4 + 2 * LRU_AFTER[q] + 1, 4 + 2 * (LRU_AFTER[q + 1] if q < 3 else 9) + 1))
                    more = lambda: evac_to(next(later, 0))
                    dve.wait_ge(l_act, 5 * c + 2 * d + 2)
                    link(dve.scalar_tensor_tensor(l_i[:], l_i[:], 1.0, l_u[:], ALU.add, ALU.mult))
                    more()
                    link(dve.scalar_tensor_tensor(l_i[:], l_a[:], 1.0, l_i[:], ALU.add, ALU.mult))
                    link(dve.tensor_tensor(l_i[:], l_i[:], l_r[:], ALU.mult))
                    more()
                    if d == 0:
                        link(dve.tensor_tensor_scan(l_h[:, 0, :], l_a[:], l_i[:], 0.0, ALU.mult, ALU.add))
                    else:
                        link(dve.tensor_tensor_scan(l_h[:, 1, 0:CTX][:, ::-1], l_a[:, 0:CTX][:, ::-1],
                                                    l_i[:, 0:CTX][:, ::-1], 0.0, ALU.mult, ALU.add))
                        link(dve.tensor_tensor_scan(l_h[:, 1, CTX:ALL][:, ::-1], l_a[:, CTX:ALL][:, ::-1],
                                                    l_i[:, CTX:ALL][:, ::-1], l_h[:, 1, 0:1], ALU.mult, ALU.add))
                        more()
                        xg, hsum, inner = p_xg[:, c, :], l_a[:, 0:SEQ], l_q[:, 0:SEQ]
                        link(dve.tensor_tensor(hsum, l_h[:, 0, CTX:ALL], l_h[:, 1, CTX:ALL], ALU.add))
                        link(dve.tensor_tensor(inner, xg, xg, ALU.mult))
                        link(dve.tensor_scalar(inner, inner, 0.044715, 1.0, ALU.mult, ALU.add))
                        dve.tensor_tensor(inner, inner, xg, ALU.mult).then_inc(l_dve, 1)
                        dve.wait_ge(l_act, 5 * c + 5)
                        link(dve.scalar_tensor_tensor(l_s[:, 0:SEQ], l_s[:, 0:SEQ], 1.0, xg, ALU.add, ALU.mult))
                        link(dve.scalar_tensor_tensor(xg, l_s[:, 0:SEQ], 0.5, hsum, ALU.mult, ALU.mult))
                    dve.nop().then_inc(l_done, 1)
            evac_to(22)

            for c in range(6):
                x, y = p_hy[:, c, :], conv[:, c % 2, :]
                w = lambda k: colB[:, 6 * k + c:6 * k + c + 1]
                if c >= 2:
                    dve.wait_ge(c_tp, c - 1)
                link(dve.tensor_scalar(y, x, w(1), colB[:, 18 + c:19 + c], ALU.mult, ALU.add))
                link(dve.scalar_tensor_tensor(y[:, 1:SEQ], x[:, 0:SEQ - 1], w(0), y[:, 1:SEQ], ALU.mult, ALU.add))
                dve.scalar_tensor_tensor(y[:, 0:SEQ - 1], x[:, 1:SEQ], w(2), y[:, 0:SEQ - 1],
                                         ALU.mult, ALU.add).then_inc(c_ok, 1)
            dve.wait_ge(u_hi_ok, 1)
            dve.tensor_tensor(u_s[:, :, 1, :], tm[:, :, 0, :], u_s[:, :, 0, :].bitcast(F32), ALU.subtract).then_inc(u_lo_ok, 1)
            dve.wait_ge(c_ev, 6)
            dve.wait_ge(hyb_ld, 16)
            for o in range(2):
                J0, E0 = J_HY + 32 * o, E_FWD + 16 * o
                dve.wait_ge(kspec_ld, 16 * (o + 1))
                with dve.Fori(0, 8) as i:
                    link.loop(i, 6)
                    k1 = kspec[:, ds(i, 1), :, :].rearrange("p m a c -> p (m a) c")

                    def transform(b, t):
                        dve.wait_ge(job_done, i * 2 + (J0 + b + 1))
                        link(dve.tensor_copy(t, ps[:, b, HY:2 * HY]))
                        link(dve.tensor_tensor(t, ps[:, b, 0:HY], t, ALU.add))
                        dve.nop().then_inc(acc_free, 1)
                        return t.unsqueeze(1).broadcast_to([P, 2, HY])

                    dve.tensor_tensor(prodA[:], transform(0, zb[:]), k1, ALU.mult)
                    link(dve.tensor_tensor(prodB[:, ::-1, :], transform(1, zs[:]), k1, ALU.mult))
                    dve.tensor_tensor(ysum[:, 0], prodA[:, 0], prodB[:, 0], ALU.subtract)
                    dve.tensor_tensor(ysum[:, 1], prodA[:, 1], prodB[:, 1], ALU.add).then_inc(y_f, 1)
                    dve.wait_ge(y_h, i + (8 * o + 1))
                    for part in range(2):
                        ins = dve.tensor_tensor(y_s[part][:, ds(i, 1), 1, :].rearrange("p a c -> p (a c)"), ysum[:, part],
                                                y_s[part][:, ds(i, 1), 0, :].bitcast(F32).rearrange("p a c -> p (a c)"), ALU.subtract)
                    link(ins)
                    dve.nop().then_inc(y_l, 1)
                link.end(8)
                with dve.Fori(0, 4) as i:
                    link.loop(i, 8 if o == 0 else 6)
                    for tp in range(2):
                        T = i * 2 + tp
                        row = lambda part: tm[:, ds(T, 1), part, :].rearrange("p a c -> p (a c)")
                        link(dve.tensor_tensor(zb[:], row(0), hyb[:, o], ALU.mult))
                        dve.wait_ge(job_done, i * 4 + (J0 + 16 + 2 * tp + 2))
                        link(dve.tensor_tensor(zb[:], ps[:, 2 + tp, HY:2 * HY], zb[:], ALU.add))
                        link(dve.tensor_tensor(zs[:], ps[:, 2 + tp, 0:HY], zb[:], ALU.add))
                        dve.nop().then_inc(inv_free, 1)
                        dve.tensor_tensor(row(0), zs[:], row(1 + o), ALU.mult).then_inc(z_ok, 1)
                        dve.wait_ge(z_ok, T + (8 * o + 1))
                        if o == 0:
                            dve.wait_ge(u_hi_ok, T + 2)
                            link(dve.tensor_tensor(u_s[:, ds(T, 1), 1, :].rearrange("p a c -> p (a c)"), row(0),
                                                   u_s[:, ds(T, 1), 0, :].bitcast(F32).rearrange("p a c -> p (a c)"),
                                                   ALU.subtract))
                            dve.nop().then_inc(u_lo_ok, 1)
                link.end(4)
            for c in range(2):
                dve.wait_ge(z_tp, c + 1)
                dve.tensor_copy(mix_hy[:, c, :], ps[:, 4 + 2 * c:6 + 2 * c, :].rearrange("p a b -> p (a b)")).then_inc(z_ev, 1)

            link(dve.memset(rpbt[0:32, :], NEG))
            dve.wait_ge(rp_tp, 1)
            dve.tensor_copy(rpbt[0:31, :], ps[0:31, 2, 0:120]).then_inc(rp_ok, 1)
            for g in range(0, 16, 2):
                dve.wait_ge(b_ps, g + 1)
                dve.tensor_copy(bias[0:64, :, 0:14, 4 * g:4 * g + 4], bias_ps(g, 0))
                dve.tensor_copy(bias[64:128, :, 0:14, 4 * g:4 * g + 4], bias_ps(g, 1)).then_inc(b_evd, 1)
            dve.wait_ge(b_evd, 8)
            dve.wait_ge(b_eva, 8)
            link(dve.tensor_copy(bias[0:64, :, 14:22, :], bias[0:64, :, 2:10, :]))
            dve.wait_ge(b_eva, 9)
            dve.wait_ge(b_ok, 1)
            with dve.Fori(0, 4) as hp:
                link.loop(hp, 58)
                for e in range(2):
                    ins = dve.tensor_scalar(bst[e][:].rearrange("p a b -> p (a b)"),
                                            bias[:].rearrange("p h a b -> p h (a b)")[:, ds(hp * 2 + e, 1), :].rearrange("p o n -> p (o n)"),
                                            1.0, None, ALU.mult)
                link(ins)
                dve.wait_ge(kh_ok, hp + 1)
                dve.tensor_tensor(kl[:], p_kv[:, ds(hp, 1), :].rearrange("p a n -> p (a n)"), kh[:].bitcast(F32), ALU.subtract)
                link(dve.tensor_tensor(ql[:], p_q[:, ds(hp, 1), :].rearrange("p a n -> p (a n)"), qh[:].bitcast(F32), ALU.subtract))
                dve.nop().then_inc(st_ok, 1)
                dve.wait_ge(v_tp, hp + 1)
                dve.tensor_copy(vtm[:, 0:4, :], ps[:, 4, :].rearrange("p (a b) -> p a b", b=P)).then_inc(v_ev, 1)
                for s in range(19):
                    if 1 <= s <= 16:
                        u, e = s - 1, (s - 1) % 2
                        n = UNITS[u // 2][2] * GRID_W + CTX
                        dve.wait_ge(exp_ok, hp * 16 + (u + 1))
                        link(dve.tensor_tensor(asum[:, e, 2:3], asum[:, e, 0:1], asum[:, e, 1:2], ALU.add))
                        link(dve.reciprocal(asum[:, e, 3:4], asum[:, e, 2:3]))
                        dve.tensor_scalar(pr[:, e, 0:n], pr[:, e, 0:n], asum[:, e, 3:4], None, ALU.mult).then_inc(nrm_ok, 1)
                    if s >= 4 and s % 2 == 0:
                        qt = (s - 4) // 2
                        dve.wait_ge(pv_done, hp * 16 + (2 * qt + 2))
                        dve.tensor_scalar(p_q[:, ds(hp, 1), qt * P:(qt + 1) * P].rearrange("p a n -> p (a n)"),
                                          ps[:, 7, (qt % 2) * P:(qt % 2 + 1) * P], 1.0, None, ALU.mult).then_inc(ot_free, 1)
                    if s < 16:
                        _, _, kr, slot0 = UNITS[s // 2]
                        L, e = kr * GRID_W, s % 2
                        if s >= 2:
                            dve.wait_ge(t_done, hp * 16 + (s - 1))
                        dve.wait_ge(qk_done, hp * 16 + (s + 1))
                        dve.tensor_reduce(amax[:, e, 1:2], s_all(s)[:, L:L + CTX], axis=AX, op=ALU.max)
                        link(dve.tensor_tensor_reduce(out=pr[:, e, 0:L], in0=s_all(s)[:, 0:L],
                                                      in1=bst[e][:, slot0:slot0 + kr, :].rearrange("p a b -> p (a b)"),
                                                      scale=1.0, scalar=-3.0e38, op0=ALU.add, op1=ALU.max,
                                                      accum_out=amax[:, e, 0:1]))
                        dve.tensor_scalar(amax[:, e, 2:3], amax[:, e, 0:1], amax[:, e, 1:2], -1.0,
                                          ALU.max, ALU.mult).then_inc(mx_ok, 1)
                        if s == 15:
                            dve.nop().then_inc(st_free, 1)
                    if s % 2 == 1 and s < 16:
                        j = s // 2
                        dve.wait_ge(ada_ld[j % 2], hp * 64 + 16 * (j // 2 + 1))
                        link(mod_products(ada1[:, j % 2, :], mprod1, 0))
                    elif 2 <= s <= 16:
                        j = s // 2 - 1
                        if j >= 2:
                            dve.wait_ge(mod_done, hp * 8 + (16 + 2 + j - 1))
                        mod_reduce(mprod1, macc1[:, j % 2, :]).then_inc(mod_rd, 1)
                        dve.wait_ge(mod_rd, hp * 8 + (16 + j + 1))
                        dve.nop().then_inc(macc_ok, 1)
                link.end(4)
                dve.wait_ge(mod_done, hp * 8 + 26)
                dve.tensor_tensor(mod[:, ds(hp * 8 + 16, 8), 0], ps[:, 7, 384:392], colA[:, ds(hp * 8 + 48, 8)], ALU.add).then_inc(modp, 1)

            dve.wait_ge(modp, 5)
            link(dve.tensor_tensor(gmix[:], mod[:, 16:24, 0], colA[:, 8:16], ALU.mult))
            link(dve.tensor_tensor(gffn[:], mod[:, 40:48, 0], colA[:, 24:32], ALU.mult))
            link(dve.scalar_tensor_tensor(affn[:], mod[:, 32:40, 0], 1.0, colA[:, 16:24], ALU.add, ALU.mult))
            for h in range(2):
                with dve.Fori(0, 4) as i:
                    for b in range(2):
                        evac(ps[:, b, :], i * 2 + (J_OUT + 8 * h + b),
                             yo[h][:, ds(i * 2 + b, 1), :].rearrange("p a n -> p (a n)"))

            def rstd_of(N):
                dve.wait_ge(n_ps, KT * N + KT)
                dve.tensor_scalar(nrm[:], ps[:, 2, :], 1.0 / D, EPS, ALU.mult, ALU.add).then_inc(n_var, 1)
                dve.wait_ge(n_sqrt, N + 1)
                link(dve.reciprocal(rstd[:], nrm[:]))

            def norm_a(N, h):
                rstd_of(N)
                for k in range(KT):
                    link(dve.scalar_tensor_tensor(a_f[:], yo[h][:, k, :], gmix[:, k:k + 1], rstd[:], ALU.mult, ALU.mult))
                    dve.wait_ge(n_tp, KT * h + k + 1)
                    dve.tensor_tensor(x1[:, k, HS[h]], a_f[:], ps[:, 4 + k % 2, :], ALU.add).then_inc(n_x1, 1)
                    dve.wait_ge(n_x1, KT * h + k + 1)

            def norm_b(N, h):
                rstd_of(N)
                for k in range(KT):
                    link(dve.scalar_tensor_tensor(a_f[:], x1[:, k, HS[h]], affn[:, k:k + 1], rstd[:], ALU.mult, ALU.mult))
                    if k >= 2:
                        dve.wait_ge(n_hl, KT * h + k - 1)
                    dve.tensor_scalar(sq[:, k % 2, :], a_f[:], mod[:, 24 + k, 0:1], None, ALU.add).then_inc(n_h, 1)
                    dve.wait_ge(n_h, KT * h + k + 1)

            norm_a(0, 0)
            norm_b(1, 0)
            dve.wait_ge(n_hl, KT)
            norm_a(2, 1)

            for h in range(2):
                J0, E0 = J_FFN + h * (GU_JOBS + DOWN_JOBS), E_GU + h * GU_JOBS
                with dve.Fori(0, FT) as i:
                    link.loop(i, 1)
                    dve.wait_ge(g_tanh, i + (FT * h + 1))
                    dve.scalar_tensor_tensor(g_s[:], g_t[:], 1.0, ps[:, 0, :], ALU.add, ALU.mult).then_inc(acc_free, 1)
                    dve.wait_ge(acc_free, i * 2 + (E0 + 3))
                    dve.wait_ge(job_done, i * 2 + (J0 + 2))
                    dve.scalar_tensor_tensor(a_f[:], g_s[:], 0.5, ps[:, 1, :], ALU.mult, ALU.mult).then_inc(acc_free, 1)
                    dve.wait_ge(acc_free, i * 2 + (E0 + 4))
                    dve.nop().then_inc(g_a, 1)
                    dve.wait_ge(g_ah, i + (FT * h + 1))
                    link(dve.tensor_tensor(a_lo[:, ds(i, 1), :].rearrange("p a c -> p (a c)"), a_f[:],
                                           a_hi[:, ds(i, 1), :].bitcast(F32).rearrange("p a c -> p (a c)"), ALU.subtract))
                    dve.nop().then_inc(g_al, 1)
                link.end(FT)
                J0 += GU_JOBS
                if h == 1:
                    for b in range(2):
                        dve.wait_ge(st_out[b], 32)
                with dve.Fori(0, 4) as i:
                    for f in range(2):
                        dve.wait_ge(job_done, i * 6 + (J0 + 3 * f + 3))
                        dve.tensor_scalar(yd[:, ds(i * 2 + f, 1), :].rearrange("p a n -> p (a n)"),
                                          ps[:, 2 + f, :], 1.0, None, ALU.mult).then_inc(dn_free, 1)
                dve.wait_ge(dn_free, 8 * h + 10)
                rstd_of(3 + 2 * h)
                for k in range(KT):
                    link(dve.scalar_tensor_tensor(a_f[:], yd[:, k, :], gffn[:, k:k + 1], rstd[:], ALU.mult, ALU.mult))
                    link(dve.tensor_tensor(x1[:, k, HS[h]], a_f[:], x1[:, k, HS[h]], ALU.add))
                dve.nop().then_inc(n_fin, 1)
                for q in range(4):
                    o = 4 * h + q
                    dve.wait_ge(o_tp, o + 1)
                    if o >= 2:
                        dve.wait_ge(st_out[q % 2], 16 * (o // 2))
                    dve.tensor_copy(xin[:, q % 2, :],
                                    ps[:, 4 + 2 * (q % 2):6 + 2 * (q % 2), :].rearrange("p a b -> p (a b)")).then_inc(o_ev, 1)
                if h == 0:
                    norm_b(4, 1)

        @block.tensor
        def _(pe):
            def product2(J, b, dst, rhs, start=True, stop=True):
                for n, (w, ready) in enumerate(((w_hi, hi_done), (w_lo, lo_done))):
                    pe.wait_ge(ready, J + 1)
                    for k in range(KT):
                        ins = pe.matmul(dst, w[:, b, k * P:(k + 1) * P], rhs[:, k].rearrange("p a c -> p (a c)"),
                                        start=start and k == 0 and n == 0, stop=stop and k == KT - 1 and n == 1)
                ins.then_inc(job_done, 1)

            def product(J, b, dst, rhs, nk=KT, start=True, stop=True):
                pe.wait_ge(hi_done, J + 1)
                for k in range(nk):
                    for n, x in enumerate(rhs(k)):
                        pe.matmul(dst, w_hi[:, b, k * P:(k + 1) * P], x, start=start and k == 0 and n == 0, stop=False)
                pe.wait_ge(lo_done, J + 1)
                for k in range(nk):
                    ins = pe.matmul(dst, w_lo[:, b, k * P:(k + 1) * P], rhs(k)[0], start=False, stop=stop and k == nk - 1)
                ins.then_inc(job_done, 1)
                return ins

            npar = 2 + 7 + sum(A[n].shape[1] if len(A[n].shape) == 3 else 1 for n in
                               ("hy_conv_w", "hy_conv_b", "lru_conv_w", "lru_conv_b", "lru_ba", "lru_bi", "lru_lam")) + 3
            pe.wait_ge(par_ld, 16 * npar)
            pe.transpose(ps[:, 2, 0:96], rowsA[0:96, :], ident[0:96, 0:96])
            pe.transpose(ps[:, 2, 96:142], rowsB[0:46, :], ident[0:46, 0:46])
            pe.transpose(ps[0:64, 2, 142:146], rowsC[0:4, 0:64], ident[0:4, 0:4]).then_inc(cols_ps, 1)
            pe.wait_ge(flt_ld, 64)
            for j in range(2):
                ins = pe.matmul(ps[0:64, 4 + j, :], w12[0:33, 0, :], zf[0:33, j * 512:(j + 1) * 512], start=True, stop=True)
            ins.then_inc(f_ps, 1)
            pe.wait_ge(f_sin, 1)
            for j in range(2):
                ins = pe.matmul(ps[0:64, 6 + j, :], w12[0:64, 1, :], h1[0:64, j * 512:(j + 1) * 512], start=True, stop=True)
            ins.then_inc(f_ps, 1)
            pe.wait_ge(f_sin, 2)

            def taps(t):
                if t >= 2:
                    pe.wait_ge(k_dec, t - 1)
                for o in range(2):
                    ins = pe.matmul(ps[:, 4 + 2 * (t % 2) + o, :], h2f[0:64, t * P:(t + 1) * P],
                                    w3s[0:64, o * 512:(o + 1) * 512], start=True, stop=True)
                ins.then_inc(k_ps, 1)

            def magnitudes(t):
                pe.wait_ge(k_abs, t + 1)
                for o in range(2):
                    ins = pe.matmul(ps[:, 2 + o, :], ones[:], kabs[:, t % 2, o * 512:(o + 1) * 512], start=t == 0, stop=t == KT - 1)
                ins.then_inc(k_sum, 1)

            taps(0)
            for t in range(KT):
                if t + 1 < KT:
                    taps(t + 1)
                magnitudes(t)

            pe.wait_ge(k_dec, KT)
            pe.wait_ge(k_lo, KT)

            def spectra(i):
                for b, (hi, lo) in enumerate(((e_hi, e_lo), (o_hi, o_lo))):
                    pe.wait_ge(acc_free, i * 2 + (E_K + b + 1))
                    product(i * 2 + (J_K + b), b, ps[:, b, :], lambda k: (hi[:, k, :], lo[:, k, :]))

            def mod_sums(i):
                for b in range(2):
                    pe.wait_ge(mod_rd, i * 2 + (b + 1))
                    for cond in range(2):
                        ins = pe.matmul(ps[:, 7, ds(i * 4 + (2 * b + cond), 1)], macc[:, b, cond, :], ones[:, 0:1], start=True, stop=True)
                    ins.then_inc(mod_done, 1)

            spectra(0)
            with pe.Fori(1, 8) as i:
                spectra(i)
                mod_sums(i - 1)
            mod_sums(7)

            def turn_tile(n, s):
                pe.wait_ge(x_n, n + 1)
                for k in range(KT):
                    ins = pe.transpose(ps[:, 2 + 2 * s + k // 4, (k % 4) * P:(k % 4 + 1) * P], xin[:, s, k * P:(k + 1) * P], ident[:])
                ins.then_inc(x_tp, 1)

            def job_pair(i, J0, blk):
                hi, lo = HB[blk]
                w = BLOCKS[blk][2] * P
                for b in range(2):
                    pe.wait_ge(acc_free, i * 2 + (J0 + b + 1))
                    product(i * 2 + (J0 + b), b, ps[:, b, 0:w], lambda k: (hi[:, k, 0:w], lo[:, k, 0:w]))

            def jobs_loop(a, z, J0=J_LAT + 22, blk=2):
                with pe.Fori(0, (z - a) // 2) as i:
                    job_pair(i, J0 + a, blk)

            turn_tile(0, 0)
            turn_tile(1, 1)
            pe.wait_ge(x_lo, 2)
            with pe.Fori(0, 2) as i:
                for s in range(2):
                    job_pair(i * 2 + s, J_CTX, 0)
                    pe.wait_ge(x_mod, i * 2 + (s + 1))
                    turn_tile(i * 2 + (2 + s), s)
            jobs_loop(8, 10, J_CTX, 0)
            pe.wait_ge(x_lo, 6)
            with pe.Fori(0, 2) as i:
                for s in range(2):
                    job_pair(i * 4 + 2 * s, J_LAT, 1)
                    pe.wait_ge(x_mod, i * 2 + (s + 5))
                    turn_tile(i * 2 + (6 + s), s)
                    job_pair(i * 4 + (2 * s + 1), J_LAT, 1)
            jobs_loop(16, 22, J_LAT, 1)
            pe.wait_ge(x_lo, 10)
            jobs_loop(0, 4)
            pe.wait_ge(lw_ld, 256)
            at_pair = 0
            for q in range(4):
                c, d = q // 2, q % 2
                jobs_loop(4 + 2 * at_pair, 4 + 2 * LRU_AFTER[q])
                at_pair = LRU_AFTER[q]
                pe.wait_ge(l_conv, c + 1)
                for g in range(2):
                    for part, (o0, w_) in enumerate(((0, 256), (256, 512), (768, 512))):
                        if q:
                            pe.wait_ge(l_gate, (q - 1) * 6 + g * 3 + part + 1)
                        pe.matmul(ps[:, 2 + g * 3 + part, 0:w_], l_w[:, g * 4 + d * 2 + c, :], l_u[:, o0:o0 + w_],
                                  start=True, stop=True).then_inc(l_gp, 1)
            jobs_loop(4 + 2 * at_pair, 22) if at_pair < 9 else None

            for c in range(6):
                pe.wait_ge(c_ok, c + 1)
                if c >= 2:
                    pe.wait_ge(c_ev, c - 1)
                for t in range(KT):
                    bank = 4 + 2 * (c % 2) + t // 4
                    ins = pe.transpose(ps[:, bank, (t % 4) * P:(t % 4 + 1) * P], conv[:, c % 2, t * P:(t + 1) * P], ident[:])
                ins.then_inc(c_tp, 1)
            for o in range(2):
                J0, E0 = J_HY + 32 * o, E_FWD + 16 * o
                pe.wait_ge(u_lo_ok, 1 + 8 * o)
                pe.wait_ge(l_gate, 24)
                with pe.Fori(0, 8) as i:
                    for b in range(2):
                        pe.wait_ge(acc_free, i * 2 + (E0 + b + 1))
                        product2(i * 2 + (J0 + b), b, ps[:, b, :], u_s)
                pe.wait_ge(y_l, 8 * (o + 1))
                J0 += 16
                with pe.Fori(0, 4) as i:
                    for tp in range(2):
                        pe.wait_ge(inv_free, i * 2 + (8 * o + tp + 1))
                        for b in range(2):
                            product2(i * 4 + (J0 + 2 * tp + b), b, ps[:, 2 + tp, :], y_s[b], start=b == 0, stop=b == 1)
            pe.wait_ge(z_ok, 16)
            for c in range(2):
                for t in range(KT):
                    ins = pe.transpose(ps[:, 4 + 2 * c + t // 4, (t % 4) * P:(t % 4 + 1) * P], tm[:, t, 0, c * P:(c + 1) * P], ident[:])
                ins.then_inc(z_tp, 1)

            pe.wait_ge(sel_ld, 32)
            pe.transpose(ps[0:31, 2, 0:120], rpbr[0:120, 0:31], ident[0:120, 0:120]).then_inc(rp_tp, 1)
            pe.wait_ge(rp_ok, 1)
            for g in range(16):
                if g >= 4:
                    pe.wait_ge(b_evd if g % 2 == 0 else b_eva, (g - 4) // 2 + 1)
                for j in range(4):
                    ins = pe.matmul(ps[:, g % 4, j * 120:(j + 1) * 120], selt[0:32, 4 * g + j, :], rpbt[0:32, :],
                                    start=True, stop=True)
                ins.then_inc(b_ps, 1)
            pe.wait_ge(b_evd, 8)
            pe.wait_ge(b_eva, 8)
            pe.wait_ge(z_ev, 2)
            with pe.Fori(0, 4) as hp:
                pe.wait_ge(st_ok, hp * 2 + 2)
                for j in range(10):
                    ins = pe.transpose(ps[:, 4 + j // 4, (j % 4) * P:(j % 4 + 1) * P], vst[:, j * P:(j + 1) * P], ident[:])
                ins.then_inc(v_tp, 1)

                def scores(s):
                    e, (_, k0, kr, _) = s % 2, UNITS[s // 2]
                    if s >= 2:
                        pe.wait_ge(exp_ok, hp * 16 + (s - 1))
                    hh, qs = slice(64 * e, 64 * e + 64), slice((s // 2) * P, (s // 2 + 1) * P)
                    L, key0 = kr * GRID_W, CTX + k0 * GRID_W
                    parts = [(ps[:, 2 * e, :], key0, 512), (ps[:, 2 * e + 1, L - 512:L - 512 + CTX], 0, CTX)]
                    if L > 512:
                        parts.insert(1, (ps[:, 2 * e + 1, 0:L - 512], key0 + 512, L - 512))
                    for dst, a, w in parts:
                        for n, (q_, k_) in enumerate(((qh, kh), (qh, kl), (ql, kh))):
                            ins = pe.matmul(dst, q_[hh, qs], k_[hh, a:a + w], start=n == 0, stop=n == 2)
                    ins.then_inc(qk_done, 1)

                def turn(u):
                    e, kr = u % 2, UNITS[u // 2][2]
                    L = kr * GRID_W
                    if u == 0:
                        pe.wait_ge(v_ev, hp * 2 + 2)
                    pe.wait_ge(nrm_ok, hp * 16 + (u + 1))
                    for c in range(4):
                        pe.transpose(ps[:, 4 + e, c * P:(c + 1) * P], pr[:, e, c * P:(c + 1) * P], ident[:])
                    if u >= 1:
                        pe.wait_ge(pt_a, hp * 16 + u)
                    for c in range(2):
                        ins = pe.transpose(ps[:, 6, c * P:(c + 1) * P], pr[:, e, L + c * P:L + (c + 1) * P], ident[:])
                    if L > 512:
                        ins = pe.transpose(ps[0:64, 6, 256:384], pr[:, e, 512:576], ident[:])
                    ins.then_inc(t_done, 1)

                def values(u):
                    e, (_, k0, kr, _) = u % 2, UNITS[u // 2]
                    pe.wait_ge(pt_a, hp * 16 + (u + 1))
                    hh, qt = slice(64 * e, 64 * e + 64), u // 2
                    o_ = ps[64 * e:64 * e + 64, 7, (qt % 2) * P:(qt % 2 + 1) * P]
                    for c in range(4):
                        pe.matmul(o_, vtm[:, 2 + k0 // 2 + c, hh], pT[:, e, c, :], start=c == 0, stop=False)
                    if kr > WIN_R:
                        pe.matmul(o_, vtm[0:64, 2 + k0 // 2 + 4, hh], pT[0:64, e, 6, :], start=False, stop=False)
                    for c in range(2):
                        ins = pe.matmul(o_, vtm[:, c, hh], pT[:, e, 4 + c, :], start=False, stop=c == 1)
                    ins.then_inc(pv_done, 1)

                for s in range(18):
                    if s < 16:
                        scores(s)
                    if 1 <= s <= 16:
                        turn(s - 1)
                    if s >= 2 and s % 2 == 0:
                        pe.wait_ge(ot_free, hp * 8 + (s // 2 + 1))
                    if s == 2:
                        pe.wait_ge(modp, hp + 1)
                    if s >= 3 and s % 2 == 1:
                        j = (s - 3) // 2
                        pe.wait_ge(macc_ok, hp * 8 + (j + 1))
                        pe.matmul(ps[:, 7, 384 + j:385 + j], macc1[:, j % 2, :], ones[:, 0:1],
                                  start=True, stop=True).then_inc(mod_done, 1)
                    if s >= 2:
                        values(s - 2)

            for h in range(2):
                J0 = J_OUT + 8 * h
                pe.wait_ge(m_lo, KT * (h + 1))
                if h == 0:
                    pe.wait_ge(ot_free, 34)
                    pe.wait_ge(modp, 5)
                with pe.Fori(0, 4) as i:
                    for b in range(2):
                        pe.wait_ge(acc_free, i * 2 + (E_OUT + 8 * h + b + 1))
                        product(i * 2 + (J0 + b), b, ps[:, b, :], lambda k: (hb_hi[:, k, :], hb_lo[:, k, :]))

            def sum_squares(N):
                if N:
                    pe.wait_ge(n_var, N)
                for k in range(KT):
                    pe.wait_ge(n_sq, KT * N + k + 1)
                    pe.matmul(ps[:, 2, :], ones[:], sq[:, k % 2, :], start=k == 0, stop=k == KT - 1).then_inc(n_ps, 1)

            def x_turns(h):
                pe.wait_ge(xr_ld, 64 * (h + 1))
                for k in range(KT):
                    if KT * h + k >= 2:
                        pe.wait_ge(n_x1, KT * h + k - 1)
                    for q in range(4):
                        ins = pe.transpose(ps[:, 4 + k % 2, q * P:(q + 1) * P], xr2[:, q, k * P:(k + 1) * P], ident[:])
                    ins.then_inc(n_tp, 1)

            sum_squares(0)
            x_turns(0)
            sum_squares(1)
            sum_squares(2)
            x_turns(1)

            for h in range(2):
                J0, E0 = J_FFN + h * (GU_JOBS + DOWN_JOBS), E_GU + h * GU_JOBS
                pe.wait_ge(n_hl, KT * (h + 1))
                with pe.Fori(0, FT) as i:
                    for b in range(2):
                        pe.wait_ge(acc_free, i * 2 + (E0 + b + 1))
                        product(i * 2 + (J0 + b), b, ps[:, b, :], lambda k: (hb_hi[:, k, :], hb_lo[:, k, :]))
                J0 += GU_JOBS
                pe.wait_ge(g_al, FT * (h + 1))
                if h == 0:
                    pe.wait_ge(n_var, 3)
                with pe.Fori(0, 4) as i:
                    for q in range(6):
                        f, c = q // 3, q % 3
                        nk = KT if c < 2 else FT - 2 * KT
                        if c == 0:
                            pe.wait_ge(dn_free, i * 2 + (8 * h + f + 1))
                        product(i * 6 + (J0 + q), q % 2, ps[:, 2 + f, :],
                                lambda k: (a_hi[:, c * KT + k, :], a_lo[:, c * KT + k, :]), nk, start=c == 0, stop=c == 2)
                pe.wait_ge(dn_free, 8 * h + 10)
                sum_squares(3 + 2 * h)
                pe.wait_ge(n_fin, h + 1)
                for q in range(4):
                    o = 4 * h + q
                    if o >= 2:
                        pe.wait_ge(o_ev, o - 1)
                    for k in range(KT):
                        ins = pe.transpose(ps[:, 4 + 2 * (q % 2) + k // 4, (k % 4) * P:(k % 4 + 1) * P],
                                           x1[:, k, h * HALF + q * P:h * HALF + (q + 1) * P], ident[:])
                    ins.then_inc(o_tp, 1)
                if h == 0:
                    sum_squares(4)


_INS = ['x', 'c', 'ctx', 'c_ctx', 'ada_w', 'ada_b', 'g_mix_pre', 'g_mix_post', 'g_ffn_pre', 'g_ffn_post',
        'w_in', 'w_out', 'hy_conv_w', 'hy_conv_b', 'hy_f_w1', 'hy_f_b1', 'hy_f_w2', 'hy_f_b2', 'hy_f_w3',
        'hy_f_freq', 'hy_bias', 'na_rpb', 'lru_conv_w', 'lru_conv_b', 'lru_wa', 'lru_ba', 'lru_wi', 'lru_bi',
        'lru_lam', 'ffn_w_gu', 'ffn_w_down']


def kernel(**inputs):
    import concourse.bacc as bacc
    from concourse.bass_utils import run_bass_kernel_spmd

    nc = bacc.Bacc("TRN2", target_bir_lowering=False, num_devices=1)
    arrays = {name: np.ascontiguousarray(inputs[name]) for name in _INS}
    arrays.update(host_tables())
    aps = {}
    for name, a in arrays.items():
        aps[name] = nc.dram_tensor(f"in_{name}", a.shape, mybir.dt.from_np(a.dtype), kind="ExternalInput").ap()
    out = nc.dram_tensor("out_y", (1, SEQ, D), F32, kind="ExternalOutput").ap()
    program(nc, aps, out)
    r = run_bass_kernel_spmd(nc, [{f"in_{name}": a for name, a in arrays.items()}], core_ids=[0])
    return r.results[0]["out_y"]
```

```python
import math
from contextlib import ExitStack

import numpy as np

import concourse.bass as bass
from concourse import mybir

F32 = mybir.dt.float32
F32R = mybir.dt.float32r
ALU = mybir.AluOpType
ACT = mybir.ActivationFunctionType
AX = mybir.AxisListType.X
ds = bass.ds

P = 128
D = 1024
SEQ = 1024
CTX = 256
KT = D // P
HALF = 512
GRID_W = 64
ROWS = SEQ // GRID_W
HY = D // 4
HEADS = 8
DH = 64
WIN_R, WIN_C = 8, 16
FF = 2816
FT = FF // P
ALL = CTX + SEQ
NEG = -1e30
EPS = 1e-6
MAGIC = 12582912.0
TWO_PI_HEAD = 6.28125
TWO_PI_REST = 2.0 * math.pi - TWO_PI_HEAD

J_K, J_CTX, J_LAT, J_HY, J_OUT, J_FFN = 0, 16, 26, 70, 134, 150
E_K, E_CTX, E_LAT, E_FWD, E_OUT, E_GU = 0, 16, 26, 70, 102, 118
GU_JOBS, DOWN_JOBS = 2 * FT, 24
LRU_AFTER = (1, 3, 5, 7)
JOBS = J_FFN + 2 * (GU_JOBS + DOWN_JOBS)


def host_tables():
    t = np.arange(SEQ)
    ang4 = 2 * np.pi * (((2 * t[:, None] + 1) * (2 * t[None, :] + 1)) % (8 * SEQ)) / (8 * SEQ)
    angk = 2 * np.pi * ((2 * t[:, None] * (2 * t[None, :] + 1)) % (8 * SEQ)) / (8 * SEQ)

    def tiles(m):
        return np.ascontiguousarray(m.reshape(KT, P, KT, P).transpose(2, 1, 0, 3).reshape(KT, P, D))

    four = np.stack([tiles(np.cos(ang4)), tiles(np.sin(ang4))], 1).astype(np.float32)
    fourk = np.stack([tiles(np.cos(angk)), tiles(np.sin(angk))], 1).astype(np.float32)
    tt = t.astype(np.float32) / np.float32(SEQ)
    bands = np.arange(1, 17, dtype=np.float32)
    ang = np.float32(2 * math.pi) * tt[:, None] * bands[None, :]
    z = np.concatenate([tt[:, None], np.cos(ang), np.sin(ang)], 1).astype(np.float32).T
    deltas = np.abs(np.linspace(math.log(1e-2) / 0.3, math.log(1e-2) / 1.5, HY, dtype=np.float32))
    decay = np.exp(-tt[:, None] * deltas[None, :]).astype(np.float32)
    sel = np.zeros((32, GRID_W, GRID_W), np.float32)
    q = np.arange(GRID_W)
    start = np.clip(q - WIN_C // 2, 0, GRID_W - WIN_C)
    for kc in range(GRID_W):
        for qc in range(GRID_W):
            if start[qc] <= kc < start[qc] + WIN_C:
                sel[kc - qc + WIN_C - 1, kc, qc] = 1.0
            else:
                sel[31, kc, qc] = 1.0
    sel = np.concatenate([sel, sel], 2).reshape(32, GRID_W * P)
    return {
        "four": four, "fourk": fourk, "zfeat": np.ascontiguousarray(z),
        "decay": np.ascontiguousarray(decay.reshape(KT, P, HY).transpose(1, 0, 2)),
        "sel": np.ascontiguousarray(sel), "ident": np.eye(P, dtype=np.float32),
        "ones": np.ones((P, P), np.float32),
    }


def units():
    out = []
    for r in range(0, ROWS, 2):
        k0 = min(max(r - WIN_R // 2, 0), ROWS - WIN_R)
        k1 = min(max(r + 1 - WIN_R // 2, 0), ROWS - WIN_R) + WIN_R
        if k1 - k0 > WIN_R:
            out.append((r, k0, k1 - k0, 14))
        else:
            out.append((r, k0, k1 - k0, k0 - r + 7 - 1))
    return out


UNITS = units()


def program(nc, A, out):
    ctx = ExitStack()
    with ctx:
        base = 16512

        def at(name, off, shape, dt=F32):
            return nc.alloc_sbuf_tensor_at(name, [P] + list(shape), dt, offset=base + off)

        def sem(name):
            return ctx.enter_context(nc.semaphore(name))

        P_HY, P_Q, P_KV, P_XG, H_, S_, SM = 24576, 49152, 65536, 116736, 124928, 157696, 206848
        arena = nc.alloc_sbuf_tensor("arena", [P, 212832 // 4], F32)
        raw = at("raw", 0, [2, D])
        w_hi = at("w_hi", 8192, [2, D], F32R)
        w_lo = at("w_lo", 16384, [2, D], F32R)
        p_hy = at("p_hy", P_HY, [6, SEQ])
        p_q = at("p_q", P_Q, [4, SEQ])
        p_kv = at("p_kv", P_KV, [10, ALL])
        p_xg = at("p_xg", P_XG, [2, SEQ])
        hb_hi = at("hb_hi", H_, [KT, HALF], F32R)
        hb_lo = at("hb_lo", H_ + 16384, [KT, HALF], F32R)
        e_hi = at("e_hi", P_HY, [KT, HALF], F32R)
        e_lo = at("e_lo", P_HY + 16384, [KT, HALF], F32R)
        o_hi = at("o_hi", P_HY + 32768, [KT, HALF], F32R)
        o_lo = at("o_lo", P_HY + 49152, [KT, HALF], F32R)
        kt_ = at("kt_", 90112, [2, 2, 2, HY])
        eo = at("eo", 98304, [2, 2, HY])
        kabs = at("kabs", 102400, [2, D])
        inv = at("inv", 110592, [2, HY])
        inv_t = at("inv_t", 112640, [2, HY])
        zf = at("zf", H_, [SEQ])
        farg = at("farg", H_ + 4096, [SEQ])
        fturn = at("fturn", H_ + 8192, [SEQ])
        h1 = at("h1", H_ + 12288, [SEQ])
        h2f = at("h2f", H_ + 16384, [SEQ])
        w3s = at("w3s", H_ + 20480, [D])
        w12 = at("w12", H_ + 24576, [2, 64])
        rowsA = at("rowsA", H_ + 25600, [P])
        rowsB = at("rowsB", H_ + 26112, [P])
        rowsC = at("rowsC", H_ + 26624, [P])
        kev = at("kev", S_, [2, 2, HY])
        mprod = at("mprod", S_ + 4096, [D])
        macc = at("macc", S_ + 8192, [2, 2, P])
        ada0 = at("ada0", S_ + 12288, [4, D])
        dec = at("dec", S_ + 40960, [KT, HY])
        xin = at("xin", S_ + 32768, [2, D])
        xmod = at("xmod", S_ + 40960, [2, D])
        hb2_hi = at("hb2_hi", S_, [KT, HALF], F32R)
        hb2_lo = at("hb2_lo", S_ + 16384, [KT, HALF], F32R)
        xstat = at("xstat", S_ + 28672, [2, D])
        xsqr = at("xsqr", S_ + 36864, [D])
        l_u, l_r, l_i, l_s, l_q, l_a = (at(f"l_{n}", S_ + 5120 * k, [ALL]) for k, n in enumerate("urisqa"))
        l_h = at("l_h", S_ + 30720, [2, ALL])
        l_w = at("l_w", S_ + 40960, [8, P])
        tm = at("tm", H_, [KT, 3, HY])
        conv = at("conv", H_ + 24576, [2, SEQ])
        kspec = at("kspec", S_, [KT, 2, HY])
        y_s = [at("y_re", P_HY, [KT, 2, HY], F32R), at("y_im", S_ + 16384, [KT, 2, HY], F32R)]
        u_s = at("u_s", S_ + 32768, [KT, 2, HY], F32R)
        hy0 = P_KV + 8 * 5120
        prodA = at("prodA", hy0, [2, HY])
        prodB = at("prodB", hy0 + 2048, [2, HY])
        ysum = at("ysum", hy0 + 4096, [2, HY])
        hyb = at("hyb", hy0 + 6144, [2, HY])
        zb = at("zb", hy0 + 8192, [HY])
        zs = at("zs", hy0 + 9216, [HY])
        mix_hy = at("mix_hy", P_HY, [2, SEQ])
        bias = at("bias", H_, [HEADS, 23, GRID_W])
        A0 = H_ + 47104
        selt = at("selt", A0, [GRID_W, P])
        pr = at("pr", A0, [2, 832])
        pT = at("pT", A0 + 6656, [2, 7, P])
        qh, ql = at("qh", A0 + 13824, [SEQ], F32R), at("ql", A0 + 17920, [SEQ], F32R)
        kh, kl = at("kh", A0 + 22016, [ALL], F32R), at("kl", A0 + 27136, [ALL], F32R)
        bst = [at("bst0", 0, [23, GRID_W]), at("bst1", 5888, [23, GRID_W])]
        vst = at("vst", 11776, [ALL])
        mprod1 = at("mprod1", 16896, [D])
        macc1 = at("macc1", 20992, [2, P])
        vtm = at("vtm", P_HY + 8192, [10, P])
        rpbt = at("rpbt", P_HY + 13312, [120])
        rpbr = at("rpbr", S_ + 8192, [32])
        ada1 = at("ada1", P_HY + 14336, [2, D])
        x1 = at("x1", S_, [KT, SEQ])
        yo = [at("yo0", P_KV, [KT, HALF]), at("yo1", P_KV + 16384, [KT, HALF])]
        xr2 = at("xr2", P_HY + 8192, [4, D])
        yd = at("yd", S_ + 32768, [KT, HALF])
        hb3_hi = at("hb3_hi", S_ + 32768, [KT, HALF], F32R)
        hb3_lo = at("hb3_lo", P_KV + 32768, [KT, HALF], F32R)
        ysq = at("ysq", S_ + 2048, [HALF])
        yacc = at("yacc", S_ + 6144, [HALF])
        x1sq = at("x1sq", H_ + 16384, [KT, HALF])
        ost = at("ost", S_ + 32768, [4, D])
        a_hi = at("a_hi", P_HY, [FT, HALF], F32R)
        a_lo = at("a_lo", P_HY + 45056, [FT, HALF], F32R)
        F0 = P_HY + 90112
        g_t = at("g_t", F0, [HALF])
        sq = at("sq", F0, [2, HALF])
        a_f = at("a_f", F0 + 4096, [HALF])
        rstd = at("rstd", F0 + 6144, [HALF])
        nrm = at("nrm", F0 + 8192, [HALF])
        so = [SM]

        def small(name, shape):
            n = 4 * int(np.prod(shape))
            n = -(-n // 32) * 32
            t = at(name, so[0], shape)
            so[0] += n
            assert so[0] <= 212832 - 0, so[0]
            return t

        ident = small("ident", [P])
        ones = small("ones", [P])
        colA = small("colA", [96])
        colB = small("colB", [48])
        colC = small("colC", [4])
        sil = small("sil", [2, KT])
        sil_t = small("sil_t", [16])
        mod = small("mod", [48, 2])
        amix = small("amix", [KT, 2])
        affn = small("affn", [KT])
        gmix = small("gmix", [KT])
        gffn = small("gffn", [KT])
        ssq = small("ssq", [10])
        rx = small("rx", [10])
        lam = small("lam", [8, 4])
        hbias = small("hbias", [8])
        amax = small("amax", [2, 4])
        asum = small("asum", [2, 4])

        ps = ctx.enter_context(nc.psum_tensor("ps", [P, 8, 512], F32))

        raw_ld = [sem("raw_ld0"), sem("raw_ld1")]
        hi_done, lo_done, job_done, acc_free = sem("hi_done"), sem("lo_done"), sem("job_done"), sem("acc_free")
        ada_ld = [sem("ada_ld0"), sem("ada_ld1")]
        mix_ld = [sem(f"mix_ld{q}") for q in range(4)]
        mod_done, mod_rd = sem("mod_done"), sem("mod_rd")
        macc_ok, kspec_ld, nrm_ok, kh_ok = [sem(n) for n in ("macc_ok", "kspec_ld", "nrm_ok", "kh_ok")]
        ks_out = [sem("ks_out0"), sem("ks_out1")]
        spec = nc.dram_tensor("spec", (2, KT, P, 2 * HY), F32, kind="Internal").ap()
        par_ld, flt_ld, dec_ld = sem("par_ld"), sem("flt_ld"), sem("dec_ld")
        x_ld = [sem("x_ld0"), sem("x_ld1")]
        xs_ld = [sem("xs_ld0"), sem("xs_ld1")]
        dchain = sem("dchain")
        achain = sem("achain")
        cols_ps, cols_ok = sem("cols_ps"), sem("cols_ok")
        silt_ok, sil_ok, silp_ok = sem("silt_ok"), sem("sil_ok"), sem("silp_ok")
        f_ps, f_arg, f_sin = sem("f_ps"), sem("f_arg"), sem("f_sin")
        k_ps, k_dec, k_abs, k_eo, k_hi, k_lo, k_sum = [sem("k_" + n) for n in ("ps", "dec", "abs", "eo", "hi", "lo", "sum")]
        amix_ok = sem("amix_ok")
        x_sq, x_rs, x_sqrt, x_n, x_tp, x_mod, x_hi, x_lo = [sem("x_" + n) for n in ("sq", "rs", "sqrt", "n", "tp", "mod", "hi", "lo")]
        lw_ld, l_conv, l_gp, l_gate, l_dve, l_act, l_done, lam_a, lam_d, l_zero = [
            sem(n) for n in ("lw_ld", "l_conv", "l_gp", "l_gate", "l_dve", "l_act", "l_done", "lam_a", "lam_d", "l_zero")]
        hyb_ld, c_ok, c_tp, c_ev, u_hi_ok, u_lo_ok, y_f, y_h, y_l, inv_free, z_ok, z_tp, z_ev = [
            sem(n) for n in ("hyb_ld", "c_ok", "c_tp", "c_ev", "u_hi_ok", "u_lo_ok", "y_f", "y_h", "y_l",
                             "inv_free", "z_ok", "z_tp", "z_ev")]
        sel_ld, rp_tp, rp_ok, b_ps, b_evd, b_eva, b_ok = [
            sem(n) for n in ("sel_ld", "rp_tp", "rp_ok", "b_ps", "b_evd", "b_eva", "b_ok")]
        st_free, st_ok, v_tp, v_ev, qk_done, mx_ok, exp_ok, t_done, pt_d, pt_a, pv_done, rec_ok, o_ok, ot_done, ot_free, modp, att_x = [
            sem(n) for n in ("st_free", "st_ok", "v_tp", "v_ev", "qk_done", "mx_ok", "exp_ok", "t_done", "pt_d",
                             "pt_a", "pv_done", "rec_ok", "o_ok", "ot_done", "ot_free", "modp", "att_x")]
        vst_ok, rp_ld = sem("vst_ok"), sem("rp_ld")
        m_ld, n_sum, o_ea = sem("m_ld"), sem("n_sum"), sem("o_ea")
        m_hi, m_lo, xr_ld, gates_ok, n_sq, n_ps, n_var, n_sqrt, n_fin, n_tp, n_x1, n_h, n_hh, n_hl, bst_ok, f_mm = [
            sem(n) for n in ("m_hi", "m_lo", "xr_ld", "gates_ok", "n_sq", "n_ps", "n_var", "n_sqrt", "n_fin",
                             "n_tp", "n_x1", "n_h", "n_hh", "n_hl", "bst_ok", "f_mm")]
        g_tanh, g_a, g_ah, g_al, dn_done, dn_free, y_ok = [
            sem(n) for n in ("g_tanh", "g_a", "g_ah", "g_al", "dn_done", "dn_free", "y_ok")]
        o_tp, o_ev, st_out = sem("o_tp"), sem("o_ev"), [sem("st_out0"), sem("st_out1")]

        block = ctx.enter_context(nc.Block())

        w_in = A["w_in"][0].rearrange("(k p) n -> p k n", p=P)
        w_out = A["w_out"][0].rearrange("(k p) n -> p k n", p=P)
        w_gu = A["ffn_w_gu"][0].rearrange("(k p) n -> p k n", p=P)
        w_dn = A["ffn_w_down"][0].rearrange("(k p) n -> p k n", p=P)
        ada = A["ada_w"][0].rearrange("(k p) n -> p k n", p=P)
        x_tok = A["x"][0]
        c_tok = A["ctx"][0]

        BLOCKS = [(c_tok, 0, 2, 1, J_CTX, 10), (x_tok, 0, 4, 0, J_LAT, 22), (x_tok, 4, 4, 0, J_LAT + 22, 22)]
        TILES = [(src, t0 + t) for src, t0, cnt, _, _, _ in BLOCKS for t in range(cnt)]
        HB = [(hb_hi, hb_lo), (hb2_hi, hb2_lo), (hb_hi, hb_lo)]
        HS = [slice(0, HALF), slice(HALF, SEQ)]

        def mix_src(k, h):
            src = (mix_hy[:, k] if k < 2 else p_q[:, k - 2] if k < 6 else p_xg[:, k - 6])
            return src[:, HS[h]]

        def bias_ps(g, half):
            v = ps[64 * half:64 * half + 64, g % 4, 0:480].rearrange("p (j h r) -> p h r j", j=4, h=HEADS)
            return v[:, :, 1:15, :] if half == 0 else v[:, :, 0:14, :]

        def s_all(s):
            return ps[:, 2 * (s % 2):2 * (s % 2) + 2, :].rearrange("p a b -> p (a b)")

        @block.sync
        def _(sp):
            sp.dma_start(ident[:], A["ident"]).then_inc(par_ld, 16)
            sp.dma_start(ones[:], A["ones"]).then_inc(par_ld, 16)
            r8 = lambda ap: ap.rearrange("(k p) -> k p", p=P)
            off = 0
            for src in [A[n][0] for n in ("g_mix_pre", "g_mix_post", "g_ffn_pre", "g_ffn_post", "ada_b", "c")] + [A["c_ctx"]]:
                src = r8(src)
                sp.dma_start(rowsA[off:off + src.shape[0], :], src).then_inc(par_ld, 16)
                off += src.shape[0]
            off = 0
            for name in ("hy_conv_w", "hy_conv_b", "lru_conv_w", "lru_conv_b", "lru_ba", "lru_bi", "lru_lam"):
                src = A[name][0] if len(A[name].shape) == 3 else A[name]
                for r in range(src.shape[0]):
                    v = r8(src[r])
                    sp.dma_start(rowsB[off:off + v.shape[0], :], v).then_inc(par_ld, 16)
                    off += v.shape[0]
            sp.dma_start(rowsC[0:1, 0:64], A["hy_f_b1"]).then_inc(par_ld, 16)
            sp.dma_start(rowsC[1:2, 0:64], A["hy_f_b2"]).then_inc(par_ld, 16)
            sp.dma_start(rowsC[2:4, 0:64], A["hy_f_freq"][0]).then_inc(par_ld, 16)
            sp.dma_start(zf[0:33, :], A["zfeat"]).then_inc(flt_ld, 16)
            sp.dma_start(w12[0:33, 0, :], A["hy_f_w1"][0]).then_inc(flt_ld, 16)
            sp.dma_start(w12[0:64, 1, :], A["hy_f_w2"][0]).then_inc(flt_ld, 16)
            sp.dma_start(w3s[0:64, :], A["hy_f_w3"][0]).then_inc(flt_ld, 16)
            sp.dma_start(dec[:], A["decay"]).then_inc(dec_ld, 16)

            def raw_dma(b, J, src, nk=KT, first=False):
                if not first:
                    sp.wait_ge(lo_done, J - 1)
                sp.dma_start(raw[:, b, 0:nk * P].rearrange("p (k n) -> p k n", n=P), src).then_inc(raw_ld[b], 16)

            def phase(J0, pairs, src, begin=1):
                with sp.Fori(begin, pairs) as i:
                    for b in range(2):
                        raw_dma(b, i * 2 + (J0 + b), src(i, b))

            def pair0(J0, src):
                for b in range(2):
                    raw_dma(b, J0 + b, src(0, b), first=J0 == 0)

            fk = A["fourk"].rearrange("m c p n -> (m c) p n")
            f4 = A["four"].rearrange("m c p n -> (m c) p n")
            one = lambda ap: ap.rearrange("o p (k n) -> p (o k) n", n=P)
            src_k = lambda i, b: one(fk[ds(i * 2 + b, 1)])
            src_4 = lambda i, b: one(f4[ds(i * 2 + b, 1)])
            src_c = lambda i, b: w_in[:, :, ds((i * 2 + (10 + b)) * P, P)]
            src_l = lambda i, b: w_in[:, :, ds((i * 2 + b) * P, P)]
            src_o = lambda i, b: w_out[:, :, ds((i * 2 + b) * P, P)]
            src_g = lambda i, b: w_gu[:, :, ds(i * P + b * FF, P)]

            def ada_dma(dst, q, n, src, landed):
                if n is not None:
                    sp.wait_ge(mod_rd, n)
                sp.dma_start(dst[:, q, :].rearrange("p (k n) -> p k n", n=P), src).then_inc(landed[q], 16)

            def lru_w_dma():
                sp.wait_ge(l_zero, 1)
                for g, name in enumerate(("lru_wa", "lru_wi")):
                    for d in range(2):
                        for c in range(2):
                            for e in range(2):
                                sp.dma_start(l_w[64 * e:64 * e + 64, g * 4 + d * 2 + c, 64 * e:64 * e + 64],
                                             A[name][0, d, 2 * c + e]).then_inc(lw_ld, 16)

            pair0(J_K, src_k)
            for q in range(4):
                ada_dma(ada0, q, None, ada[:, :, q * P:(q + 1) * P], mix_ld)
            ks_dst = spec.rearrange("o m p (c n) -> c p m o n", c=2)

            def spectrum_out(i, b, n):
                sp.wait_ge(acc_free, n)
                sp.dma_start(ks_dst[b, :, ds(i, 1)].rearrange("p m o n -> p (m o) n"), kev[:, b]).then_inc(ks_out[b], 16)

            raw_dma(0, J_K + 2, src_k(1, 0))
            with sp.Fori(0, 3) as i:
                for q in range(4):
                    b, pair = (q + 1) % 2, i * 2 + (q + 3) // 2
                    raw_dma(b, i * 4 + (J_K + q + 3), src_k(pair, b))
                    spectrum_out(i * 2 + q // 2, q % 2, i * 4 + (q + 3))
                    ada_dma(ada0, q, i * 4 + (q + 1), ada[:, :, ds((i * 4 + (q + 4)) * P, P)], mix_ld)
            raw_dma(1, J_K + 15, src_k(7, 1))
            for b in range(2):
                spectrum_out(6, b, 15 + b)
            pair0(J_CTX, src_c)
            for b in range(2):
                spectrum_out(7, b, 17 + b)
            phase(J_CTX, 5, src_c)
            for J0 in (J_LAT, J_LAT + 22):
                pair0(J0, lambda i, b: w_in[:, :, (18 + b) * P:(19 + b) * P])
                pair0(J0 + 2, lambda i, b: w_in[:, :, (20 + b) * P:(21 + b) * P])
                if J0 == J_LAT + 22:
                    lru_w_dma()
                phase(J0 + 4, 9, src_l, 0)
            pair0(J_HY, src_4)
            sp.wait_ge(l_done, 4)
            sp.dma_start(hyb[:].rearrange("p a b -> p (a b)"),
                         A["hy_bias"].rearrange("a o c -> a (o c)").broadcast_to([P, 2 * HY])).then_inc(hyb_ld, 16)
            def kspec_dma(o):
                sp.dma_start(kspec[:].rearrange("p m c n -> p m (c n)"), spec[o].rearrange("m p n -> p m n")).then_inc(kspec_ld, 16)

            for b in range(2):
                sp.wait_ge(ks_out[b], 144)
            kspec_dma(0)
            for p in range(4):
                phase(J_HY + 16 * p, 8, src_4)
                if p == 1:
                    sp.wait_ge(inv_free, 3)
                    kspec_dma(1)
                if p < 3:
                    pair0(J_HY + 16 * (p + 1), src_4)
            sp.wait_ge(y_l, 16)
            sp.dma_start(rpbr[0:120, 0:31], A["na_rpb"][0].rearrange("h r c -> (h r) c")).then_inc(rp_ld, 16)
            sp.wait_ge(job_done, J_OUT)
            sp.dma_start(selt[0:32, :, :], A["sel"].rearrange("j (k q) -> j k q", q=P)).then_inc(sel_ld, 16)
            sp.wait_ge(z_tp, 2)
            for b in range(2):
                ada_dma(ada1, b, 15 + b, ada[:, :, (16 + b) * P:(17 + b) * P], ada_ld)
            with sp.Fori(1, 16) as i:
                for b in range(2):
                    ada_dma(ada1, b, i * 2 + (15 + b), ada[:, :, ds((i * 2 + (16 + b)) * P, P)], ada_ld)
            sp.wait_ge(pv_done, 64)
            sp.wait_ge(mod_done, 50)
            pair0(J_OUT, src_o)
            for q in range(4):
                sp.dma_start(xr2[:, q, :], x_tok[q * P:(q + 1) * P, :]).then_inc(xr_ld, 16)
            phase(J_OUT, 4, src_o)
            pair0(J_OUT + 8, src_o)
            phase(J_OUT + 8, 4, src_o)
            pair0(J_FFN, src_g)
            sp.wait_ge(n_tp, 8)
            for q in range(4):
                sp.dma_start(xr2[:, q, :], x_tok[(4 + q) * P:(5 + q) * P, :]).then_inc(xr_ld, 16)
            for h in range(2):
                J0 = J_FFN + h * (GU_JOBS + DOWN_JOBS)

                def outputs(q):
                    sp.wait_ge(o_ev, q + 1)
                    sp.dma_start(out[0, q * P:(q + 1) * P, :], xin[:, q % 2, :]).then_inc(st_out[q % 2], 16)

                if h == 0:
                    phase(J0, FT, src_g)
                else:
                    for i in range(1, 5):
                        for b in range(2):
                            raw_dma(b, J0 + 2 * i + b, src_g(i, b))
                        if i >= 3:
                            outputs(2 * (i - 3))
                            outputs(2 * (i - 3) + 1)
                    phase(J0, FT, src_g, 5)
                J0 += GU_JOBS
                with sp.Fori(0, 4) as i:
                    for q in range(6):
                        c = q % 3
                        nk = KT if c < 2 else FT - 2 * KT
                        raw_dma(q % 2, i * 6 + (J0 + q),
                                w_dn[:, c * KT:c * KT + nk, ds((i * 2 + q // 3) * P, P)], nk)
                if h == 0:
                    pair0(J0 + DOWN_JOBS, src_g)
            for q, done, n in ((0, o_ev, 5), (2, o_ea, 1), (1, o_ev, 6), (3, o_ea, 2)):
                sp.wait_ge(done, n)
                sp.dma_start(out[0, (4 + q) * P:(5 + q) * P, :], ost[:, q, :]).then_inc(st_out[q % 2], 16)
            for b in range(2):
                sp.wait_ge(st_out[b], 64)

        @block.scalar
        def _(act):
            def split(J, half, b, first=False):
                act.wait_ge(raw_ld[b], half * 16 + 16)
                if not first:
                    act.wait_ge(job_done, J - 1)
                act.activation(w_hi[:, b, :], raw[:, b, :], ACT.Copy).then_inc(hi_done, 1)

            def split_next(i, J0, b):
                split(i * 2 + (J0 + b + 1), i + (J0 // 2 + b), 1 - b)

            def split_loop(n, J0):
                with act.Fori(0, n // 2) as i:
                    for b in range(2):
                        split_next(i, J0, b)

            def x_dma(n):
                src, t = TILES[n]
                act.dma_start(xin[:, n % 2, :], src[t * P:(t + 1) * P, :]).then_inc(x_ld[n % 2], 16)

            def stats_dma(n):
                src, t = TILES[n]
                act.dma_start(xstat[:, n % 2, :], src[t * P:(t + 1) * P, :]).then_inc(xs_ld[n % 2], 16)

            def mean_square(n):
                if n:
                    act.wait_ge(x_sq, n)
                act.wait_ge(xs_ld[n % 2], 16 * (n // 2 + 1))
                act.activation(xsqr[:], xstat[:, n % 2, :], ACT.Square, accum_out=ssq[:, n:n + 1]).then_inc(x_sq, 1)
                if n + 2 < len(TILES):
                    act.wait_ge(x_sq, n + 1)
                    stats_dma(n + 2)

            stats_dma(0)
            stats_dma(1)
            act.wait_ge(cols_ok, 1)
            act.activation(sil_t[:], colA[:, 80:96], ACT.Tanh, scale=0.5).then_inc(silt_ok, 1)
            for layer, dst in ((0, h1), (1, h2f)):
                act.wait_ge(f_arg, layer + 1)
                act.activation(dst[0:64, :], farg[0:64, :], ACT.Sin).then_inc(f_sin, 1)
            split(0, 0, 0, first=True)
            split(1, 0, 1, first=True)
            mean_square(0)
            mean_square(1)
            for t in range(KT):
                s = t % 2
                mean_square(t + 2)
                act.wait_ge(k_dec, t + 1)
                if t >= 2:
                    act.wait_ge(k_sum, t - 1)
                act.activation(kabs[:, s, :], kt_[:, s].rearrange("p a b c -> p (a b c)"), ACT.Abs).then_inc(k_abs, 1)
                act.wait_ge(k_eo, t + 1)
                act.activation(e_hi[:, t, :], eo[:, 0].rearrange("p a b -> p (a b)"), ACT.Copy)
                act.activation(o_hi[:, t, :], eo[:, 1].rearrange("p a b -> p (a b)"), ACT.Copy).then_inc(k_hi, 1)
            act.wait_ge(x_rs, 1)
            act.activation(rx[:], rx[:], ACT.Sqrt).then_inc(x_sqrt, 1)
            act.wait_ge(x_sq, 10)
            x_dma(0)
            x_dma(1)
            with act.Fori(1, 8) as i:
                for b in range(2):
                    split(i * 2 + (J_K + b), i + J_K // 2, b)

            def head_of(J):
                split(J, J // 2, J % 2)

            def tile_head(n, blk, t):
                act.wait_ge(x_mod, n + 1)
                if n + 2 < len(TILES):
                    x_dma(n + 2)
                act.activation(HB[blk][0][:, :, t * P:(t + 1) * P],
                               xmod[:, n % 2, :].rearrange("p (k n) -> p k n", n=P), ACT.Copy).then_inc(x_hi, 1)

            head_of(J_CTX)
            tile_head(0, 0, 0)
            tile_head(1, 0, 1)
            for b in range(2):
                act.wait_ge(ks_out[b], 144)
            for t in range(4):
                head_of(J_CTX + 2 * t + 1)
                head_of(J_CTX + 2 * t + 2)
                tile_head(2 + t, 1, t)
            head_of(J_CTX + 9)
            head_of(J_LAT)
            act.wait_ge(lam_d, 1)
            act.activation(lam[:, 1, :], lam[:, 0, :], ACT.Exp, scale=-1.0).then_inc(lam_a, 1)
            for t in range(4):
                for m in range(1, 5):
                    if m == 3:
                        if t == 0:
                            act.wait_ge(job_done, J_LAT)
                        tile_head(6 + t, 2, t)
                    head_of(J_LAT + 4 * t + m)
            with act.Fori(8, 11) as i:
                for b in range(2):
                    split_next(i, J_LAT, b)

            J0 = J_LAT + 22
            step = iter(range(22))

            def split_step(n=1):
                for _ in range(n):
                    j = next(step)
                    split_next(j // 2, J0, j % 2)

            split_step(4)
            act.wait_ge(lam_d, 2)
            for c in range(2):
                for d in range(2):
                    q = c * 2 + d
                    split_step(LRU_AFTER[q] * 2 - (LRU_AFTER[q - 1] * 2 + 2 if q else 0))
                    if q:
                        act.wait_ge(l_done, q)
                    for g, dst in ((0, l_r), (1, l_i)):
                        for part, (o0, w) in enumerate(((0, 256), (256, 512), (768, 512))):
                            act.wait_ge(l_gp, (q * 2 + g) * 3 + part + 1)
                            act.activation(dst[:, o0:o0 + w], ps[:, 2 + g * 3 + part, 0:w], ACT.Tanh, scale=0.5,
                                           bias=hbias[:, g * 4 + d * 2 + c:g * 4 + d * 2 + c + 1]).then_inc(l_gate, 1)
                    if d == 0:
                        act.wait_ge(l_dve, c + 1)
                        act.activation(l_q[:, 0:SEQ], l_q[:, 0:SEQ], ACT.Tanh, scale=0.7978845608028654).then_inc(l_act, 1)
                    split_step()
                    act.wait_ge(l_gate, q * 6 + 6)
                    act.activation(l_a[:], l_r[:], ACT.Exp, scale=lam[:, 7, d * 2 + c:d * 2 + c + 1],
                                   bias=lam[:, 7, d * 2 + c:d * 2 + c + 1])
                    act.activation(l_s[:], l_r[:], ACT.Tanh, scale=lam[:, 2, d * 2 + c:d * 2 + c + 1],
                                   bias=lam[:, 2, d * 2 + c:d * 2 + c + 1]).then_inc(l_act, 1)
                    act.wait_ge(l_act, 5 * c + 2 * d + 2)
                    act.activation(l_r[:], l_s[:], ACT.Sqrt, scale=0.25).then_inc(l_act, 1)
                    split_step()
            split_step(2)
            assert next(step, None) is None

            def channels_in(c):
                act.wait_ge(c_tp, c + 1)
                act.activation(tm[:, :, c // 2, (c % 2) * P:(c % 2) * P + P],
                               ps[:, 4 + 2 * (c % 2):6 + 2 * (c % 2), :].rearrange("p a (t n) -> p (a t) n", n=P),
                               ACT.Copy).then_inc(c_ev, 1)

            channels_in(0)
            channels_in(1)
            act.wait_ge(c_ev, 2)
            act.activation(u_s[:, :, 0, :], tm[:, :, 0, :], ACT.Copy).then_inc(u_hi_ok, 1)
            for o in range(2):
                J0 = J_HY + 32 * o
                def y_heads(i):
                    act.wait_ge(y_f, i + (8 * o + 1))
                    act.wait_ge(cols_ok, 1)
                    for part in range(2):
                        ins = act.activation(y_s[part][:, ds(i, 1), 0, :].rearrange("p a c -> p (a c)"), ysum[:, part], ACT.Copy)
                    ins.then_inc(y_h, 1)

                def z_head(i):
                    act.wait_ge(z_ok, i + 1)
                    act.wait_ge(cols_ok, 1)
                    act.activation(u_s[:, ds(i, 1), 0, :].rearrange("p a c -> p (a c)"),
                                   tm[:, ds(i, 1), 0, :].rearrange("p a c -> p (a c)"), ACT.Copy).then_inc(u_hi_ok, 1)

                for J, between in ((J0, y_heads), (J0 + 16, z_head if o == 0 else None)):
                    split_next(0, J, 0)
                    split_next(0, J, 1)
                    first = 1
                    if J == J_HY:
                        for i in range(1, 6):
                            split_next(i, J, 0)
                            y_heads(i - 1)
                            if i >= 2:
                                channels_in(i)
                            split_next(i, J, 1)
                        first = 6
                    with act.Fori(first, 7 if between is None else 8) as i:
                        split_next(i, J, 0)
                        if between:
                            between(i - 1)
                        split_next(i, J, 1)
                    if between:
                        between(7)
            split_next(7, J_HY + 48, 0)

            for g in range(1, 16, 2):
                act.wait_ge(b_ps, g + 1)
                act.activation(bias[0:64, :, 0:14, 4 * g:4 * g + 4], bias_ps(g, 0), ACT.Copy)
                act.activation(bias[64:128, :, 0:14, 4 * g:4 * g + 4], bias_ps(g, 1), ACT.Copy).then_inc(b_eva, 1)
            act.wait_ge(b_evd, 8)
            act.wait_ge(b_eva, 8)
            act.activation(bias[64:128, :, 15:23, :], bias[64:128, :, 3:11, :], ACT.Copy).then_inc(b_eva, 1)
            with act.Fori(0, 4) as hp:
                act.wait_ge(st_free, hp + 1)
                act.wait_ge(cols_ok, 1)
                act.activation(vst[:], p_kv[:, ds(hp + 4, 1), :].rearrange("p a n -> p (a n)"), ACT.Copy).then_inc(vst_ok, 1)
                act.activation(kh[:], p_kv[:, ds(hp, 1), :].rearrange("p a n -> p (a n)"), ACT.Copy)
                act.activation(qh[:], p_q[:, ds(hp, 1), :].rearrange("p a n -> p (a n)"), ACT.Copy).then_inc(kh_ok, 1)
                act.wait_ge(v_tp, hp + 1)
                act.activation(vtm[:, 4:8, :], ps[:, 5, :].rearrange("p (a b) -> p a b", b=P), ACT.Copy)
                act.activation(vtm[:, 8:10, :], ps[:, 6, 0:256].rearrange("p (a b) -> p a b", b=P), ACT.Copy).then_inc(v_ev, 1)
                for s in range(17):
                    if s < 16:
                        L = UNITS[s // 2][2] * GRID_W
                        act.wait_ge(mx_ok, hp * 16 + (s + 1))
                        act.activation(pr[:, s % 2, 0:L], pr[:, s % 2, 0:L], ACT.Exp,
                                       bias=amax[:, s % 2, 2:3], accum_out=asum[:, s % 2, 0:1])
                        act.activation(pr[:, s % 2, L:L + CTX], s_all(s)[:, L:L + CTX], ACT.Exp,
                                       bias=amax[:, s % 2, 2:3], accum_out=asum[:, s % 2, 1:2]).then_inc(exp_ok, 1)
                    if s >= 1:
                        u = s - 1
                        if u >= 2:
                            act.wait_ge(pv_done, hp * 16 + (u - 1))
                        act.wait_ge(t_done, hp * 16 + (u + 1))
                        act.activation(pT[:, u % 2, 0:4, :], ps[:, 4 + u % 2, :].rearrange("p (a b) -> p a b", b=P), ACT.Copy)
                        ins = act.activation(pT[:, u % 2, 4:6, :], ps[:, 6, 0:256].rearrange("p (a b) -> p a b", b=P), ACT.Copy)
                        if UNITS[u // 2][2] > WIN_R:
                            ins = act.activation(pT[0:64, u % 2, 6, :], ps[0:64, 6, 256:384], ACT.Copy)
                        ins.then_inc(pt_a, 1)

            act.wait_ge(ot_free, 34)
            def mix_heads(h, hi):
                for k in range(KT):
                    act.activation(hi[:, k, :], mix_src(k, h), ACT.Copy).then_inc(m_hi, 1)

            def evac_out(j):
                act.wait_ge(job_done, J_OUT + j + 1)
                act.activation(yo[j // 8][:, j % 8, :], ps[:, j % 2, :], ACT.Copy).then_inc(acc_free, 1)

            def root(N):
                act.wait_ge(n_var, N + 1)
                act.activation(nrm[:], nrm[:], ACT.Sqrt).then_inc(n_sqrt, 1)

            def h2_heads(h, ks):
                for k in ks:
                    act.wait_ge(n_h, KT * h + k + 1)
                    act.activation(hb_hi[:, k, :], sq[:, k % 2, :], ACT.Copy).then_inc(n_hh, 1)

            def x1_squares(ks):
                for k in ks:
                    act.wait_ge(n_x1, k + 1)
                    act.activation(x1sq[:, k, :], x1[:, k, HS[0]], ACT.Square).then_inc(n_sq, 1)

            mix_heads(0, hb_hi)
            head_of(J_OUT)
            head_of(J_OUT + 1)
            for j in range(8):
                evac_out(j)
                head_of(J_OUT + j + 2)
                if j == 1:
                    mix_heads(1, hb3_hi)
            root(0)
            between = {1: lambda: x1_squares(range(3)), 2: lambda: x1_squares(range(3, 6)),
                       3: lambda: x1_squares(range(6, 8)), 4: lambda: root(1), 5: lambda: h2_heads(0, range(1)),
                       6: lambda: h2_heads(0, range(1, 4)), 7: lambda: h2_heads(0, range(4, 8))}
            for j in range(8):
                evac_out(8 + j)
                if j < 7:
                    head_of(J_OUT + 8 + j + 2)
                if j in between:
                    between[j]()

            for h in range(2):
                J0 = J_FFN + h * (GU_JOBS + DOWN_JOBS)

                def gu_tile(i, mid=None):
                    split_next(i, J0, 0)
                    if mid:
                        mid()
                    act.wait_ge(job_done, i * 2 + (J0 + 1))
                    act.activation(g_t[:], ps[:, 0, :], ACT.Tanh, scale=0.5).then_inc(g_tanh, 1)
                    split_next(i, J0, 1)
                    act.wait_ge(g_a, i + (FT * h + 1))
                    act.wait_ge(cols_ok, 1)
                    act.activation(a_hi[:, ds(i, 1), :].rearrange("p a c -> p (a c)"), a_f[:], ACT.Copy).then_inc(g_ah, 1)

                for i in range(4):
                    gu_tile(i, (lambda: root(2)) if (h, i) == (0, 1) else (lambda: root(4)) if (h, i) == (1, 0) else None)
                with act.Fori(4, FT) as i:
                    gu_tile(i)
                J0 += GU_JOBS
                if h == 0:
                    for i in range(4):
                        for q in range(6):
                            head_of(J0 + 6 * i + q + 1)
                            if i == q == 0:
                                root(3)
                            if q % 3 == 1:
                                h2_heads(1, range(2 * i + q // 3, 2 * i + q // 3 + 1))
                else:
                    with act.Fori(0, 3) as i:
                        for q in range(6):
                            split(i * 6 + (J0 + q + 1), i * 3 + (J0 // 2 + (q + 1) // 2), (q + 1) % 2)
                    for q in range(5):
                        head_of(18 + J0 + q + 1)
            root(5)
            for q in range(2, 4):
                act.wait_ge(o_tp, 4 + q + 1)
                act.activation(ost[:, q, :], ps[:, 2 * q:2 * q + 2, :].rearrange("p a b -> p (a b)"), ACT.Copy).then_inc(o_ea, 1)

        @block.gpsimd
        def _(pool):
            def rest(i, J0, b):
                pool.wait_ge(hi_done, i * 2 + (J0 + b + 1))
                pool.tensor_tensor(w_lo[:, b, :], raw[:, b, :], w_hi[:, b, :].bitcast(F32), ALU.subtract).then_inc(lo_done, 1)

            def rests(n, J0):
                with pool.Fori(0, n // 2) as i:
                    for b in range(2):
                        rest(i, J0, b)

            for t in range(KT):
                pool.wait_ge(k_hi, t + 1)
                pool.tensor_tensor(e_lo[:, t, :], eo[:, 0].rearrange("p a b -> p (a b)"), e_hi[:, t, :].bitcast(F32), ALU.subtract)
                pool.tensor_tensor(o_lo[:, t, :], eo[:, 1].rearrange("p a b -> p (a b)"), o_hi[:, t, :].bitcast(F32),
                                   ALU.subtract).then_inc(k_lo, 1)
            rests(16, J_K)

            def rest_of(J):
                rest(0, J - J % 2, J % 2)

            def tile_rest(n, blk, t):
                pool.wait_ge(x_hi, n + 1)
                hi, lo = HB[blk]
                pool.tensor_tensor(lo[:, :, t * P:(t + 1) * P], xmod[:, n % 2, :].rearrange("p (k n) -> p k n", n=P),
                                   hi[:, :, t * P:(t + 1) * P].bitcast(F32), ALU.subtract).then_inc(x_lo, 1)

            rest_of(J_CTX)
            tile_rest(0, 0, 0)
            tile_rest(1, 0, 1)
            for t in range(4):
                rest_of(J_CTX + 2 * t + 1)
                rest_of(J_CTX + 2 * t + 2)
                tile_rest(2 + t, 1, t)
            rest_of(J_CTX + 9)
            rest_of(J_LAT)
            for t in range(4):
                for m in range(1, 5):
                    if m == 3:
                        tile_rest(6 + t, 2, t)
                    rest_of(J_LAT + 4 * t + m)
            pool.memset(l_w[:], 0.0).then_inc(l_zero, 1)
            rest_of(J_LAT + 17)
            with pool.Fori(9, 22) as i:
                for b in range(2):
                    rest(i, J_LAT, b)
            for p in range(4):
                rests(16, J_HY + 16 * p)
            pool.wait_ge(y_h, 16)
            pool.wait_ge(z_tp, 2)
            pool.memset(bias[0:64, :, 22:23, :], NEG)
            pool.memset(bias[64:128, :, 14:15, :], NEG).then_inc(b_ok, 1)
            def mix_rests(h, ks, hi, lo):
                for k in ks:
                    pool.wait_ge(m_hi, KT * h + k + 1)
                    pool.tensor_tensor(lo[:, k, :], mix_src(k, h), hi[:, k, :].bitcast(F32), ALU.subtract).then_inc(m_lo, 1)

            def h2_rests(h, ks):
                for k in ks:
                    pool.wait_ge(n_hh, KT * h + k + 1)
                    pool.tensor_tensor(hb_lo[:, k, :], sq[:, k % 2, :], hb_hi[:, k, :].bitcast(F32), ALU.subtract).then_inc(n_hl, 1)

            mix_rests(0, range(5, 8), hb_hi, hb_lo)
            rest_of(J_OUT)
            for j in range(1, 16):
                rest_of(J_OUT + j)
                if j in (3, 4):
                    mix_rests(1, range(4 * (j - 3), 4 * (j - 3) + 4), hb3_hi, hb3_lo)
            h2_rests(0, range(1))
            rest_of(J_FFN)
            h2_rests(0, range(1, 8))
            for h in range(2):
                J0 = J_FFN + h * (GU_JOBS + DOWN_JOBS)
                with pool.Fori(0, FT) as i:
                    rest(i, J0, 1)
                    rest(i, J0 + 2, 0)
                J0 += GU_JOBS
                if h == 0:
                    for i in range(4):
                        for q in range(6):
                            rest_of(J0 + 6 * i + q + 1)
                            if q % 3 == 1:
                                h2_rests(1, range(2 * i + q // 3, 2 * i + q // 3 + 1))
                else:
                    with pool.Fori(0, 11) as i:
                        rest(i, J0, 1)
                        rest(i, J0 + 2, 0)
                    rest_of(J0 + 23)

        @block.vector
        def _(dve):
            class Chain:

                def __init__(self):
                    self.n, self.i, self.per = 0, None, 0

                def __call__(self, ins):
                    ins.then_inc(dchain, 1)
                    self.n += 1
                    dve.wait_ge(dchain, self.n if self.i is None else self.i * self.per + self.n)

                def loop(self, i, per):
                    self.i, self.per, self.start = i, per, self.n

                def end(self, times):
                    assert self.n - self.start == self.per, (self.n - self.start, self.per)
                    self.n, self.i = self.start + self.per * times, None

            link = Chain()

            def evac(i, J, dst, scale=1.0):
                dve.wait_ge(job_done, J + 1)
                dve.tensor_scalar(dst, i, scale, None, ALU.mult).then_inc(acc_free, 1)

            for _ in range(2):
                dve.nop().then_inc(acc_free, 1)
                dve.nop().then_inc(inv_free, 1)
                dve.nop().then_inc(dn_free, 1)
                dve.nop().then_inc(mod_done, 1)
                dve.nop().then_inc(ks_out[_], 16)
                dve.nop().then_inc(ot_free, 1)
            dve.nop().then_inc(modp, 1)
            dve.nop().then_inc(st_free, 1)

            dve.wait_ge(cols_ps, 1)
            dve.tensor_copy(colA[:], ps[:, 2, 0:96])
            dve.tensor_copy(colB[:, 0:46], ps[:, 2, 96:142])
            dve.tensor_copy(colC[0:64, :], ps[0:64, 2, 142:146]).then_inc(cols_ok, 1)
            dve.wait_ge(cols_ok, 1)
            dve.wait_ge(silt_ok, 1)
            link(dve.scalar_tensor_tensor(sil_t[:], sil_t[:], 1.0, colA[:, 80:96], ALU.add, ALU.mult))
            dve.tensor_scalar(sil[:].rearrange("p a b -> p (a b)"), sil_t[:], 0.5, None, ALU.mult).then_inc(sil_ok, 1)

            for layer in range(2):
                dve.wait_ge(f_ps, layer + 1)
                z = ps[0:64, 4 + 2 * layer:6 + 2 * layer, :].rearrange("p a b -> p (a b)")
                if layer == 1:
                    dve.wait_ge(f_sin, 1)
                link(dve.tensor_scalar(farg[0:64, :], z, colC[0:64, layer:layer + 1], colC[0:64, 2 + layer:3 + layer],
                                       ALU.add, ALU.mult))
                link(dve.tensor_scalar(fturn[0:64, :], farg[0:64, :], 1.0 / (2 * math.pi), MAGIC, ALU.mult, ALU.add))
                link(dve.tensor_scalar(fturn[0:64, :], fturn[0:64, :], MAGIC, None, ALU.subtract))
                for part in (TWO_PI_HEAD, TWO_PI_REST):
                    link(dve.scalar_tensor_tensor(farg[0:64, :], fturn[0:64, :], -part, farg[0:64, :], ALU.mult, ALU.add))
                dve.tensor_scalar(farg[0:64, :], farg[0:64, :], 3.1415925, -3.1415925, ALU.min, ALU.max).then_inc(f_arg, 1)

            dve.wait_ge(dec_ld, 16)
            for t in range(KT):
                s = t % 2
                dve.wait_ge(k_ps, t + 1)
                if t >= 2:
                    dve.wait_ge(k_abs, t - 1)
                for o in range(2):
                    link(dve.tensor_tensor(kt_[:, s, o], ps[:, 4 + 2 * s + o, :].rearrange("p (a b) -> p a b", a=2),
                                           dec[:, t:t + 1, :].broadcast_to([P, 2, HY]), ALU.mult))
                if t == 0:
                    link(dve.memset(kt_[0:1, s, :, 1, :], 0.0))
                dve.nop().then_inc(k_dec, 1)
                if t >= 1:
                    dve.wait_ge(k_hi, t)
                    dve.wait_ge(k_lo, t)
                dve.tensor_tensor(eo[:, 0], kt_[:, s, :, 0, :], kt_[:, s, :, 1, :], ALU.add)
                dve.tensor_tensor(eo[:, 1], kt_[:, s, :, 0, :], kt_[:, s, :, 1, :], ALU.subtract).then_inc(k_eo, 1)
            dve.wait_ge(k_sum, KT)
            dve.tensor_copy(inv_t[:, 0], ps[:, 2, 0:HY])
            link(dve.tensor_copy(inv_t[:, 1], ps[:, 3, 0:HY]))
            for o in range(2):
                link(dve.tensor_tensor(inv_t[:, o], inv_t[:, o], ps[:, 2 + o, HY:2 * HY], ALU.add))
            link(dve.tensor_scalar(inv_t[:], inv_t[:], float(SEQ), None, ALU.mult))
            link(dve.reciprocal(inv[:], inv_t[:]))
            def mod_products(tile, prod, cond):
                return dve.tensor_tensor(prod[:].rearrange("p (k n) -> p k n", n=P), tile.rearrange("p (k n) -> p k n", n=P),
                                         sil[:, cond, :].unsqueeze(2).broadcast_to([P, KT, P]), ALU.mult)

            def mod_reduce(prod, acc):
                return dve.tensor_reduce(acc, prod[:].rearrange("p (k n) -> p n k", n=P), axis=AX, op=ALU.add)

            dve.wait_ge(x_sq, 10)
            dve.tensor_scalar(rx[:], ssq[:], 1.0 / D, EPS, ALU.mult, ALU.add).then_inc(x_rs, 1)
            with dve.Fori(0, 4) as i:
                link.loop(i, 16)
                for q in range(4):
                    b = q % 2
                    dve.wait_ge(ks_out[b], i * 32 + 16 * (q // 2 + 1))
                    dve.wait_ge(job_done, i * 4 + (J_K + q + 1))
                    dve.tensor_tensor(kev[:, b], ps[:, b, :].rearrange("p (a c) -> p a c", a=2), inv[:], ALU.mult).then_inc(acc_free, 1)
                    dve.wait_ge(mix_ld[q], i * 16 + 16)
                    dve.wait_ge(mod_done, i * 4 + (q + 1))
                    for cond in range(2):
                        link(mod_products(ada0[:, q, :], mprod, cond))
                        link(mod_reduce(mprod, macc[:, b, cond, :]))
                    dve.nop().then_inc(mod_rd, 1)
            link.end(4)
            dve.wait_ge(mod_done, 18)
            link(dve.tensor_tensor(mod[:, 0:16, :], ps[:, 7, 0:32].rearrange("p (a b) -> p a b", b=2),
                                   colA[:, 32:48].unsqueeze(2).broadcast_to([P, 16, 2]), ALU.add))
            link(dve.tensor_scalar(amix[:], mod[:, 8:16, :], 1.0, None, ALU.add))
            link(dve.tensor_tensor(amix[:], amix[:], colA[:, 0:8].unsqueeze(2).broadcast_to([P, KT, 2]), ALU.mult))

            def SPANS(h):
                hs = HS[h]
                lat = slice(CTX + hs.start, CTX + hs.stop)
                flat = lambda ap: ap.rearrange("p a n -> p (a n)")
                return ((18, 20, lambda t: flat(p_kv[:, ds(t + 8, 1), lat]), 1.0),
                        (20, 22, lambda t: flat(p_xg[:, ds(t, 1), hs]), 1.0),
                        (0, 6, lambda t: flat(p_hy[:, ds(t, 1), hs]), 1.0),
                        (6, 10, lambda t: flat(p_q[:, ds(t, 1), hs]), DH ** -0.5),
                        (10, 18, lambda t: flat(p_kv[:, ds(t, 1), lat]), 1.0))

            dve.wait_ge(x_sqrt, 1)
            link(dve.reciprocal(rx[:], rx[:]))

            def normalise(n):
                dve.wait_ge(x_ld[n % 2], 16 * (n // 2 + 1))
                dve.tensor_scalar(xin[:, n % 2, :], xin[:, n % 2, :], rx[:, n:n + 1], None, ALU.mult).then_inc(x_n, 1)

            def modulate(n):
                cond = 1 if n < 2 else 0
                if n >= 2:
                    dve.wait_ge(x_lo, n - 1)
                dve.wait_ge(x_tp, n + 1)
                bank = 2 + 2 * (n % 2)
                src = ps[:, bank:bank + 2, :].rearrange("p a (k n) -> p (a k) n", n=P)
                x3 = xmod[:, n % 2, :].rearrange("p (k n) -> p k n", n=P)
                col = lambda v: v.broadcast_to([P, KT, P])
                link(dve.tensor_tensor(x3, src, col(amix[:, :, cond:cond + 1]), ALU.mult))
                dve.tensor_tensor(x3, x3, col(mod[:, 0:8, cond:cond + 1]), ALU.add).then_inc(x_mod, 1)

            def evac_span(J0, a, z):
                for f0, f1, dst, scale in SPANS(0):
                    j0 = (f0 + 4) % 22
                    lo, hi = max(a, j0), min(z, j0 + f1 - f0)
                    for j in range(lo, hi):
                        evac(ps[:, j % 2, :], J0 + j, dst(j - j0), scale)

            normalise(0)
            normalise(1)
            modulate(0)
            modulate(1)
            normalise(2)
            for t in range(5):
                for b in range(2):
                    evac(ps[:, b, 0:CTX], J_CTX + 2 * t + b, p_kv[:, 2 * t + b, 0:CTX])
                if t < 4:
                    modulate(2 + t)
                    normalise(3 + t)
            x_, e_, two_sp, mlam, z_, z2, poly = (lam[:, r, :] for r in (0, 1, 2, 3, 4, 5, 6))
            link(dve.tensor_scalar(mlam, colB[:, 42:46], -1.0, None, ALU.mult))
            link(dve.scalar_tensor_tensor(x_, mlam, -1.0, mlam, ALU.mult, ALU.max))
            dve.nop().then_inc(lam_d, 1)
            dve.wait_ge(lam_a, 1)
            link(dve.tensor_scalar(z_, e_, 2.0, None, ALU.add))
            link(dve.reciprocal(z_, z_))
            link(dve.tensor_tensor(z_, z_, e_, ALU.mult))
            link(dve.tensor_tensor(z2, z_, z_, ALU.mult))
            link(dve.tensor_scalar(poly, z2, 1.0 / 19, 1.0 / 17, ALU.mult, ALU.add))
            for k in (15, 13, 11, 9, 7, 5, 3, 1):
                link(dve.tensor_tensor(poly, poly, z2, ALU.mult))
                link(dve.tensor_scalar(poly, poly, 1.0 / k, None, ALU.add))
            link(dve.tensor_tensor(poly, poly, z_, ALU.mult))
            link(dve.tensor_scalar(two_sp, mlam, 0.0, 2.0, ALU.max, ALU.mult))
            link(dve.scalar_tensor_tensor(two_sp, poly, 4.0, two_sp, ALU.mult, ALU.add))
            link(dve.tensor_scalar(lam[:, 7, :], two_sp, -2.0, None, ALU.mult))
            dve.tensor_scalar(hbias[:], colB[:, 34:42], 0.5, None, ALU.mult).then_inc(lam_d, 1)
            for t in range(4):
                evac_span(J_LAT, 4 * t, 4 * t + 2)
                modulate(6 + t)
                if t < 3:
                    normalise(7 + t)
                evac_span(J_LAT, 4 * t + 2, 4 * t + 4)
            evac_span(J_LAT, 16, 22)

            J0 = J_LAT + 22
            jobs1 = iter([(j, dst, scale) for a, z, dst, scale in SPANS(1) for j in [None]
                          for j, dst, scale in [((a + 4) % 22 + t, (lambda t=t, dst=dst: dst(t)), scale) for t in range(z - a)]])
            count1 = [0]

            def evac_to(n):
                while count1[0] < n:
                    j, dst, scale = next(jobs1)
                    evac(ps[:, j % 2, :], J0 + j, dst(), scale)
                    count1[0] += 1

            evac_to(4)
            dve.wait_ge(x_lo, 10)
            for b in range(2):
                dve.wait_ge(ks_out[b], 144)
            for c in range(2):
                xr = p_kv[:, 8 + c, :]
                w = lambda k: colB[:, 24 + 2 * k + c:25 + 2 * k + c]
                link(dve.tensor_scalar(l_u[:], xr, w(2), colB[:, 32 + c:33 + c], ALU.mult, ALU.add))
                for k, sh in ((0, -2), (1, -1), (3, 1)):
                    for a, z in ((0, CTX), (CTX, ALL)):
                        lo, hi = (a - sh, z) if sh < 0 else (a, z - sh)
                        ins = dve.scalar_tensor_tensor(l_u[:, lo:hi], xr[:, lo + sh:hi + sh], w(k), l_u[:, lo:hi],
                                                       ALU.mult, ALU.add)
                        link(ins)
                    if c == 0:
                        evac_to(min(count1[0] + 1, 4 + 2 * LRU_AFTER[0]))
                dve.nop().then_inc(l_conv, 1)
                xg, inner = p_xg[:, c, :], l_q[:, 0:SEQ]
                link(dve.tensor_tensor(inner, xg, xg, ALU.mult))
                link(dve.tensor_scalar(inner, inner, 0.044715, 1.0, ALU.mult, ALU.add))
                dve.tensor_tensor(inner, inner, xg, ALU.mult).then_inc(l_dve, 1)
                for d in range(2):
                    q = c * 2 + d
                    evac_to(4 + 2 * LRU_AFTER[q])
                    later = iter(range(4 + 2 * LRU_AFTER[q] + 1, 4 + 2 * (LRU_AFTER[q + 1] if q < 3 else 9) + 1))
                    more = lambda: evac_to(next(later, 0))
                    dve.wait_ge(l_act, 5 * c + 2 * d + 3)
                    link(dve.scalar_tensor_tensor(l_i[:], l_i[:], 1.0, l_u[:], ALU.add, ALU.mult))
                    more()
                    link(dve.scalar_tensor_tensor(l_i[:], l_a[:], 1.0, l_i[:], ALU.add, ALU.mult))
                    link(dve.tensor_tensor(l_i[:], l_i[:], l_r[:], ALU.mult))
                    more()
                    if d == 0:
                        link(dve.tensor_tensor_scan(l_h[:, 0, :], l_a[:], l_i[:], 0.0, ALU.mult, ALU.add))
                    else:
                        link(dve.tensor_tensor_scan(l_h[:, 1, 0:CTX][:, ::-1], l_a[:, 0:CTX][:, ::-1],
                                                    l_i[:, 0:CTX][:, ::-1], 0.0, ALU.mult, ALU.add))
                        link(dve.tensor_tensor_scan(l_h[:, 1, CTX:ALL][:, ::-1], l_a[:, CTX:ALL][:, ::-1],
                                                    l_i[:, CTX:ALL][:, ::-1], l_h[:, 1, 0:1], ALU.mult, ALU.add))
                        more()
                        hsum = l_a[:, 0:SEQ]
                        link(dve.tensor_tensor(hsum, l_h[:, 0, CTX:ALL], l_h[:, 1, CTX:ALL], ALU.add))
                        link(dve.scalar_tensor_tensor(inner, inner, 1.0, xg, ALU.add, ALU.mult))
                        link(dve.scalar_tensor_tensor(xg, inner, 0.5, hsum, ALU.mult, ALU.mult))
                    dve.nop().then_inc(l_done, 1)
            evac_to(22)

            def short_conv(c):
                x, y = p_hy[:, c, :], conv[:, c % 2, :]
                w = lambda k: colB[:, 6 * k + c:6 * k + c + 1]
                if c >= 2:
                    dve.wait_ge(c_tp, c - 1)
                link(dve.tensor_scalar(y, x, w(1), colB[:, 18 + c:19 + c], ALU.mult, ALU.add))
                link(dve.scalar_tensor_tensor(y[:, 1:SEQ], x[:, 0:SEQ - 1], w(0), y[:, 1:SEQ], ALU.mult, ALU.add))
                link(dve.scalar_tensor_tensor(y[:, 0:SEQ - 1], x[:, 1:SEQ], w(2), y[:, 0:SEQ - 1], ALU.mult, ALU.add))
                dve.nop().then_inc(c_ok, 1)

            short_conv(0)
            short_conv(1)
            dve.wait_ge(u_hi_ok, 1)
            dve.tensor_tensor(u_s[:, :, 1, :], tm[:, :, 0, :], u_s[:, :, 0, :].bitcast(F32), ALU.subtract).then_inc(u_lo_ok, 1)
            for o in range(2):
                J0, E0 = J_HY + 32 * o, E_FWD + 16 * o
                dve.wait_ge(kspec_ld, 16 * (o + 1))
                def filter_tile(i):
                    k1 = kspec[:, ds(i, 1), :, :].rearrange("p m a c -> p (m a) c")

                    def transform(b, t):
                        dve.wait_ge(job_done, i * 2 + (J0 + b + 1))
                        link(dve.tensor_copy(t, ps[:, b, HY:2 * HY]))
                        link(dve.tensor_tensor(t, ps[:, b, 0:HY], t, ALU.add))
                        dve.nop().then_inc(acc_free, 1)
                        return t.unsqueeze(1).broadcast_to([P, 2, HY])

                    dve.tensor_tensor(prodA[:], transform(0, zb[:]), k1, ALU.mult)
                    link(dve.tensor_tensor(prodB[:, ::-1, :], transform(1, zs[:]), k1, ALU.mult))
                    dve.tensor_tensor(ysum[:, 0], prodA[:, 0], prodB[:, 0], ALU.subtract)
                    dve.tensor_tensor(ysum[:, 1], prodA[:, 1], prodB[:, 1], ALU.add).then_inc(y_f, 1)
                    dve.wait_ge(y_h, i + (8 * o + 1))
                    for part in range(2):
                        ins = dve.tensor_tensor(y_s[part][:, ds(i, 1), 1, :].rearrange("p a c -> p (a c)"), ysum[:, part],
                                                y_s[part][:, ds(i, 1), 0, :].bitcast(F32).rearrange("p a c -> p (a c)"), ALU.subtract)
                    link(ins)
                    dve.nop().then_inc(y_l, 1)
                if o == 0:
                    for i in range(4):
                        filter_tile(i)
                        short_conv(2 + i)
                with dve.Fori(4 * (1 - o), 8) as i:
                    link.loop(i - 4 * (1 - o), 6)
                    filter_tile(i)
                link.end(4 + 4 * o)
                if o == 0:
                    dve.wait_ge(c_ev, 6)
                    dve.wait_ge(hyb_ld, 16)
                with dve.Fori(0, 4) as i:
                    link.loop(i, 8 if o == 0 else 6)
                    for tp in range(2):
                        T = i * 2 + tp
                        row = lambda part: tm[:, ds(T, 1), part, :].rearrange("p a c -> p (a c)")
                        link(dve.tensor_tensor(zb[:], row(0), hyb[:, o], ALU.mult))
                        dve.wait_ge(job_done, i * 4 + (J0 + 16 + 2 * tp + 2))
                        link(dve.tensor_tensor(zb[:], ps[:, 2 + tp, HY:2 * HY], zb[:], ALU.add))
                        link(dve.tensor_tensor(zs[:], ps[:, 2 + tp, 0:HY], zb[:], ALU.add))
                        dve.nop().then_inc(inv_free, 1)
                        dve.tensor_tensor(row(0), zs[:], row(1 + o), ALU.mult).then_inc(z_ok, 1)
                        dve.wait_ge(z_ok, T + (8 * o + 1))
                        if o == 0:
                            dve.wait_ge(u_hi_ok, T + 2)
                            link(dve.tensor_tensor(u_s[:, ds(T, 1), 1, :].rearrange("p a c -> p (a c)"), row(0),
                                                   u_s[:, ds(T, 1), 0, :].bitcast(F32).rearrange("p a c -> p (a c)"),
                                                   ALU.subtract))
                            dve.nop().then_inc(u_lo_ok, 1)
                link.end(4)
            link(dve.memset(rpbt[0:32, :], NEG))
            dve.wait_ge(rp_tp, 1)
            dve.tensor_copy(rpbt[0:31, :], ps[0:31, 2, 0:120]).then_inc(rp_ok, 1)
            for c in range(2):
                dve.wait_ge(z_tp, c + 1)
                dve.tensor_copy(mix_hy[:, c, :], ps[:, 4 + 2 * c:6 + 2 * c, :].rearrange("p a b -> p (a b)")).then_inc(z_ev, 1)

            for g in range(0, 16, 2):
                dve.wait_ge(b_ps, g + 1)
                dve.tensor_copy(bias[0:64, :, 0:14, 4 * g:4 * g + 4], bias_ps(g, 0))
                dve.tensor_copy(bias[64:128, :, 0:14, 4 * g:4 * g + 4], bias_ps(g, 1)).then_inc(b_evd, 1)
            dve.wait_ge(b_evd, 8)
            dve.wait_ge(b_eva, 8)
            link(dve.tensor_copy(bias[0:64, :, 14:22, :], bias[0:64, :, 2:10, :]))
            dve.wait_ge(b_eva, 9)
            dve.wait_ge(b_ok, 1)
            with dve.Fori(0, 4) as hp:
                link.loop(hp, 58)
                for e in range(2):
                    ins = dve.tensor_scalar(bst[e][:].rearrange("p a b -> p (a b)"),
                                            bias[:].rearrange("p h a b -> p h (a b)")[:, ds(hp * 2 + e, 1), :].rearrange("p o n -> p (o n)"),
                                            1.0, None, ALU.mult)
                link(ins)
                dve.wait_ge(kh_ok, hp + 1)
                dve.tensor_tensor(kl[:], p_kv[:, ds(hp, 1), :].rearrange("p a n -> p (a n)"), kh[:].bitcast(F32), ALU.subtract)
                link(dve.tensor_tensor(ql[:], p_q[:, ds(hp, 1), :].rearrange("p a n -> p (a n)"), qh[:].bitcast(F32), ALU.subtract))
                dve.nop().then_inc(st_ok, 1)
                dve.wait_ge(v_tp, hp + 1)
                dve.tensor_copy(vtm[:, 0:4, :], ps[:, 4, :].rearrange("p (a b) -> p a b", b=P)).then_inc(v_ev, 1)
                for s in range(19):
                    if 1 <= s <= 16:
                        u, e = s - 1, (s - 1) % 2
                        n = UNITS[u // 2][2] * GRID_W + CTX
                        dve.wait_ge(exp_ok, hp * 16 + (u + 1))
                        link(dve.tensor_tensor(asum[:, e, 2:3], asum[:, e, 0:1], asum[:, e, 1:2], ALU.add))
                        link(dve.reciprocal(asum[:, e, 3:4], asum[:, e, 2:3]))
                        dve.tensor_scalar(pr[:, e, 0:n], pr[:, e, 0:n], asum[:, e, 3:4], None, ALU.mult).then_inc(nrm_ok, 1)
                    if s >= 4 and s % 2 == 0:
                        qt = (s - 4) // 2
                        dve.wait_ge(pv_done, hp * 16 + (2 * qt + 2))
                        dve.tensor_scalar(p_q[:, ds(hp, 1), qt * P:(qt + 1) * P].rearrange("p a n -> p (a n)"),
                                          ps[:, 7, (qt % 2) * P:(qt % 2 + 1) * P], 1.0, None, ALU.mult).then_inc(ot_free, 1)
                    if s < 16:
                        _, _, kr, slot0 = UNITS[s // 2]
                        L, e = kr * GRID_W, s % 2
                        if s >= 2:
                            dve.wait_ge(t_done, hp * 16 + (s - 1))
                        dve.wait_ge(qk_done, hp * 16 + (s + 1))
                        dve.tensor_reduce(amax[:, e, 1:2], s_all(s)[:, L:L + CTX], axis=AX, op=ALU.max)
                        link(dve.tensor_tensor_reduce(out=pr[:, e, 0:L], in0=s_all(s)[:, 0:L],
                                                      in1=bst[e][:, slot0:slot0 + kr, :].rearrange("p a b -> p (a b)"),
                                                      scale=1.0, scalar=-3.0e38, op0=ALU.add, op1=ALU.max,
                                                      accum_out=amax[:, e, 0:1]))
                        dve.tensor_scalar(amax[:, e, 2:3], amax[:, e, 0:1], amax[:, e, 1:2], -1.0,
                                          ALU.max, ALU.mult).then_inc(mx_ok, 1)
                        if s == 15:
                            dve.nop().then_inc(st_free, 1)
                    if s % 2 == 1 and s < 16:
                        j = s // 2
                        dve.wait_ge(ada_ld[j % 2], hp * 64 + 16 * (j // 2 + 1))
                        link(mod_products(ada1[:, j % 2, :], mprod1, 0))
                    elif 2 <= s <= 16:
                        j = s // 2 - 1
                        if j >= 2:
                            dve.wait_ge(mod_done, hp * 8 + (16 + 2 + j - 1))
                        mod_reduce(mprod1, macc1[:, j % 2, :]).then_inc(mod_rd, 1)
                        dve.wait_ge(mod_rd, hp * 8 + (16 + j + 1))
                        dve.nop().then_inc(macc_ok, 1)
                link.end(4)
                dve.wait_ge(mod_done, hp * 8 + 26)
                dve.tensor_tensor(mod[:, ds(hp * 8 + 16, 8), 0], ps[:, 7, 384:392], colA[:, ds(hp * 8 + 48, 8)], ALU.add).then_inc(modp, 1)

            dve.wait_ge(modp, 5)
            link(dve.tensor_tensor(gmix[:], mod[:, 16:24, 0], colA[:, 8:16], ALU.mult))
            link(dve.tensor_tensor(gffn[:], mod[:, 40:48, 0], colA[:, 24:32], ALU.mult))
            link(dve.scalar_tensor_tensor(affn[:], mod[:, 32:40, 0], 1.0, colA[:, 16:24], ALU.add, ALU.mult))
            for k in range(5):
                dve.wait_ge(m_hi, k + 1)
                dve.tensor_tensor(hb_lo[:, k, :], mix_src(k, 0), hb_hi[:, k, :].bitcast(F32), ALU.subtract).then_inc(m_ld, 1)

            def add_square(v, k, acc, tmp):
                link(dve.tensor_tensor(acc[:] if k == 0 else tmp[:], v, v, ALU.mult))
                if k:
                    link(dve.tensor_tensor(acc[:], acc[:], tmp[:], ALU.add))

            def rstd_of(N):
                dve.wait_ge(n_ps, N + 1)
                dve.tensor_scalar(nrm[:], ps[:, 6, :], 1.0 / D, EPS, ALU.mult, ALU.add).then_inc(n_var, 1)
                dve.wait_ge(n_sqrt, N + 1)
                link(dve.reciprocal(rstd[:], nrm[:]))

            def add_mixed(h, ks):
                for k in ks:
                    T = KT * h + k
                    link(dve.scalar_tensor_tensor(a_f[:], yo[h][:, k, :], gmix[:, k:k + 1], rstd[:], ALU.mult, ALU.mult))
                    dve.wait_ge(n_tp, T + 1)
                    dve.tensor_tensor(x1[:, k, HS[h]], a_f[:], ps[:, 2 + T % 4, :], ALU.add).then_inc(n_x1, 1)
                    dve.wait_ge(n_x1, T + 1)
                    if h == 1:
                        add_square(x1[:, k, HS[h]], k, nrm, a_f)

            def ffn_input(h, ks):
                for k in ks:
                    link(dve.scalar_tensor_tensor(a_f[:], x1[:, k, HS[h]], affn[:, k:k + 1], rstd[:], ALU.mult, ALU.mult))
                    if k >= 2:
                        dve.wait_ge(n_hl, KT * h + k - 1)
                    dve.tensor_scalar(sq[:, k % 2, :], a_f[:], mod[:, 24 + k, 0:1], None, ALU.add).then_inc(n_h, 1)
                    dve.wait_ge(n_h, KT * h + k + 1)

            def add_ffn(h, ks):
                for k in ks:
                    link(dve.scalar_tensor_tensor(a_f[:], yd[:, k, :], gffn[:, k:k + 1], rstd[:], ALU.mult, ALU.mult))
                    link(dve.tensor_tensor(x1[:, k, HS[h]], a_f[:], x1[:, k, HS[h]], ALU.add))
                    if h == 1:
                        dve.nop().then_inc(n_fin, 1)

            for k in range(KT):
                dve.wait_ge(acc_free, E_OUT + k + 3)
                add_square(yo[0][:, k, :], k, yacc, ysq)
            dve.nop().then_inc(n_sum, 1)
            dve.wait_ge(m_lo, 11)
            rstd_of(0)
            add_mixed(0, range(KT))
            for k in range(1, KT):
                dve.wait_ge(n_sq, k + 1)
                link(dve.tensor_tensor(nrm[:], x1sq[:, 0, :] if k == 1 else nrm[:], x1sq[:, k, :], ALU.add))
            dve.nop().then_inc(n_sum, 1)
            rstd_of(1)
            ffn_input(0, range(KT))

            for h in range(2):
                J0, E0 = J_FFN + h * (GU_JOBS + DOWN_JOBS), E_GU + h * GU_JOBS

                def gu_tile(i):
                    dve.wait_ge(g_tanh, i + (FT * h + 1))
                    dve.scalar_tensor_tensor(g_t[:], g_t[:], 1.0, ps[:, 0, :], ALU.add, ALU.mult).then_inc(acc_free, 1)
                    dve.wait_ge(acc_free, i * 2 + (E0 + 3))
                    dve.wait_ge(job_done, i * 2 + (J0 + 2))
                    dve.scalar_tensor_tensor(a_f[:], g_t[:], 0.5, ps[:, 1, :], ALU.mult, ALU.mult).then_inc(acc_free, 1)
                    dve.wait_ge(acc_free, i * 2 + (E0 + 4))
                    dve.nop().then_inc(g_a, 1)
                    dve.wait_ge(g_ah, i + (FT * h + 1))
                    link(dve.tensor_tensor(a_lo[:, ds(i, 1), :].rearrange("p a c -> p (a c)"), a_f[:],
                                           a_hi[:, ds(i, 1), :].bitcast(F32).rearrange("p a c -> p (a c)"), ALU.subtract))
                    dve.nop().then_inc(g_al, 1)

                if h == 0:
                    dve.wait_ge(n_hl, KT)
                    for k in range(KT):
                        dve.wait_ge(acc_free, E_OUT + KT + k + 3)
                        add_square(yo[1][:, k, :], k, nrm, a_f)
                    dve.nop().then_inc(n_sum, 1)
                    gu_tile(0)
                    rstd_of(2)
                    gu_tile(1)
                    add_mixed(1, range(0, 3))
                    gu_tile(2)
                    add_mixed(1, range(3, 6))
                    gu_tile(3)
                    add_mixed(1, range(6, 8))
                    dve.nop().then_inc(n_sum, 1)
                else:
                    rstd_of(4)
                    gu_tile(0)
                    add_ffn(0, range(0, 4))
                    gu_tile(1)
                    add_ffn(0, range(4, 8))
                    dve.nop().then_inc(n_fin, 1)
                    for q in range(4):
                        if q % 2 == 0:
                            gu_tile(2 + q // 2)
                        dve.wait_ge(o_tp, q + 1)
                        if q >= 2:
                            dve.wait_ge(st_out[q % 2], 16)
                        dve.tensor_copy(xin[:, q % 2, :],
                                        ps[:, 4 + 2 * (q % 2):6 + 2 * (q % 2), :].rearrange("p a b -> p (a b)")).then_inc(o_ev, 1)
                with dve.Fori(4, FT) as i:
                    link.loop(i - 4, 1)
                    gu_tile(i)
                link.end(FT - 4)
                J0 += GU_JOBS
                if h == 0:
                    rstd_of(3)
                else:
                    for b in range(2):
                        dve.wait_ge(st_out[b], 32)
                for k in range(KT):
                    if h == 0:
                        ffn_input(1, range(k, k + 1))
                    dve.wait_ge(job_done, J0 + 3 * k + 3)
                    dve.tensor_scalar(yd[:, k, :], ps[:, 2 + k % 2, :], 1.0, None, ALU.mult).then_inc(dn_free, 1)
                    dve.wait_ge(dn_free, 8 * h + k + 3)
                    add_square(yd[:, k, :], k, nrm, a_f)
                dve.nop().then_inc(n_sum, 1)
            rstd_of(5)
            add_ffn(1, range(KT))
            for q in range(2):
                dve.wait_ge(o_tp, 4 + q + 1)
                dve.tensor_copy(ost[:, q, :], ps[:, 2 * q:2 * q + 2, :].rearrange("p a b -> p (a b)")).then_inc(o_ev, 1)

        @block.tensor
        def _(pe):
            def product2(J, b, dst, rhs, start=True, stop=True, ready=None):
                for n, (w, split) in enumerate(((w_hi, hi_done), (w_lo, lo_done))):
                    pe.wait_ge(split, J + 1)
                    for k in range(KT):
                        if ready and n == 0:
                            ready(k)
                        ins = pe.matmul(dst, w[:, b, k * P:(k + 1) * P], rhs[:, k].rearrange("p a c -> p (a c)"),
                                        start=start and k == 0 and n == 0, stop=stop and k == KT - 1 and n == 1)
                ins.then_inc(job_done, 1)

            def product(J, b, dst, rhs, nk=KT, start=True, stop=True, between=None, ready=None):
                pe.wait_ge(hi_done, J + 1)
                for k in range(nk):
                    if ready:
                        ready(k)
                    for n, x in enumerate(rhs(k)):
                        pe.matmul(dst, w_hi[:, b, k * P:(k + 1) * P], x, start=start and k == 0 and n == 0, stop=False)
                if between:
                    between()
                pe.wait_ge(lo_done, J + 1)
                for k in range(nk):
                    ins = pe.matmul(dst, w_lo[:, b, k * P:(k + 1) * P], rhs(k)[0], start=False, stop=stop and k == nk - 1)
                ins.then_inc(job_done, 1)
                return ins

            npar = 2 + 7 + sum(A[n].shape[1] if len(A[n].shape) == 3 else 1 for n in
                               ("hy_conv_w", "hy_conv_b", "lru_conv_w", "lru_conv_b", "lru_ba", "lru_bi", "lru_lam")) + 3
            pe.wait_ge(par_ld, 16 * npar)
            pe.transpose(ps[:, 2, 0:96], rowsA[0:96, :], ident[0:96, 0:96])
            pe.transpose(ps[:, 2, 96:142], rowsB[0:46, :], ident[0:46, 0:46])
            pe.transpose(ps[0:64, 2, 142:146], rowsC[0:4, 0:64], ident[0:4, 0:4]).then_inc(cols_ps, 1)
            pe.wait_ge(flt_ld, 64)
            for j in range(2):
                ins = pe.matmul(ps[0:64, 4 + j, :], w12[0:33, 0, :], zf[0:33, j * 512:(j + 1) * 512], start=True, stop=True)
            ins.then_inc(f_ps, 1)
            pe.wait_ge(f_sin, 1)
            for j in range(2):
                ins = pe.matmul(ps[0:64, 6 + j, :], w12[0:64, 1, :], h1[0:64, j * 512:(j + 1) * 512], start=True, stop=True)
            ins.then_inc(f_ps, 1)
            pe.wait_ge(f_sin, 2)

            def taps(t):
                if t >= 2:
                    pe.wait_ge(k_dec, t - 1)
                for o in range(2):
                    ins = pe.matmul(ps[:, 4 + 2 * (t % 2) + o, :], h2f[0:64, t * P:(t + 1) * P],
                                    w3s[0:64, o * 512:(o + 1) * 512], start=True, stop=True)
                ins.then_inc(k_ps, 1)

            def magnitudes(t):
                pe.wait_ge(k_abs, t + 1)
                for o in range(2):
                    ins = pe.matmul(ps[:, 2 + o, :], ones[:], kabs[:, t % 2, o * 512:(o + 1) * 512], start=t == 0, stop=t == KT - 1)
                ins.then_inc(k_sum, 1)

            taps(0)
            for t in range(KT):
                if t + 1 < KT:
                    taps(t + 1)
                magnitudes(t)

            pe.wait_ge(k_dec, KT)
            pe.wait_ge(k_lo, KT)

            def spectra(i):
                for b, (hi, lo) in enumerate(((e_hi, e_lo), (o_hi, o_lo))):
                    pe.wait_ge(acc_free, i * 2 + (E_K + b + 1))
                    product(i * 2 + (J_K + b), b, ps[:, b, :], lambda k: (hi[:, k, :], lo[:, k, :]))

            def mod_sums(i):
                for b in range(2):
                    pe.wait_ge(mod_rd, i * 2 + (b + 1))
                    for cond in range(2):
                        ins = pe.matmul(ps[:, 7, ds(i * 4 + (2 * b + cond), 1)], macc[:, b, cond, :], ones[:, 0:1], start=True, stop=True)
                    ins.then_inc(mod_done, 1)

            spectra(0)
            with pe.Fori(1, 8) as i:
                spectra(i)
                mod_sums(i - 1)
            mod_sums(7)

            def turn_tile(n, s):
                pe.wait_ge(x_n, n + 1)
                for k in range(KT):
                    ins = pe.transpose(ps[:, 2 + 2 * s + k // 4, (k % 4) * P:(k % 4 + 1) * P], xin[:, s, k * P:(k + 1) * P], ident[:])
                ins.then_inc(x_tp, 1)

            def job_pair(i, J0, blk):
                hi, lo = HB[blk]
                w = BLOCKS[blk][2] * P
                for b in range(2):
                    pe.wait_ge(acc_free, i * 2 + (J0 + b + 1))
                    product(i * 2 + (J0 + b), b, ps[:, b, 0:w], lambda k: (hi[:, k, 0:w], lo[:, k, 0:w]))

            def jobs_loop(a, z, J0=J_LAT + 22, blk=2):
                with pe.Fori(0, (z - a) // 2) as i:
                    job_pair(i, J0 + a, blk)

            turn_tile(0, 0)
            turn_tile(1, 1)
            pe.wait_ge(x_lo, 2)
            with pe.Fori(0, 2) as i:
                for s in range(2):
                    job_pair(i * 2 + s, J_CTX, 0)
                    pe.wait_ge(x_mod, i * 2 + (s + 1))
                    turn_tile(i * 2 + (2 + s), s)
            jobs_loop(8, 10, J_CTX, 0)
            pe.wait_ge(x_lo, 6)
            with pe.Fori(0, 2) as i:
                for s in range(2):
                    job_pair(i * 4 + 2 * s, J_LAT, 1)
                    pe.wait_ge(x_mod, i * 2 + (s + 5))
                    turn_tile(i * 2 + (6 + s), s)
                    job_pair(i * 4 + (2 * s + 1), J_LAT, 1)
            jobs_loop(16, 22, J_LAT, 1)
            pe.wait_ge(x_lo, 10)
            jobs_loop(0, 4)
            pe.wait_ge(lw_ld, 256)
            at_pair = 0
            for q in range(4):
                c, d = q // 2, q % 2
                jobs_loop(4 + 2 * at_pair, 4 + 2 * LRU_AFTER[q])
                at_pair = LRU_AFTER[q]
                pe.wait_ge(l_conv, c + 1)
                for g in range(2):
                    for part, (o0, w_) in enumerate(((0, 256), (256, 512), (768, 512))):
                        if q:
                            pe.wait_ge(l_gate, (q - 1) * 6 + g * 3 + part + 1)
                        pe.matmul(ps[:, 2 + g * 3 + part, 0:w_], l_w[:, g * 4 + d * 2 + c, :], l_u[:, o0:o0 + w_],
                                  start=True, stop=True).then_inc(l_gp, 1)
            jobs_loop(4 + 2 * at_pair, 22) if at_pair < 9 else None

            def turn_channels(c):
                pe.wait_ge(c_ok, c + 1)
                if c >= 2:
                    pe.wait_ge(c_ev, c - 1)
                for t in range(KT):
                    bank = 4 + 2 * (c % 2) + t // 4
                    ins = pe.transpose(ps[:, bank, (t % 4) * P:(t % 4 + 1) * P], conv[:, c % 2, t * P:(t + 1) * P], ident[:])
                ins.then_inc(c_tp, 1)

            turn_channels(0)
            turn_channels(1)
            for o in range(2):
                J0, E0 = J_HY + 32 * o, E_FWD + 16 * o
                if o == 0:
                    pe.wait_ge(u_lo_ok, 1)
                pe.wait_ge(l_gate, 24)
                def forward(i, ready=None):
                    for b in range(2):
                        pe.wait_ge(acc_free, i * 2 + (E0 + b + 1))
                        product2(i * 2 + (J0 + b), b, ps[:, b, :], u_s, ready=ready if b == 0 else None)

                if o == 0:
                    forward(0)
                    for i in range(1, 5):
                        forward(i)
                        turn_channels(1 + i)
                else:
                    forward(0, lambda k: pe.wait_ge(u_lo_ok, k + 2))
                with pe.Fori(5 if o == 0 else 1, 8) as i:
                    forward(i)
                J0 += 16

                def inverse(i, ready=None):
                    for tp in range(2):
                        pe.wait_ge(inv_free, i * 2 + (8 * o + tp + 1))
                        for b in range(2):
                            product2(i * 4 + (J0 + 2 * tp + b), b, ps[:, 2 + tp, :], y_s[b], start=b == 0, stop=b == 1,
                                     ready=ready if tp == b == 0 else None)

                inverse(0, lambda k: pe.wait_ge(y_l, 8 * o + k + 1))
                with pe.Fori(1, 4) as i:
                    inverse(i)
            pe.wait_ge(inv_free, 17)
            pe.wait_ge(rp_ld, 16)
            pe.transpose(ps[0:31, 2, 0:120], rpbr[0:120, 0:31], ident[0:120, 0:120]).then_inc(rp_tp, 1)
            pe.wait_ge(z_ok, 16)
            for c in range(2):
                for t in range(KT):
                    ins = pe.transpose(ps[:, 4 + 2 * c + t // 4, (t % 4) * P:(t % 4 + 1) * P], tm[:, t, 0, c * P:(c + 1) * P], ident[:])
                ins.then_inc(z_tp, 1)

            pe.wait_ge(sel_ld, 16)
            pe.wait_ge(rp_ok, 1)
            for g in range(16):
                if g >= 4:
                    pe.wait_ge(b_evd if g % 2 == 0 else b_eva, (g - 4) // 2 + 1)
                for j in range(4):
                    ins = pe.matmul(ps[:, g % 4, j * 120:(j + 1) * 120], selt[0:32, 4 * g + j, :], rpbt[0:32, :],
                                    start=True, stop=True)
                ins.then_inc(b_ps, 1)
            pe.wait_ge(b_evd, 8)
            pe.wait_ge(b_eva, 8)
            pe.wait_ge(z_ev, 2)
            with pe.Fori(0, 4) as hp:
                pe.wait_ge(vst_ok, hp + 1)
                for j in range(10):
                    ins = pe.transpose(ps[:, 4 + j // 4, (j % 4) * P:(j % 4 + 1) * P], vst[:, j * P:(j + 1) * P], ident[:])
                ins.then_inc(v_tp, 1)
                pe.wait_ge(st_ok, hp + 1)

                def scores(s):
                    e, (_, k0, kr, _) = s % 2, UNITS[s // 2]
                    if s >= 2:
                        pe.wait_ge(exp_ok, hp * 16 + (s - 1))
                    hh, qs = slice(64 * e, 64 * e + 64), slice((s // 2) * P, (s // 2 + 1) * P)
                    L, key0 = kr * GRID_W, CTX + k0 * GRID_W
                    parts = [(ps[:, 2 * e, :], key0, 512), (ps[:, 2 * e + 1, L - 512:L - 512 + CTX], 0, CTX)]
                    if L > 512:
                        parts.insert(1, (ps[:, 2 * e + 1, 0:L - 512], key0 + 512, L - 512))
                    for dst, a, w in parts:
                        for n, (q_, k_) in enumerate(((qh, kh), (qh, kl), (ql, kh))):
                            ins = pe.matmul(dst, q_[hh, qs], k_[hh, a:a + w], start=n == 0, stop=n == 2)
                    ins.then_inc(qk_done, 1)

                def turn(u):
                    e, kr = u % 2, UNITS[u // 2][2]
                    L = kr * GRID_W
                    if u == 0:
                        pe.wait_ge(v_ev, hp * 2 + 2)
                    pe.wait_ge(nrm_ok, hp * 16 + (u + 1))
                    for c in range(4):
                        pe.transpose(ps[:, 4 + e, c * P:(c + 1) * P], pr[:, e, c * P:(c + 1) * P], ident[:])
                    if u >= 1:
                        pe.wait_ge(pt_a, hp * 16 + u)
                    for c in range(2):
                        ins = pe.transpose(ps[:, 6, c * P:(c + 1) * P], pr[:, e, L + c * P:L + (c + 1) * P], ident[:])
                    if L > 512:
                        ins = pe.transpose(ps[0:64, 6, 256:384], pr[:, e, 512:576], ident[:])
                    ins.then_inc(t_done, 1)

                def values(u):
                    e, (_, k0, kr, _) = u % 2, UNITS[u // 2]
                    pe.wait_ge(pt_a, hp * 16 + (u + 1))
                    hh, qt = slice(64 * e, 64 * e + 64), u // 2
                    o_ = ps[64 * e:64 * e + 64, 7, (qt % 2) * P:(qt % 2 + 1) * P]
                    for c in range(4):
                        pe.matmul(o_, vtm[:, 2 + k0 // 2 + c, hh], pT[:, e, c, :], start=c == 0, stop=False)
                    if kr > WIN_R:
                        pe.matmul(o_, vtm[0:64, 2 + k0 // 2 + 4, hh], pT[0:64, e, 6, :], start=False, stop=False)
                    for c in range(2):
                        ins = pe.matmul(o_, vtm[:, c, hh], pT[:, e, 4 + c, :], start=False, stop=c == 1)
                    ins.then_inc(pv_done, 1)

                for s in range(18):
                    if s < 16:
                        scores(s)
                    if 1 <= s <= 16:
                        turn(s - 1)
                    if s >= 2 and s % 2 == 0:
                        pe.wait_ge(ot_free, hp * 8 + (s // 2 + 1))
                    if s == 2:
                        pe.wait_ge(modp, hp + 1)
                    if s >= 3 and s % 2 == 1:
                        j = (s - 3) // 2
                        pe.wait_ge(macc_ok, hp * 8 + (j + 1))
                        pe.matmul(ps[:, 7, 384 + j:385 + j], macc1[:, j % 2, :], ones[:, 0:1],
                                  start=True, stop=True).then_inc(mod_done, 1)
                    if s >= 2:
                        values(s - 2)

            hb_of = lambda k: (hb_hi[:, k, :], hb_lo[:, k, :])

            def sum_over_features(N, acc):
                pe.wait_ge(n_sum, N + 1)
                pe.matmul(ps[:, 6, :], ones[:], acc[:], start=True, stop=True).then_inc(n_ps, 1)

            def x_turns(Ts):
                for T in Ts:
                    pe.wait_ge(xr_ld, 64 * (T // KT + 1))
                    if T >= 4:
                        pe.wait_ge(n_x1, T - 3)
                    k = T % KT
                    for q in range(4):
                        ins = pe.transpose(ps[:, 2 + T % 4, q * P:(q + 1) * P], xr2[:, q, k * P:(k + 1) * P], ident[:])
                    ins.then_inc(n_tp, 1)

            pe.wait_ge(ot_free, 34)
            pe.wait_ge(modp, 5)

            def project(i, ready=None):
                for b in range(2):
                    pe.wait_ge(acc_free, i * 2 + (E_OUT + b + 1))
                    product(i * 2 + (J_OUT + b), b, ps[:, b, :], hb_of, ready=ready if b == 0 else None)

            project(0, lambda k: pe.wait_ge(m_ld, k + 1) if k < 5 else pe.wait_ge(m_lo, k - 4))
            with pe.Fori(1, 4) as i:
                project(i)
            pe.wait_ge(m_lo, 11)
            for j in range(8):
                pe.wait_ge(acc_free, E_OUT + 8 + j + 1)
                product(J_OUT + 8 + j, j % 2, ps[:, j % 2, :], lambda k: (hb3_hi[:, k, :], hb3_lo[:, k, :]),
                        between={0: lambda: sum_over_features(0, yacc), 5: lambda: sum_over_features(1, nrm)}.get(j))
                if j == 0:
                    x_turns(range(4))
                if j == 2:
                    x_turns(range(4, 8))

            for h in range(2):
                J0, E0 = J_FFN + h * (GU_JOBS + DOWN_JOBS), E_GU + h * GU_JOBS
                def gu_tile(i, between=None, ready=None):
                    for b in range(2):
                        pe.wait_ge(acc_free, i * 2 + (E0 + b + 1))
                        product(i * 2 + (J0 + b), b, ps[:, b, :], hb_of, between=between if b == 0 else None,
                                ready=ready if b == 0 else None)

                input_ready = lambda k: pe.wait_ge(n_hl, KT * h + k + 1)

                def output_turns(q):
                    for k in range(KT):
                        ins = pe.transpose(ps[:, 4 + 2 * (q % 2) + k // 4, (k % 4) * P:(k % 4 + 1) * P],
                                           x1[:, k, q * P:(q + 1) * P], ident[:])
                    ins.then_inc(o_tp, 1)

                if h == 0:
                    gu_tile(0, ready=input_ready)
                    x_turns(range(8, 12))
                    gu_tile(1, lambda: sum_over_features(2, nrm))
                    gu_tile(2)
                    x_turns(range(12, 15))
                    gu_tile(3)
                    x_turns(range(15, 16))
                else:
                    gu_tile(0, lambda: sum_over_features(4, nrm), input_ready)
                    gu_tile(1)
                    gu_tile(2)
                    pe.wait_ge(n_fin, 1)
                    output_turns(0)
                    output_turns(1)
                    gu_tile(3)
                    pe.wait_ge(o_ev, 1)
                    output_turns(2)
                    pe.wait_ge(o_ev, 2)
                    output_turns(3)
                with pe.Fori(4, FT) as i:
                    gu_tile(i)
                J0 += GU_JOBS
                if h == 0:
                    sum_over_features(3, nrm)
                    pe.wait_ge(n_x1, 16)
                pe.wait_ge(g_al, FT * (h + 1))
                with pe.Fori(0, 4) as i:
                    for q in range(6):
                        f, c = q // 3, q % 3
                        nk = KT if c < 2 else FT - 2 * KT
                        if c == 0:
                            pe.wait_ge(dn_free, i * 2 + (8 * h + f + 1))
                        product(i * 6 + (J0 + q), q % 2, ps[:, 2 + f, :],
                                lambda k: (a_hi[:, c * KT + k, :], a_lo[:, c * KT + k, :]), nk, start=c == 0, stop=c == 2)
            pe.wait_ge(o_ev, 4)
            sum_over_features(5, nrm)
            for k in range(KT):
                pe.wait_ge(n_fin, k + 2)
                for q in range(4):
                    ins = pe.transpose(ps[:, 2 * q + k // 4, (k % 4) * P:(k % 4 + 1) * P],
                                       x1[:, k, HALF + q * P:HALF + (q + 1) * P], ident[:])
                    if k == KT - 1:
                        ins.then_inc(o_tp, 1)


_INS = ['x', 'c', 'ctx', 'c_ctx', 'ada_w', 'ada_b', 'g_mix_pre', 'g_mix_post', 'g_ffn_pre', 'g_ffn_post',
        'w_in', 'w_out', 'hy_conv_w', 'hy_conv_b', 'hy_f_w1', 'hy_f_b1', 'hy_f_w2', 'hy_f_b2', 'hy_f_w3',
        'hy_f_freq', 'hy_bias', 'na_rpb', 'lru_conv_w', 'lru_conv_b', 'lru_wa', 'lru_ba', 'lru_wi', 'lru_bi',
        'lru_lam', 'ffn_w_gu', 'ffn_w_down']


def kernel(**inputs):
    import concourse.bacc as bacc
    from concourse.bass_utils import run_bass_kernel_spmd

    nc = bacc.Bacc("TRN2", target_bir_lowering=False, num_devices=1)
    arrays = {name: np.ascontiguousarray(inputs[name]) for name in _INS}
    arrays.update(host_tables())
    aps = {}
    for name, a in arrays.items():
        aps[name] = nc.dram_tensor(f"in_{name}", a.shape, mybir.dt.from_np(a.dtype), kind="ExternalInput").ap()
    out = nc.dram_tensor("out_y", (1, SEQ, D), F32, kind="ExternalOutput").ap()
    program(nc, aps, out)
    r = run_bass_kernel_spmd(nc, [{f"in_{name}": a for name, a in arrays.items()}], core_ids=[0])
    return r.results[0]["out_y"]
```
